# Optimizing a Trainium2 kernel written in Bass

```python
import math
import jax
import jax.numpy as jnp
from jax import lax
import numpy as np

D_MODEL = 1024
BATCH = 1
SEQ = 1024
DEPTH = 1
DEC_BATCH = 8
DEC_SEQ = 8
PAST_LEN = 1024
PAGE_SIZE = 128

M_HEADS = 4
M_DK = 128
M_DV = 128
M_QK_WIDTH = M_HEADS * M_DK
M_WIDTH = M_HEADS * M_DV
MLSTM_CHUNK = 64
A_GROUPS = ((128, 1), (512, 4), (2048, 16))
A_HPG = 4
A_HD = 64
A_HEADS = len(A_GROUPS) * A_HPG
A_WIDTH = A_HEADS * A_HD
A_OUT_WIDTH = A_HPG * A_HD
A_BLOCK = 128
ROPE_THETA = 10000.0
D_FF = 2816
EPS = 1e-6
COL_SIZES = (M_QK_WIDTH, M_QK_WIDTH, M_WIDTH, M_HEADS, M_HEADS, M_WIDTH,
             A_WIDTH, A_WIDTH, A_WIDTH, D_MODEL, D_MODEL)
D_IN = sum(COL_SIZES)

kernel_name = "mlstm_dilated_swa_gated_macaron_step"

F32 = jnp.float32

def rmsnorm(x, g):
    xf = x.astype(F32)
    y = xf * lax.rsqrt(jnp.mean(xf * xf, axis=-1, keepdims=True) + EPS)
    return (y * g.astype(F32)).astype(x.dtype)

def swiglu(h, w_gate, w_up, w_down):
    return (jax.nn.silu(h @ w_gate) * (h @ w_up)) @ w_down

def rope(t, pos):
    dh = t.shape[-1]
    half = dh // 2
    inv_freq = ROPE_THETA ** (-2.0 * jnp.arange(half, dtype=F32) / dh)
    ang = pos.astype(F32)[:, None] * inv_freq[None, :]
    cos = jnp.cos(ang)[None, :, None, :]
    sin = jnp.sin(ang)[None, :, None, :]
    tf = t.astype(F32)
    t1, t2 = tf[..., :half], tf[..., half:]
    return jnp.concatenate([t1 * cos - t2 * sin, t1 * sin + t2 * cos], axis=-1).astype(t.dtype)

def mlstm_chunk_step(carry, inp):
    C, n, m = carry
    q, k, v, ig, lf = inp
    L = q.shape[2]
    b = jnp.cumsum(lf, axis=-1)
    causal = jnp.tril(jnp.ones((L, L), dtype=bool))
    log_w = jnp.where(causal, b[..., :, None] - b[..., None, :] + ig[..., None, :], -jnp.inf)
    log_inter = b + m[..., None]
    m_t = jnp.maximum(log_inter, jnp.max(log_w, axis=-1))
    w_intra = jnp.exp(log_w - m_t[..., None])
    w_inter = jnp.exp(log_inter - m_t)
    qk = jnp.einsum('bhtk,bhsk->bhts', q, k) * w_intra
    num = w_inter[..., None] * jnp.einsum('bhvk,bhtk->bhtv', C, q) + jnp.einsum('bhts,bhsv->bhtv', qk, v)
    den = w_inter * jnp.einsum('bhk,bhtk->bht', n, q) + jnp.sum(qk, axis=-1)
    h = num / jnp.maximum(jnp.abs(den), jnp.exp(-m_t))[..., None]
    m_new = m_t[..., -1]
    decay = jnp.exp(b[..., -1] + m - m_new)
    w_s = jnp.exp(b[..., -1:] - b + ig - m_new[..., None])
    C_new = decay[..., None, None] * C + jnp.einsum('bhs,bhsv,bhsk->bhvk', w_s, v, k)
    n_new = decay[..., None] * n + jnp.einsum('bhs,bhsk->bhk', w_s, k)
    return (C_new, n_new, m_new), h

def mlstm_scan(q, k, v, ig, lf, C, n, m):
    B, S, H, _ = q.shape
    L = math.gcd(S, MLSTM_CHUNK)
    nc = S // L

    def to_chunks(t):
        return t.astype(F32).reshape(B, nc, L, H, -1).transpose(1, 0, 3, 2, 4)

    def gate_chunks(t):
        return t.astype(F32).reshape(B, nc, L, H).transpose(1, 0, 3, 2)

    (C, n, m), h = lax.scan(
        mlstm_chunk_step,
        (C.astype(F32), n.astype(F32), m.astype(F32)),
        (to_chunks(q), to_chunks(k), to_chunks(v), gate_chunks(ig), gate_chunks(lf)))
    h = h.transpose(1, 0, 3, 2, 4).reshape(B, S, H, -1)
    return h, (C, n, m)

def dilated_attn_prompt(q, k, v, window, dilation):
    B, S, H, dh = q.shape
    n_sub = S // dilation
    reach = window // dilation
    nb = -(-n_sub // A_BLOCK)
    n_pad = nb * A_BLOCK
    Z = B * dilation

    def residues(t):
        return t.reshape(B, n_sub, dilation, H, dh).transpose(0, 2, 1, 3, 4).reshape(Z, n_sub, H, dh)

    qb = jnp.pad(residues(q), ((0, 0), (0, n_pad - n_sub), (0, 0), (0, 0))).reshape(Z, nb, A_BLOCK, H, dh)

    def key_blocks(t):
        tp = jnp.pad(residues(t), ((0, 0), (A_BLOCK, n_pad - n_sub), (0, 0), (0, 0)))
        tp = tp.reshape(Z, nb + 1, A_BLOCK, H, dh)
        return jnp.concatenate([tp[:, :-1], tp[:, 1:]], axis=2)

    kb = key_blocks(k)
    vb = key_blocks(v)
    qi = jnp.arange(nb)[:, None] * A_BLOCK + jnp.arange(A_BLOCK)[None, :]
    ki = jnp.arange(nb)[:, None] * A_BLOCK + jnp.arange(2 * A_BLOCK)[None, :] - A_BLOCK
    dist = qi[:, :, None] - ki[:, None, :]
    valid = (dist >= 0) & (dist <= reach) & (ki[:, None, :] >= 0)
    s = jnp.einsum('znqhd,znkhd->znhqk', qb.astype(F32), kb.astype(F32)) * (dh ** -0.5)
    s = jnp.where(valid[None, :, None], s, -jnp.inf)
    mx = jnp.max(s, axis=-1, keepdims=True)
    e = jnp.exp(s - mx)
    den = jnp.sum(e, axis=-1, keepdims=True)
    o = jnp.einsum('znhqk,znkhd->znqhd', e / den, vb.astype(F32))
    lse = (mx + jnp.log(den))[..., 0]
    o = o.reshape(B, dilation, n_pad, H, dh)[:, :, :n_sub].transpose(0, 2, 1, 3, 4).reshape(B, S, H, dh)
    lse = lse.transpose(0, 1, 3, 2).reshape(B, dilation, n_pad, H)[:, :, :n_sub]
    lse = lse.transpose(0, 2, 1, 3).reshape(B, S, H)
    return o, lse

def dilated_attn_cached(q, k, v, kv_cache, window, dilation):
    B, T, H, dh = q.shape
    n_cached = kv_cache.shape[1]
    k_all = jnp.concatenate([kv_cache[:, :, 0].astype(k.dtype), k], axis=1)
    v_all = jnp.concatenate([kv_cache[:, :, 1].astype(v.dtype), v], axis=1)
    reach = window // dilation
    idx = n_cached + jnp.arange(T)[:, None] - dilation * jnp.arange(reach + 1)[None, :]
    valid = idx >= 0
    idx = jnp.maximum(idx, 0)
    kg = k_all[:, idx]
    vg = v_all[:, idx]
    s = jnp.einsum('bthd,btjhd->bhtj', q.astype(F32), kg.astype(F32)) * (dh ** -0.5)
    s = jnp.where(valid[None, None], s, -jnp.inf)
    mx = jnp.max(s, axis=-1, keepdims=True)
    e = jnp.exp(s - mx)
    den = jnp.sum(e, axis=-1, keepdims=True)
    o = jnp.einsum('bhtj,btjhd->bthd', e / den, vg.astype(F32))
    lse = (mx + jnp.log(den))[..., 0].transpose(0, 2, 1)
    return o, lse

def hybrid_layer(x, pos, C0, n0, m0, win_kv, g_ffn1, w1_gate, w1_up, w1_down, g_mix, w_in,
                 b_igate, b_fgate, g_mhead, w_up_m, w_up_a, w_out, g_ffn2, w2_gate, w2_up, w2_down):
    B, S, _ = x.shape
    dt = x.dtype
    x = x + 0.5 * swiglu(rmsnorm(x, g_ffn1), w1_gate, w1_up, w1_down)
    h = rmsnorm(x, g_mix)
    z = h @ w_in
    offs = np.cumsum(COL_SIZES)[:-1].tolist()
    qm, km, vm, ig, fg, og, qa, ka, va, gm, ga = jnp.split(z, offs, axis=-1)

    qm = qm.reshape(B, S, M_HEADS, M_DK)
    km = km.reshape(B, S, M_HEADS, M_DK) * (M_DK ** -0.5)
    vm = vm.reshape(B, S, M_HEADS, M_DV)
    ig_log = ig.astype(F32) + b_igate.astype(F32)
    lf = jax.nn.log_sigmoid(fg.astype(F32) + b_fgate.astype(F32))
    hm, (C, n, m) = mlstm_scan(qm, km, vm, ig_log, lf, C0, n0, m0)
    hm = hm * lax.rsqrt(jnp.mean(hm * hm, axis=-1, keepdims=True) + EPS)
    hm = hm.reshape(B, S, M_WIDTH) * g_mhead.astype(F32) * jax.nn.sigmoid(og.astype(F32))
    y_m = hm.astype(dt) @ w_up_m

    qa = rope(qa.reshape(B, S, A_HEADS, A_HD), pos)
    ka = rope(ka.reshape(B, S, A_HEADS, A_HD), pos)
    va = va.reshape(B, S, A_HEADS, A_HD)
    outs, lses, new_kv = [], [], []
    for g, (window, dilation) in enumerate(A_GROUPS):
        sl = slice(g * A_HPG, (g + 1) * A_HPG)
        qg, kg, vg = qa[:, :, sl], ka[:, :, sl], va[:, :, sl]
        kv_rows = jnp.stack([kg, vg], axis=2)
        if win_kv is None:
            o, lse = dilated_attn_prompt(qg, kg, vg, window, dilation)
            new_kv.append(kv_rows[:, S - min(window, S):])
        else:
            o, lse = dilated_attn_cached(qg, kg, vg, win_kv[g], window, dilation)
            new_kv.append(kv_rows)
        outs.append(o)
        lses.append(lse)
    wts = jax.nn.softmax(jnp.stack(lses), axis=0)
    y_a = jnp.einsum('gbsh,gbshd->bshd', wts, jnp.stack(outs)).reshape(B, S, A_OUT_WIDTH).astype(dt)
    y_a = y_a @ w_up_a

    merged = jax.nn.sigmoid(gm) * y_m + jax.nn.sigmoid(ga) * y_a
    x = x + merged @ w_out
    x = x + 0.5 * swiglu(rmsnorm(x, g_ffn2), w2_gate, w2_up, w2_down)
    return x, (C.astype(dt), n.astype(dt), m.astype(dt)), new_kv

def setup_inputs(seed: int = 0) -> dict:
    key = jax.random.key(seed)
    ks = jax.random.split(key, 32)

    def nrm(k, shape, scale):
        return jax.random.normal(k, shape, F32) * scale

    def gain(k, shape):
        return 1.0 + 0.02 * jax.random.normal(k, shape, F32)

    win_shape = lambda w: (DEPTH, DEC_BATCH, min(w, PAST_LEN), 2, A_HPG, A_HD)
    return {
        "x_prompt": nrm(ks[0], (BATCH, SEQ, D_MODEL), 1.0),
        "x_sample": nrm(ks[1], (DEC_BATCH, DEC_SEQ, D_MODEL), 1.0),
        "state_mlstm_C": nrm(ks[2], (DEPTH, DEC_BATCH, M_HEADS, M_DV, M_DK), 0.5),
        "state_mlstm_n": nrm(ks[3], (DEPTH, DEC_BATCH, M_HEADS, M_DK), 0.5),
        "state_mlstm_m": nrm(ks[4], (DEPTH, DEC_BATCH, M_HEADS), 1.0),
        "cache_win128_kv": nrm(ks[5], win_shape(A_GROUPS[0][0]), 1.0),
        "cache_win512_kv": nrm(ks[6], win_shape(A_GROUPS[1][0]), 1.0),
        "cache_win2048_kv": nrm(ks[7], win_shape(A_GROUPS[2][0]), 1.0),
        "g_ffn1": gain(ks[8], (DEPTH, D_MODEL)),
        "w1_gate": nrm(ks[9], (DEPTH, D_MODEL, D_FF), D_MODEL ** -0.5),
        "w1_up": nrm(ks[10], (DEPTH, D_MODEL, D_FF), D_MODEL ** -0.5),
        "w1_down": nrm(ks[11], (DEPTH, D_FF, D_MODEL), D_FF ** -0.5),
        "g_mix": gain(ks[12], (DEPTH, D_MODEL)),
        "w_in": nrm(ks[13], (DEPTH, D_MODEL, D_IN), D_MODEL ** -0.5),
        "b_igate": nrm(ks[14], (DEPTH, M_HEADS), 0.1),
        "b_fgate": 3.0 + 3.0 * jax.random.uniform(ks[15], (DEPTH, M_HEADS), F32),
        "g_mhead": gain(ks[16], (DEPTH, M_WIDTH)),
        "w_up_m": nrm(ks[17], (DEPTH, M_WIDTH, D_MODEL), M_WIDTH ** -0.5),
        "w_up_a": nrm(ks[18], (DEPTH, A_OUT_WIDTH, D_MODEL), A_OUT_WIDTH ** -0.5),
        "w_out": nrm(ks[19], (DEPTH, D_MODEL, D_MODEL), D_MODEL ** -0.5),
        "g_ffn2": gain(ks[20], (DEPTH, D_MODEL)),
        "w2_gate": nrm(ks[21], (DEPTH, D_MODEL, D_FF), D_MODEL ** -0.5),
        "w2_up": nrm(ks[22], (DEPTH, D_MODEL, D_FF), D_MODEL ** -0.5),
        "w2_down": nrm(ks[23], (DEPTH, D_FF, D_MODEL), D_FF ** -0.5),
        "g_final": gain(ks[24], (D_MODEL,)),
    }

def reference(x_prompt, x_sample, state_mlstm_C, state_mlstm_n, state_mlstm_m,
              cache_win128_kv, cache_win512_kv, cache_win2048_kv,
              g_ffn1, w1_gate, w1_up, w1_down, g_mix, w_in, b_igate, b_fgate, g_mhead,
              w_up_m, w_up_a, w_out, g_ffn2, w2_gate, w2_up, w2_down, g_final):
    B, S, _ = x_prompt.shape
    T = x_sample.shape[1]
    pos_prompt = jnp.arange(S, dtype=jnp.int32)
    pos_sample = PAST_LEN + jnp.arange(T, dtype=jnp.int32)
    xp, xs = x_prompt, x_sample
    Cp, Np_, Mp, K1p, K2p, K3p = [], [], [], [], [], []
    Cs, Ns, Ms, K1s, K2s, K3s = [], [], [], [], [], []
    for l in range(DEPTH):
        lw = (g_ffn1[l], w1_gate[l], w1_up[l], w1_down[l], g_mix[l], w_in[l], b_igate[l], b_fgate[l],
              g_mhead[l], w_up_m[l], w_up_a[l], w_out[l], g_ffn2[l], w2_gate[l], w2_up[l], w2_down[l])
        C0 = jnp.zeros((B, M_HEADS, M_DV, M_DK), F32)
        n0 = jnp.zeros((B, M_HEADS, M_DK), F32)
        m0 = jnp.zeros((B, M_HEADS), F32)
        xp, (c, n, m), kv = hybrid_layer(xp, pos_prompt, C0, n0, m0, None, *lw)
        Cp.append(c); Np_.append(n); Mp.append(m)
        K1p.append(kv[0]); K2p.append(kv[1]); K3p.append(kv[2])
        xs, (c, n, m), kv = hybrid_layer(
            xs, pos_sample, state_mlstm_C[l], state_mlstm_n[l], state_mlstm_m[l],
            (cache_win128_kv[l], cache_win512_kv[l], cache_win2048_kv[l]), *lw)
        Cs.append(c); Ns.append(n); Ms.append(m)
        K1s.append(kv[0]); K2s.append(kv[1]); K3s.append(kv[2])
    y_prompt = rmsnorm(xp, g_final)
    y_sample = rmsnorm(xs, g_final)
    return (y_prompt, y_sample,
            jnp.stack(Cp), jnp.stack(Np_), jnp.stack(Mp),
            jnp.stack(K1p), jnp.stack(K2p), jnp.stack(K3p),
            jnp.stack(Cs), jnp.stack(Ns), jnp.stack(Ms),
            jnp.stack(K1s), jnp.stack(K2s), jnp.stack(K3s))


_drawn_inputs = setup_inputs


def setup_inputs(seed=0):
    import zlib

    import numpy as np

    out = dict(_drawn_inputs(seed))
    spreads = {}
    factors = {'g_ffn1': 4.366,
     'g_mhead': 48.738,
     'g_ffn2': 7.614,
     'g_final': 8.134,
     'cache_win128_kv': 8.0,
     'cache_win512_kv': 8.0,
     'cache_win2048_kv': 8.0,
     'w_up_a': 4.216}
    for name, (base, spread) in spreads.items():
        noise = np.random.default_rng([zlib.crc32(name.encode()), seed]).standard_normal(out[name].shape)
        drawn = base * np.exp(spread * noise) if base else spread * noise
        out[name] = jnp.asarray(drawn.astype(out[name].dtype))
    for name, factor in factors.items():
        out[name] = (out[name] * factor).astype(out[name].dtype)
    return out
```

```python
from contextlib import ExitStack

import numpy as np

import concourse.bass as bass
from concourse import mybir

F32 = mybir.dt.float32
F32R = mybir.dt.float32r
BF16 = mybir.dt.bfloat16
ALU = mybir.AluOpType
ACT = mybir.ActivationFunctionType
AX = mybir.AxisListType

P = 128
D = 1024
KT = D // P
SEQ, NB, T = 1024, 8, 8
SAMP = NB * T
TOK = SEQ + SAMP
F = 2816
FFN_ITERS = F // (2 * P)
CHUNKS = ((0, 384), (384, 384), (768, TOK - 768))
NC = len(CHUNKS)
H = 4
DK = 128
HD = 64
G = 3
NBLK = SEQ // P
EPS = 1e-6
NEG = -1e30

SLAB = 2048
S_IF = 3 * FFN_ITERS
S_V = S_IF + 1
S_F = S_V + 5
S_UP = S_F + 20
S_OUT = S_UP + 3
S_FFN2 = S_OUT + 4
SLABS = S_FFN2 + 3 * FFN_ITERS
PU_F = 6 * FFN_ITERS
PU_UP = PU_F + 20 * NC
PU_FFN2 = PU_UP + KT * NC
AU_IF = 24 * FFN_ITERS
AU_V = AU_IF + NC
AU_OUT = AU_V + 5 * 9
AU_FFN2 = AU_OUT + KT * NC
AU_END = AU_FFN2 + 24 * FFN_ITERS

C_ONES, C_ID, C_G, C_GM, C_EPS, C_ONE, C_BI, C_BF, C_MS, C_N = 0, 128, 256, 288, 292, 293, 294, 295, 296, 297
M_CAUSAL, M_SAMPLE, M_BLOCK, M_N = 0, 128, 192, 200
A_BAND, A_PAIR, A_ID, A_SAMP, A_N = 0, 256, 384, 512, 512 + 1176
KEYS_S = 128 + 512 + 512 + 24
SC_OFF = (0, 512, 1024)


def attention_units():
    out = []
    for g, blocks in ((0, NBLK), (1, NBLK), (2, NBLK)):
        for blk in range(blocks):
            first = (blk == 0, blk % 2 == 0, True)[g]
            out += [(g, blk, 0, 4, 1)] if first else [(g, blk, 0, 2, 2), (g, blk, 2, 2, 2)]
    return out


UNITS = attention_units()
ATT_IN = (16 * 5, 16 * 8, 16 * (5 + 5))


def program(nc, stream, xT, cols, masks, amasks, cos_t, sin_t, state_in, m_in, kc_in, vc_in,
            y_out, c_out, m_out, cs_out, ms_out, kr_out, va_out):
    dram = lambda name, shape: nc.dram_tensor(name, shape, F32).ap()
    zqko = dram("zqko", (12, P, TOK))
    zgate = dram("zgate", (16, P, TOK))
    qr = dram("qr", (G, 2, P, TOK))
    vm = dram("vm", (TOK, H, DK + 1))
    zif = dram("zif", (8, TOK))
    lastrow = dram("lastrow", (2, 32))
    rows = dram("rows", (3, H, TOK))
    mix = dram("mix", (6, P, TOK))
    o_att = dram("o_att", (SEQ, G, H, HD + 2))

    ctx = ExitStack()
    with ctx:
        at = [16512]

        def place(name, shape, dt=F32, offset=None):
            size = int(np.prod(shape[1:])) * (2 if dt == BF16 else 4)
            size = -(-size // 32) * 32
            o = at[0] if offset is None else offset
            t = nc.alloc_sbuf_tensor_at(name, shape, dt, offset=o)
            if offset is None:
                at[0] += size
            return t

        def overlay(base):
            o = [base]

            def put(name, shape, dt=F32):
                t = place(name, shape, dt, o[0])
                o[0] += -(-int(np.prod(shape[1:])) * (2 if dt == BF16 else 4) // 32) * 32
                assert o[0] <= 229344, (name, o[0])
                return t
            return put

        x = place("x", [P, KT, TOK])
        raw = place("raw", [P, 3, SLAB])
        whi = place("whi", [P, 3, SLAB], F32R)
        wlo = place("wlo", [P, 3, SLAB], F32R)
        con = place("con", [P, C_N])
        idb = place("idb", [P, P], BF16)
        MIX = at[0]
        h_hi = place("h_hi", [P, KT, TOK], F32R)
        h_lo = place("h_lo", [P, KT, TOK], F32R)
        ACTS = at[0]
        act_hi = place("act_hi", [P, 2, TOK], F32R)
        act_lo = place("act_lo", [P, 2, TOK], F32R)
        TEMP = at[0]
        put = overlay(TEMP)
        sq = put("sq", [P, 2, 384])
        htmp = put("htmp", [P, 2, 384])
        rstd = put("rstd", [P, 2, 384])
        put = overlay(TEMP)
        stage = put("stage", [P, 2, 2, 384])
        svm = put("svm", [P, 2, 2, DK + 1])
        sva = put("sva", [P, 2, H, HD + 1])
        at[0] = TEMP + 10496
        silu = place("silu", [P, 2, 384])
        zif_s = place("zif_s", [8, NC, 384], F32, at[0] - 3072)
        assert at[0] <= 229344
        put = overlay(ACTS)
        cost = put("cost", [P, TOK])
        sint = put("sint", [P, TOK])
        W32 = P + T
        zi = put("zi", [32, W32])
        zf = put("zf", [32, W32])
        gna = put("gna", [32, W32])
        gmn = put("gmn", [32, W32])
        ge = put("ge", [32, W32])
        gl = put("gl", [32, W32])
        scan_b = put("scan_b", [32, 2, 204])
        scan_g = put("scan_g", [32, 2, 204])
        lrow = put("lrow", [1, 2, 32])
        mrow = put("mrow", [1, H, NBLK + 1])
        mtmp = put("mtmp", [1, NBLK, H])
        mcol = put("mcol", [32, 1])
        put = overlay(MIX)
        qT = put("qT", [P, 2, TOK])
        kT = put("kT", [P, 2, TOK])
        oT = put("oT", [P, 2, TOK])
        nM = put("nM", [P, 2, TOK])
        nm = put("nm", [P, 2, TOK])
        v1 = put("v1", [P, 2, 9, DK + 1])
        Wd = put("Wd", [P, 2, TOK])
        qw = put("qw", [P, 2, TOK])
        hn = put("hn", [P, 2, TOK])
        ss = put("ss", [P, TOK])
        Cs = put("Cs", [P, 2, NB, DK + 1])
        Cp = put("Cp", [P, 2, DK + 1])
        kw = put("kw", [P, 2, DK])
        Pm = put("Pm", [P, 2, P])
        vex = put("vex", [SAMP, NB, DK + 1])
        den = put("den", [P, P])
        msk = put("msk", [P, M_N])
        gcol = put("gcol", [P, 9, H])
        mpb = put("mpb", [P, H, 8])
        msb = put("msb", [P, H, NB])
        ecol = put("ecol", [P, 2, 3, 8])
        own = put("own", [SAMP, 2, 8])
        wsc = put("wsc", [SAMP, 2, 2])
        qn = put("qn", [P, SAMP])
        put = overlay(MIX)
        aq = put("aq", [HD, 2, H, SEQ])
        ak = put("ak", [HD, 2, H, SEQ])
        av = put("av", [P, 2, NBLK, H * (HD + 1)])
        ap_ = put("ap_", [P, 2, 512])
        apt = put("apt", [P, 2, 512])
        ao = put("ao", [P, 2, H, HD + 2])
        amx = put("amx", [P, 4, 4])
        amf = put("amf", [P, A_SAMP])
        amb = put("amb", [P, 384], BF16)
        put = overlay(MIX)
        kc = put("kc", [HD, 2, H, 1152])
        vc = put("vc", [P, 2, 9, H * (HD + 1)])
        sqs = put("sqs", [HD, G, H, SAMP])
        sks = put("sks", [HD, G, H, SAMP])
        vnw = put("vnw", [G * T, NB, H * (HD + 1)])
        sqr = put("sqr", [HD, G, H, NB, 32])
        spx = put("spx", [P, 2, KEYS_S])
        soT = put("soT", [HD, H, NB, T])
        spt = put("spt", [P, 10, P])
        smb = put("smb", [P, KEYS_S], BF16)
        smx = put("smx", [P, 2, 4])
        so = put("so", [P, 2, HD + 1])
        put = overlay(MIX)
        oc = put("oc", [P, 2, G, H, HD + 2])
        ocw = put("ocw", [P, 2, G, H])
        ocm = put("ocm", [P, 2, H])
        oacc = put("oacc", [P, 2, H, HD + 1])
        yat = put("yat", [P, 2, H * HD])
        yT = put("yT", [P, 2, 2, P])
        put = overlay(ACTS)
        mx_hi = put("mx_hi", [P, 6, 384], F32R)
        mx_lo = put("mx_lo", [P, 6, 384], F32R)
        mxin = put("mxin", [P, 2, 384])
        sgate = put("sgate", [P, 2, 2, 384])
        mgt = put("mgt", [P, 384])
        ps = nc.alloc_psum_tensor("ps", [P, 8, 512], F32)
        bank = lambda b, w: ps[:, b, 0:w]
        sem = lambda name: ctx.enter_context(nc.semaphore(name))
        acc_free = sem("acc_free")
        acc_full = sem("acc_full")
        acthi_done = sem("acthi_done")
        amb_ready = sem("amb_ready")
        arg_ready = sem("arg_ready")
        as_full = sem("as_full")
        att_const = sem("att_const")
        att_in = [sem(f"att_in{i}") for i in range(2)]
        blk_ready = sem("blk_ready")
        c_in = [sem(f"c_in{i}") for i in range(2)]
        c_out_ = [sem(f"c_out_{i}") for i in range(2)]
        con_in = sem("con_in")
        cp_out = sem("cp_out")
        cp_ready = sem("cp_ready")
        cs_outd = sem("cs_outd")
        cs_ready = sem("cs_ready")
        cu_full = sem("cu_full")
        dve_step = sem("dve_step")
        exp_ready = sem("exp_ready")
        gM_ready = sem("gM_ready")
        gate_full = sem("gate_full")
        gates_in = sem("gates_in")
        ge_ready = sem("ge_ready")
        gl_ready = sem("gl_ready")
        gna_ready = sem("gna_ready")
        grow_io = sem("grow_io")
        grows_out = sem("grows_out")
        h_ready = sem("h_ready")
        head_done = sem("head_done")
        head_in = [sem(f"head_in{i}") for i in range(2)]
        hhi_ready = sem("hhi_ready")
        hi_split = sem("hi_split")
        hm_out = sem("hm_out")
        hn_ready = sem("hn_ready")
        ht_ready = sem("ht_ready")
        idb_ready = sem("idb_ready")
        if_staged = sem("if_staged")
        if_stored = sem("if_stored")
        kw_ready = sem("kw_ready")
        mg_hid = sem("mg_hid")
        mg_ready = sem("mg_ready")
        mix_const = sem("mix_const")
        mrow_ready = sem("mrow_ready")
        ms_stored = sem("ms_stored")
        mul_done = sem("mul_done")
        mx_full = sem("mx_full")
        mx_hid = sem("mx_hid")
        mx_in = [sem(f"mx_in{i}") for i in range(2)]
        mx_ready = sem("mx_ready")
        nd_full = sem("nd_full")
        o_ready = sem("o_ready")
        o_stored = [sem(f"o_stored{i}") for i in range(2)]
        oc_read = sem("oc_read")
        oce_ready = sem("oce_ready")
        ocw_ready = sem("ocw_ready")
        ov_full = sem("ov_full")
        p_ready = sem("p_ready")
        pair_free = sem("pair_free")
        pm_ready = sem("pm_ready")
        pt_full = sem("pt_full")
        pt_ready = sem("pt_ready")
        qw_ready = sem("qw_ready")
        raw_in = [sem(f"raw_in{i}") for i in range(3)]
        rope_ready = sem("rope_ready")
        rs_read = sem("rs_read")
        rs_ready = sem("rs_ready")
        rstd_ready = sem("rstd_ready")
        s_const = sem("s_const")
        s_in = [sem(f"s_in{i}") for i in range(2)]
        s_out = sem("s_out")
        samp_ready = sem("samp_ready")
        sg_in = [sem(f"sg_in{i}") for i in range(2)]
        sg_read = sem("sg_read")
        silu_done = sem("silu_done")
        slab_free = sem("slab_free")
        slab_ready = sem("slab_ready")
        smx_ready = sem("smx_ready")
        soT_ready = sem("soT_ready")
        so_ready = sem("so_ready")
        sot_full = sem("sot_full")
        sp_ready = sem("sp_ready")
        spt_ready = sem("spt_ready")
        sq_free = sem("sq_free")
        sq_ready = sem("sq_ready")
        sqh_ready = sem("sqh_ready")
        sqr_ready = sem("sqr_ready")
        ss2_full = sem("ss2_full")
        ss_full = sem("ss_full")
        st_full = sem("st_full")
        std_ready = sem("std_ready")
        stored = [sem(f"stored{i}") for i in range(2)]
        su_full = sem("su_full")
        sv_full = sem("sv_full")
        tab_in = sem("tab_in")
        ts_full = sem("ts_full")
        up_full = sem("up_full")
        v_staged = sem("v_staged")
        v_stored = [sem(f"v_stored{i}") for i in range(2)]
        x_in = [sem(f"x_in{i}") for i in range(3)]
        yT_ready = sem("yT_ready")
        y_ready = sem("y_ready")
        y_stored = [sem(f"y_stored{i}") for i in range(2)]
        ya_ready = sem("ya_ready")
        yt_full = sem("yt_full")
        block = ctx.enter_context(nc.Block())
        def ch(t, c):
            a, w = CHUNKS[c]
            return t[..., a:a + w]

        @block.sync
        def _(sp):
            def slab(s, j):
                sp.dma_start(raw[:, j, :], stream[s]).then_inc(raw_in[j], 16)

            def slab_behind(s, j):
                sp.wait_ge(slab_ready, s - 2)
                slab(s, j)

            sp.dma_start(con[:], cols).then_inc(con_in, 16)
            sp.dma_start(ch(x[:, :, :], 0), ch(xT, 0)).then_inc(x_in[0], 16)
            slab(0, 0)
            sp.dma_start(ch(x[:, :, :], 1), ch(xT, 1)).then_inc(x_in[1], 16)
            sp.dma_start(ch(x[:, :, :], 2), ch(xT, 2)).then_inc(x_in[2], 16)
            slab(1, 1)
            slab(2, 2)
            LOOPED = (S_UP + 3) // 3
            with sp.Fori(1, LOOPED) as i:
                for j in range(3):
                    slab_behind(3 * i + j, j)
            for s in range(3 * LOOPED, S_UP + 6):
                slab_behind(s, s % 3)

            sp.wait_ge(up_full, PU_UP)
            sp.wait_ge(stored[0], 16 * 30)
            sp.wait_ge(stored[1], 16 * 30)
            sp.wait_ge(v_stored[0], 16 * 23)
            sp.wait_ge(v_stored[1], 16 * 22)
            sp.wait_ge(grows_out, 16 * (1 + 24))
            sp.dma_start(msk[:], masks).then_inc(mix_const, 16)
            for h in range(H):
                sp.dma_start(gcol[:, 0:8, h], rows[2, h, 0:SEQ].rearrange("(n p) -> p n", p=P),
                             allow_slow_non_contiguous=True).then_inc(mix_const, 16)
            sp.dma_start(gcol[0:SAMP, 8, :], rows[2, :, SEQ:TOK].rearrange("h p -> p h"), allow_slow_non_contiguous=True).then_inc(mix_const, 16)
            sp.dma_start(mpb[:], m_out[:, 0:8].unsqueeze(0).to_broadcast([P, H, 8])).then_inc(mix_const, 16)
            sp.dma_start(msb[:], m_in.unsqueeze(0).to_broadcast([P, H, NB])).then_inc(mix_const, 16)

            def load_head(h):
                s = h % 2
                for dst, src in ((qT[:, s], zqko[h]), (kT[:, s], zqko[4 + h]), (oT[:, s], zqko[8 + h]),
                                 (nM[:, s], rows[0, h].unsqueeze(0).to_broadcast([P, TOK])),
                                 (nm[:, s], rows[1, h].unsqueeze(0).to_broadcast([P, TOK])),
                                 (v1[:, s, 0:8], vm[0:SEQ, h].rearrange("(n p) e -> p n e", p=P)),
                                 (v1[0:SAMP, s, 8], vm[SEQ:TOK, h]), (Cs[:, s], state_in[h])):
                    sp.dma_start(dst, src).then_inc(head_in[s], 16)

            load_head(0)
            load_head(1)
            for h in range(H):
                sp.wait_ge(cp_ready, 8 * (h + 1))
                sp.dma_start(c_out[h], Cp[:, 0]).then_inc(cp_out, 16)
                sp.wait_ge(head_done, h + 1)
                sp.dma_start(mix[h], ss[:]).then_inc(hm_out, 16)
                sp.dma_start(cs_out[h], Cs[:, h % 2]).then_inc(cs_outd, 16)
                if h + 2 < H:
                    sp.wait_ge(cs_outd, 16 * (h + 1))
                    load_head(h + 2)

            sp.wait_ge(hm_out, 16 * H)
            sp.wait_ge(cs_outd, 16 * H)
            sp.wait_ge(cp_out, 16 * H)
            sp.dma_start(amf[:], amasks[:, 0:A_SAMP]).then_inc(att_const, 16)

            def load_group(g):
                s = g % 2
                for half in range(2):
                    for dst, src in ((aq, qr), (ak, kr_out)):
                        sp.dma_start(dst[32 * half:32 * half + 32, s],
                                     src[g, half, :, 0:SEQ].rearrange("(h p) t -> p h t", h=H)).then_inc(att_in[s], 16)
                if g == 0:
                    sp.dma_start(av[:, s], va_out[0:SEQ, g].rearrange("(n p) e -> p n e", p=P)).then_inc(att_in[s], 16)
                elif g == 1:
                    v = va_out[0:SEQ, g].rearrange("(q p r) e -> r p q e", p=P, r=4)
                    for r in range(4):
                        sp.dma_start(av[:, s, 2 * r:2 * r + 2], v[r]).then_inc(att_in[s], 16)
                else:
                    sp.dma_start(av[:, s], va_out[0:SEQ, g].rearrange("(i u) e -> i u e", u=8)).then_inc(att_in[s], 16)

            load_group(0)
            load_group(1)
            last_of = [max(u for u, x_ in enumerate(UNITS) if x_[0] == g) for g in range(G)]
            for u, (g, blk, h0, nh, nk) in enumerate(UNITS):
                sp.wait_ge(o_ready, u + 1)
                o = o_att[:, g, h0:h0 + nh, :]
                src = ao[:, u % 2, 0:nh]
                if g == 0:
                    sp.dma_start(o[blk * P:(blk + 1) * P], src).then_inc(o_stored[u % 2], 16)
                elif g == 1:
                    r, qb = blk // 2, blk % 2
                    o = o.rearrange("(q p r) h e -> r q p h e", p=P, r=4)
                    sp.dma_start(o[r, qb], src).then_inc(o_stored[u % 2], 16)
                else:
                    sp.dma_start(o.rearrange("(i u) h e -> u i h e", u=8)[blk], src).then_inc(o_stored[u % 2], 16)
                if u == last_of[0]:
                    load_group(2)

            for s in range(2):
                sp.wait_ge(o_stored[s], 16 * len(UNITS[s::2]))
            for n in range(NBLK):
                if n >= 2:
                    sp.wait_ge(oc_read, n - 1)
                sp.dma_start(oc[:, n % 2], o_att[n * P:(n + 1) * P]).then_inc(c_in[n % 2], 16)
                if n >= 1:
                    sp.wait_ge(yT_ready, n)
                    sp.dma_start(mix[4:6, :, (n - 1) * P:n * P].rearrange("j p t -> p j t"),
                                 yT[:, (n - 1) % 2]).then_inc(c_out_[(n - 1) % 2], 16)
            sp.wait_ge(yT_ready, NBLK)
            sp.dma_start(mix[4:6, :, SEQ - P:SEQ].rearrange("j p t -> p j t"), yT[:, 1]).then_inc(c_out_[1], 16)

            sp.wait_ge(c_out_[0], 16 * 4)
            sp.wait_ge(c_out_[1], 16 * 4)
            for g in range(G):
                for half in range(2):
                    for dst, src in ((sqs, qr), (sks, kr_out)):
                        sp.dma_start(dst[32 * half:32 * half + 32, g],
                                     src[g, half, :, SEQ:TOK].rearrange("(h p) t -> p h t", h=H)).then_inc(s_const, 16)
                sp.dma_start(vnw[T * g:T * g + T], va_out[SEQ:TOK, g].rearrange("(b t) e -> t b e", t=T)).then_inc(s_const, 16)
            sp.dma_start(spx[:, 1, :], amasks[:, A_SAMP:A_N]).then_inc(s_const, 16)
            for b in range(NB):
                if b >= 2:
                    sp.wait_ge(so_ready, b - 1)
                sp.dma_start(kc[:, b % 2], kc_in[b]).then_inc(s_in[b % 2], 16)
                sp.dma_start(vc[:, b % 2], vc_in[b]).then_inc(s_in[b % 2], 16)
            sp.wait_ge(soT_ready, NB)
            for h in range(H):
                sp.dma_start(mix[4 + h // 2, 64 * (h % 2):64 * (h % 2) + 64, SEQ:TOK],
                             soT[:, h].rearrange("d b t -> d (b t)")).then_inc(s_out, 16)

            sp.wait_ge(s_out, 16 * H)
            for c in range(NC):
                a, w = CHUNKS[c]
                for k in range(6):
                    n = 6 * c + k
                    if n >= 2:
                        sp.wait_ge(mx_ready, n - 1)
                    sp.dma_start(mxin[:, n % 2, 0:w], mix[k, :, a:a + w]).then_inc(mx_in[n % 2], 16)
                for d in range(KT):
                    n = KT * c + d
                    if n >= 2:
                        sp.wait_ge(sg_read, n - 1)
                    sp.dma_start(sgate[:, n % 2, :, 0:w],
                                 zgate.rearrange("(j d) p t -> d p j t", j=2)[d, :, :, a:a + w]).then_inc(sg_in[n % 2], 16)

            for s in range(S_UP + 6, 3 * (-(-(S_UP + 6) // 3))):
                slab_behind(s, s % 3)
            with sp.Fori(-(-(S_UP + 6) // 3), SLABS // 3) as i:
                for j in range(3):
                    slab_behind(3 * i + j, j)

            for c in range(NC):
                a, w = CHUNKS[c]
                for k in range(KT):
                    q = KT * c + k
                    sp.wait_ge(y_ready, q + 1)
                    sp.dma_start(y_out[:, k, a:a + w], htmp[:, q % 2, 0:w]).then_inc(y_stored[q % 2], 16)
            sp.wait_ge(y_stored[0], 16 * 12)
            sp.wait_ge(y_stored[1], 16 * 12)

        @block.gpsimd
        def _(pool):
            pool.wait_ge(con_in, 16)
            with pool.Fori(0, SLABS // 3) as i:
                for j in range(3):
                    pool.wait_ge(raw_in[j], 16 * i + 16)
                    pool.wait_ge(slab_free, 3 * i + j + 1)
                    pool.tensor_tensor(whi[:, j, :], raw[:, j, :], con[:, C_ONES:C_ONES + 1].to_broadcast([P, SLAB]), ALU.mult).then_inc(hi_split, 1)
                    pool.wait_ge(hi_split, 3 * i + j + 1)
                    pool.tensor_tensor(wlo[:, j, :], raw[:, j, :], whi[:, j, :].bitcast(F32),
                                       ALU.subtract).then_inc(slab_ready, 1)

        @block.tensor
        def _(pe):
            ones = con[:, C_ONES:C_ONES + P]
            ident = con[:, C_ID:C_ID + P]

            def products(out, parts, nk):
                for k in range(nk):
                    w_hi, w_lo, x_hi, x_lo = parts(k)
                    pe.matmul(out, w_hi, x_hi, start=(k == 0), stop=False)
                    pe.matmul(out, w_hi, x_lo, start=False, stop=False)
                    last = pe.matmul(out, w_lo, x_hi, start=False, stop=(k == nk - 1))
                return last

            def norm(n, free):
                pe.wait_ge(acc_free, free)
                for c, (a, w) in enumerate(CHUNKS):
                    for k in range(KT):
                        q = 24 * n + 8 * c + k
                        pe.wait_ge(sq_ready, q + 1)
                        mm = pe.matmul(bank(4 + c, w), ones, sq[:, q % 2, 0:w], start=(k == 0), stop=(k == KT - 1))
                        mm.then_inc(sq_free, 1)

            def pair_unit(j, c, unit, par):
                a, w = CHUNKS[c]
                pe.wait_ge(pair_free, unit + 1)
                for half, full in ((0, gate_full), (1, up_full)):
                    products(bank(2 * par + half, w), lambda k: (
                        whi[:, j, (8 * half + k) * P:(8 * half + k + 1) * P],
                        wlo[:, j, (8 * half + k) * P:(8 * half + k + 1) * P],
                        h_hi[:, k, a:a + w], h_lo[:, k, a:a + w]), KT).then_inc(full, 1)

            def ffn(n):
                s0, pu, au = (0, 0, 0) if n == 0 else (S_FFN2, PU_FFN2, AU_FFN2)
                norm_n = 2 * n
                with pe.Fori(0, FFN_ITERS) as i:
                    for j in range(2):
                        pe.wait_ge(slab_ready, 3 * i + (s0 + j + 1))
                        for c in range(NC):
                            pe.wait_ge(h_ready, 24 * norm_n + 8 * (c + 1))
                            pair_unit(j, c, 6 * i + (pu + 3 * j + c), (3 * j + c) % 2)
                        pe.wait_ge(up_full, 6 * i + (pu + 3 * j + 3))
                        pe.sem_inc(slab_free, 1)
                    pe.wait_ge(slab_ready, 3 * i + (s0 + 3))
                    for c, (a, w) in enumerate(CHUNKS):
                        pe.wait_ge(pair_free, 6 * i + (pu + 3 + c + 1 + 2))
                        for d in range(KT):
                            v = 8 * c + d
                            pe.wait_ge(acc_free, 24 * i + (au + v + 1))
                            products(bank(4 + v % 4, w), lambda k: (
                                whi[:, 2, k * D + d * P:k * D + (d + 1) * P], wlo[:, 2, k * D + d * P:k * D + (d + 1) * P],
                                act_hi[:, k, a:a + w], act_lo[:, k, a:a + w]), 2).then_inc(acc_full, 1)
                    pe.wait_ge(acc_full, 24 * i + (au + 24))
                    pe.sem_inc(slab_free, 1)

            pe.wait_ge(con_in, 16)
            norm(0, 4)
            ffn(0)
            norm(1, 4 + AU_IF)

            pe.wait_ge(slab_ready, S_IF + 1)
            for c, (a, w) in enumerate(CHUNKS):
                pe.wait_ge(h_ready, 24 + 8 * (c + 1))
                pe.wait_ge(acc_free, AU_IF + c + 1)
                products(bank(4 + c, w), lambda k: (whi[:, 0, k * 256:k * 256 + P], wlo[:, 0, k * 256:k * 256 + P],
                                                    h_hi[:, k, a:a + w], h_lo[:, k, a:a + w]), KT).then_inc(acc_full, 1)
            pe.wait_ge(acc_full, AU_IF + 3)
            pe.sem_inc(slab_free, 1)
            for s in range(5):
                j = (S_V + s) % 3
                pe.wait_ge(slab_ready, S_V + s + 1)
                for t in range(9):
                    v = AU_V + 9 * s + t
                    a = min(t * P, TOK - P)
                    pe.wait_ge(acc_free, v + 1)
                    products(bank(4 + v % 4, 256), lambda k: (h_hi[:, k, a:a + P], h_lo[:, k, a:a + P],
                                                              whi[:, j, k * 256:(k + 1) * 256],
                                                              wlo[:, j, k * 256:(k + 1) * 256]), KT).then_inc(acc_full, 1)
                pe.wait_ge(acc_full, AU_V + 9 * s + 9)
                pe.sem_inc(slab_free, 1)
            with pe.Fori(0, 3) as i:
                for j in range(6):
                    pe.wait_ge(slab_ready, 6 * i + (S_F + j + 1))
                    for c in range(NC):
                        pair_unit(j % 3, c, 18 * i + (PU_F + 3 * j + c), (3 * j + c) % 2)
                    pe.wait_ge(up_full, 18 * i + (PU_F + 3 * j + 3))
                    pe.sem_inc(slab_free, 1)
            for j in range(2):
                pe.wait_ge(slab_ready, S_F + 18 + j + 1)
                for c in range(NC):
                    pair_unit(j, c, PU_F + 54 + 3 * j + c, (3 * j + c) % 2)
                pe.wait_ge(up_full, PU_F + 54 + 3 * j + 3)
                pe.sem_inc(slab_free, 1)

            def where(w):
                h, c = divmod(w, 9)
                return h, c, (SAMP if c == 8 else P), slice(c * P, c * P + (SAMP if c == 8 else P))

            def scores(w):
                h, c, n, tok = where(w)
                s = h % 2
                if c == 0:
                    pe.wait_ge(head_in[s], 128 * (h // 2 + 1))
                if w == 0:
                    pe.wait_ge(pair_free, PU_UP + 2)
                    pe.wait_ge(acc_free, 4 + AU_OUT)
                if w >= 2:
                    pe.wait_ge(kw_ready, w - 1)
                    pe.wait_ge(pm_ready, w - 1)
                pe.transpose(ps[0:n, 2 + w % 2, 0:P], kT[:, s, tok], ident)
                pe.matmul(ps[0:n, w % 2, 0:n], kT[:, s, tok], qT[:, s, tok], start=True, stop=True).then_inc(ts_full, 1)

            def outputs(w):
                h, c, n, tok = where(w)
                s = h % 2
                b = 4 + w % 2
                num, dn = ps[:, b, 0:n], ps[:, b, P:P + n]
                pe.wait_ge(pm_ready, w + 1)
                if w >= 2:
                    pe.wait_ge(hn_ready, w - 1)
                if c == 1:
                    pe.wait_ge(qw_ready, h + 1)
                if 0 < c < 8:
                    pe.wait_ge(cp_ready, 8 * h + c)
                if c == 8:
                    pe.wait_ge(samp_ready, h + 1)
                more = c > 0
                pe.matmul(num, v1[0:n, s, c, 0:DK], Pm[0:n, w % 2, 0:n], start=True, stop=not more)
                if c == 8:
                    for q in range(NB):
                        pe.matmul(num[:, T * q:T * q + T], Cs[:, s, q, 0:DK], qw[:, s, SEQ + T * q:SEQ + T * q + T],
                                  start=False, stop=(q == NB - 1))
                elif more:
                    pe.matmul(num, Cp[:, c % 2, 0:DK], qw[:, s, tok], start=False, stop=True)
                mm = pe.matmul(dn, ones[0:n], Pm[0:n, w % 2, 0:n], start=True, stop=not more)
                if c == 8:
                    mm = pe.matmul(dn, ones, qn[:], start=False, stop=True)
                elif more:
                    mm = pe.matmul(dn, Cp[:, c % 2, DK:DK + 1].to_broadcast([P, P]), qw[:, s, tok], start=False, stop=True)
                mm.then_inc(nd_full, 1)

            def states(w):
                h, c, n, tok = where(w)
                s = h % 2
                pe.wait_ge(kw_ready, w + 1)
                if c < 8:
                    pe.wait_ge(cp_ready, 8 * h + c)
                    if c == 0 and h > 0:
                        pe.wait_ge(cs_ready, 8 * h)
                    pe.matmul(ps[:, 6, 0:DK + 1], kw[:, w % 2, :], v1[:, s, c, :], start=True, stop=True).then_inc(cu_full, 1)
                else:
                    pe.wait_ge(cp_ready, 8 * h + 8)
                    if h > 0:
                        pe.wait_ge(rs_read, 3 * h)
                    for q in range(NB):
                        if q >= 2:
                            pe.wait_ge(cs_ready, 8 * h + q - 1)
                        pe.matmul(ps[:, 6 + q % 2, 0:DK + 1], kw[0:SAMP, w % 2, :], vex[:, q, :],
                                  start=True, stop=True).then_inc(su_full, 1)

            def norm_head(h):
                pe.wait_ge(sqh_ready, h + 1)
                pe.wait_ge(cs_ready, 8 * h + 8)
                for c, (a, w) in enumerate(CHUNKS):
                    if 3 * h + c > 0:
                        pe.wait_ge(rs_read, 3 * h + c)
                    pe.matmul(bank(7, w), ones, ss[:, a:a + w], start=True, stop=True).then_inc(ss_full, 1)

            scores(0)
            for w in range(9 * H):
                if w + 1 < 9 * H:
                    scores(w + 1)
                if w % 9 < 8:
                    states(w)
                    outputs(w)
                else:
                    outputs(w)
                    states(w)
                if w % 9 == 0 and w > 0:
                    norm_head(w // 9 - 1)
            norm_head(H - 1)

            def tokens(t, g, blk, n=1):
                if g == 0:
                    return t[:, blk * P:(blk + n) * P]
                if g == 1:
                    r, q = divmod(blk, 2)
                    return t.rearrange("p (n r) -> p r n", r=4)[:, r, q * P:(q + n) * P]
                return t.rearrange("p (i u) -> p u i", u=8)[:, blk, :]

            def att_scores(u):
                g, blk, h0, nh, nk = UNITS[u]
                s = g % 2
                if u == 0:
                    pe.wait_ge(amb_ready, 1)
                    pe.wait_ge(rs_read, 3 * H)
                    pe.wait_ge(hn_ready, 9 * H)
                if u == 0 or UNITS[u - 1][0] != g:
                    pe.wait_ge(att_in[s], ATT_IN[g])
                if u >= 2:
                    pe.wait_ge(p_ready, u - 1)
                b = u % 2
                mask = (amb[:, 256:384] if g == 2 else amb[:, 256 - 128 * nk:256])
                pe.matmul(ps[:, b, :], idb[:], mask.unsqueeze(1).to_broadcast([P, nh, nk * P]), start=True, stop=False)
                for i in range(nh):
                    q = tokens(aq[:, s, h0 + i, :], g, blk)
                    k = tokens(ak[:, s, h0 + i, :], g, blk - (nk - 1), nk)
                    mm = pe.matmul(ps[:, b, i * nk * P:(i + 1) * nk * P], q, k, start=False, stop=(i == nh - 1))
                mm.then_inc(as_full, 1)

            def att_turn(u):
                pe.wait_ge(p_ready, u + 1)
                if u >= 2:
                    pe.wait_ge(pt_ready, u - 1)
                for i in range(4):
                    mm = pe.transpose(ps[:, 2 + u % 2, i * P:(i + 1) * P], ap_[:, u % 2, i * P:(i + 1) * P], ident)
                mm.then_inc(pt_full, 1)

            def att_values(u):
                g, blk, h0, nh, nk = UNITS[u]
                pe.wait_ge(pt_ready, u + 1)
                if u >= 2:
                    pe.wait_ge(o_ready, u - 1)
                for i in range(nh):
                    for k in range(nk):
                        hh = (h0 + i) * (HD + 1)
                        mm = pe.matmul(ps[:, 4 + u % 2, i * (HD + 1):(i + 1) * (HD + 1)],
                                       apt[:, u % 2, (i * nk + k) * P:(i * nk + k + 1) * P],
                                       av[:, g % 2, blk - (nk - 1) + k, hh:hh + HD + 1], start=(k == 0), stop=(k == nk - 1))
                mm.then_inc(ov_full, 1)

            NU = len(UNITS)
            att_scores(0)
            att_scores(1)
            att_turn(0)
            for u in range(NU):
                if u + 2 < NU:
                    att_scores(u + 2)
                if u + 1 < NU:
                    att_turn(u + 1)
                att_values(u)

            for n in range(NBLK):
                pe.wait_ge(ya_ready, n + 1)
                if n == 0:
                    pe.wait_ge(o_ready, NU)
                if n >= 2:
                    pe.wait_ge(yT_ready, n - 1)
                for i in range(2):
                    mm = pe.transpose(ps[:, n % 2, i * P:(i + 1) * P], yat[:, n % 2, i * P:(i + 1) * P], ident)
                mm.then_inc(yt_full, 1)

            def s_scores(b):
                if b == 0:
                    pe.wait_ge(sqr_ready, 1)
                    pe.wait_ge(yT_ready, NBLK)
                else:
                    pe.wait_ge(sp_ready, b)
                pe.wait_ge(s_in[b % 2], 32 * (b // 2 + 1))
                pe.matmul(ps[:, 0, 0:152], idb[:], smb[:, 0:152], start=True, stop=False)
                pe.matmul(ps[:, 1, :], idb[:], smb[:, 152:664], start=True, stop=False)
                pe.matmul(ps[:, 2, :], idb[:], smb[:, 664:1176], start=True, stop=False)
                for h in range(H):
                    row = slice(32 * h, 32 * h + 32)
                    pe.matmul(ps[row, 0, 0:128], sqr[:, 0, h, b, :], kc[:, b % 2, h, 0:128], start=False, stop=False)
                    for g in range(G):
                        pe.matmul(ps[row, 0, 128 + T * g:128 + T * g + T], sqr[:, g, h, b, :],
                                  sks[:, g, h, T * b:T * b + T], start=False, stop=(g == G - 1))
                    pe.matmul(ps[row, 1, :], sqr[:, 1, h, b, :], kc[:, b % 2, h, 128:640], start=False, stop=True)
                    mm = pe.matmul(ps[row, 2, :], sqr[:, 2, h, b, :], kc[:, b % 2, h, 640:1152], start=False, stop=True)
                mm.then_inc(ss2_full, 1)

            def s_turn(b):
                pe.wait_ge(sp_ready, b + 1)
                if b >= 1:
                    pe.wait_ge(spt_ready, b)
                for i in range(9):
                    a = 0 if i == 0 else 152 + (i - 1) * P
                    pe.transpose(ps[:, 3 + i // 4, (i % 4) * P:(i % 4 + 1) * P], spx[:, b % 2][:, a:a + P], ident)
                pe.transpose(ps[0:G * T, 5, P:2 * P], spx[:, b % 2][:, 128:152], ident).then_inc(st_full, 1)

            def s_values(b):
                pe.wait_ge(spt_ready, b + 1)
                if b >= 1:
                    pe.wait_ge(so_ready, b)
                for h in range(H):
                    row, e = slice(32 * h, 32 * h + 32), slice(h * (HD + 1), (h + 1) * (HD + 1))
                    for i in range(9):
                        pe.matmul(ps[row, 6, 0:HD + 1], spt[:, i, row], vc[:, b % 2, i, e], start=(i == 0), stop=False)
                    mm = pe.matmul(ps[row, 6, 0:HD + 1], spt[0:G * T, 9, row], vnw[:, b, e], start=False, stop=True)
                mm.then_inc(sv_full, 1)

            def s_out_turn(b):
                pe.wait_ge(so_ready, b + 1)
                if b >= 1:
                    pe.wait_ge(soT_ready, b)
                pe.transpose(ps[0:HD, 7, 0:P], so[:, b % 2, 0:HD], ident).then_inc(sot_full, 1)

            for b in range(NB):
                s_scores(b)
                s_turn(b)
                if b > 0:
                    s_out_turn(b - 1)
                s_values(b)
            s_out_turn(NB - 1)

            pe.wait_ge(slab_ready, S_UP + 3)
            pe.wait_ge(soT_ready, NB)
            jm = [(S_UP + i) % 3 for i in range(3)]
            for c, (a, w) in enumerate(CHUNKS):
                pe.wait_ge(mx_ready, 6 * (c + 1))
                for d in range(KT):
                    unit = PU_UP + KT * c + d
                    par = d % 2
                    pe.wait_ge(pair_free, unit + 1)
                    for k0, nk, full, half in ((0, 4, gate_full, 0), (4, 2, up_full, 1)):
                        products(bank(2 * par + half, w), lambda k: (
                            whi[:, jm[(k0 + k) // 2], (k % 2) * D + d * P:(k % 2) * D + (d + 1) * P],
                            wlo[:, jm[(k0 + k) // 2], (k % 2) * D + d * P:(k % 2) * D + (d + 1) * P],
                            mx_hi[:, k0 + k, 0:w], mx_lo[:, k0 + k, 0:w]), nk).then_inc(full, 1)
            pe.wait_ge(up_full, PU_FFN2)
            pe.sem_inc(slab_free, 3)
            for s in range(4):
                j = (S_OUT + s) % 3
                pe.wait_ge(slab_ready, S_OUT + s + 1)
                for c, (a, w) in enumerate(CHUNKS):
                    pe.wait_ge(pair_free, PU_UP + KT * (c + 1) + 2)
                    for dd in range(2):
                        v = AU_OUT + 6 * s + 2 * c + dd
                        pe.wait_ge(acc_free, v + 1)
                        products(bank(4 + v % 4, w), lambda k: (
                            whi[:, j, k * 256 + dd * P:k * 256 + (dd + 1) * P], wlo[:, j, k * 256 + dd * P:k * 256 + (dd + 1) * P],
                            h_hi[:, k, a:a + w], h_lo[:, k, a:a + w]), KT).then_inc(acc_full, 1)
                pe.wait_ge(acc_full, AU_OUT + 6 * s + 6)
                pe.sem_inc(slab_free, 1)

            norm(2, 4 + AU_FFN2)
            ffn(1)
            norm(3, 4 + AU_END)

        @block.scalar
        def _(act):
            eps = con[:, C_EPS:C_EPS + 1]

            def norm(n, x_done):
                def squares(c):
                    a, w = CHUNKS[c]
                    x_done(c)
                    for k in range(KT):
                        q = 24 * n + 8 * c + k
                        if q >= 2:
                            act.wait_ge(sq_free, q - 1)
                        act.activation(sq[:, q % 2, 0:w], x[:, k, a:a + w], ACT.Square).then_inc(sq_ready, 1)
                    act.wait_ge(sq_free, 24 * n + 8 * (c + 1))
                    if c == 2:
                        act.wait_ge(*((ht_ready, 24 * n + 8) if n < 3 else (y_ready, 8)))
                    act.activation(rstd[:, c % 2, 0:w], bank(4 + c, w), ACT.Sqrt, bias=eps, scale=1.0 / D).then_inc(std_ready, 1)

                def highs(c):
                    a, w = CHUNKS[c]
                    for k in range(KT):
                        q = 24 * n + 8 * c + k
                        act.wait_ge(ht_ready, q + 1)
                        act.activation(h_hi[:, k, a:a + w], htmp[:, q % 2, 0:w], ACT.Copy).then_inc(hhi_ready, 1)

                squares(0)
                squares(1)
                if n < 3:
                    highs(0)
                squares(2)
                if n < 3:
                    highs(1)
                    highs(2)

            def ffn(n):
                pu, fu = (0, 0) if n == 0 else (PU_FFN2, 6 * FFN_ITERS)
                with act.Fori(0, FFN_ITERS) as i:
                    for j in range(2):
                        for c, (a, w) in enumerate(CHUNKS):
                            k = 3 * j + c
                            par = k % 2
                            act.wait_ge(gate_full, 6 * i + (pu + k + 1))
                            act.activation(silu[:, par, 0:w], bank(2 * par, w), ACT.Silu).then_inc(silu_done, 1)
                            act.wait_ge(mul_done, 6 * i + (fu + k + 1))
                            act.activation(act_hi[:, j, a:a + w], bank(2 * par + 1, w), ACT.Copy).then_inc(acthi_done, 1)

            def x0(c):
                act.wait_ge(x_in[c], 16)
            act.wait_ge(con_in, 16)
            norm(0, x0)
            ffn(0)
            norm(1, lambda c: act.wait_ge(acc_free, 4 + AU_IF - 16 + 8 * c))

            act.wait_ge(acc_free, 4 + AU_IF)
            act.dma_start(cost[:], cos_t).then_inc(tab_in, 16)
            act.dma_start(sint[:], sin_t).then_inc(tab_in, 16)
            for c, (a, w) in enumerate(CHUNKS):
                act.wait_ge(if_staged, c + 1)
                act.dma_start(zif[:, a:a + w], zif_s[:, c, 0:w]).then_inc(if_stored, 16)
            act.wait_ge(if_stored, 48)
            for dst, h0 in ((zi, 0), (zf, H)):
                for h in range(H):
                    r = slice(8 * h, 8 * h + 8)
                    act.dma_start(dst[r, 0:P], zif[h0 + h, 0:SEQ].rearrange("(c t) -> c t", t=P)).then_inc(gates_in, 16)
                    act.dma_start(dst[r, P:W32], zif[h0 + h, SEQ:TOK].rearrange("(b t) -> b t", t=T)).then_inc(gates_in, 16)
            for s in range(5):
                for t in range(9):
                    n = 9 * s + t
                    rws, tok = (slice(0, P), slice(t * P, (t + 1) * P)) if t < 8 else (slice(SAMP, P), slice(SEQ, TOK))
                    act.wait_ge(v_staged, n + 1)
                    if s < 2:
                        act.dma_start(vm[tok, 2 * s:2 * s + 2, :], svm[rws, n % 2]).then_inc(v_stored[n % 2], 16)
                    else:
                        act.dma_start(va_out[tok, s - 2, :], sva[rws, n % 2].rearrange("p h e -> p (h e)")).then_inc(v_stored[n % 2], 16)

            def store(u, dst):
                act.dma_start(dst, stage[:, u % 2, :, 0:dst.shape[-1]]).then_inc(stored[u % 2], 16)

            def plain(u, kind, pair, c):
                a, w = CHUNKS[c]
                par = u % 2
                if u >= 2:
                    act.wait_ge(stored[par], 16 * (u // 2))
                for half, full in ((0, gate_full), (1, up_full)):
                    act.wait_ge(full, PU_F + u + 1)
                    ins = act.activation(stage[:, par, half, 0:w], bank(2 * par + half, w),
                                         ACT.Sigmoid if kind == 2 else ACT.Copy, scale=DK ** -0.5 if kind == 1 else 1.0)
                ins.then_inc(pair_free, 1)
                act.wait_ge(pair_free, 2 + PU_F + u + 1)
                store(u, zqko[4 * kind + 2 * pair:4 * kind + 2 * pair + 2, :, a:a + w].rearrange("j p t -> p j t"))

            for j in range(3):
                for c in range(NC):
                    plain(3 * j + c, j, 0, c)

            act.wait_ge(gna_ready, 1)
            act.activation(ge[:], gna[:], ACT.Exp).then_inc(ge_ready, 1)
            act.wait_ge(ge_ready, 1)
            act.activation(gl[:], ge[:], ACT.Ln, bias=con[0:32, C_ONE:C_ONE + 1]).then_inc(gl_ready, 1)
            for j in range(3):
                for c in range(NC):
                    plain(9 + 3 * j + c, j, 1, c)
            act.wait_ge(blk_ready, 1)
            act.dma_start(lastrow[0].unsqueeze(1), scan_b[:, 1, 191:192]).then_inc(grow_io, 16)
            act.dma_start(lastrow[1].unsqueeze(1), scan_g[:, 1, 191:192]).then_inc(grow_io, 16)
            act.wait_ge(grow_io, 32)
            act.dma_start(lrow[:], lastrow.unsqueeze(0)).then_inc(grow_io, 16)
            act.wait_ge(mrow_ready, 1)
            act.dma_start(m_out.unsqueeze(0), mrow[:]).then_inc(grows_out, 16)
            act.wait_ge(grows_out, 16)
            for h in range(H):
                act.dma_start(mcol[8 * h:8 * h + 8, :], m_out[h, 0:8].unsqueeze(1)).then_inc(grow_io, 16)
            act.wait_ge(gM_ready, 1)
            for n, t in enumerate((ge, gl, gna)):
                for h in range(H):
                    r = slice(8 * h, 8 * h + 8)
                    act.dma_start(rows[n, h, 0:SEQ].rearrange("(c t) -> c t", t=P), t[r, 0:P]).then_inc(grows_out, 16)
                    act.dma_start(rows[n, h, SEQ:TOK].rearrange("(b t) -> b t", t=T), t[r, P:W32]).then_inc(grows_out, 16)
            act.dma_start(ms_out, gmn[:, P + T - 1:P + T]).then_inc(ms_stored, 16)

            for j in range(6):
                for c, (a, w) in enumerate(CHUNKS):
                    u = 18 + 3 * j + c
                    act.wait_ge(rope_ready, 3 * j + c + 1)
                    act.sem_inc(pair_free, 1)
                    dst = (qr if j < 3 else kr_out)[j % 3]
                    store(u, dst[:, :, a:a + w].rearrange("s p t -> p s t"))
            with act.Fori(0, 4) as i:
                for j in range(2):
                    for c, (a, w) in enumerate(CHUNKS):
                        k = 3 * j + c
                        par = k % 2
                        act.wait_ge(stored[par], 48 * i + 16 * (18 + k // 2))
                        for half, full in ((0, gate_full), (1, up_full)):
                            act.wait_ge(full, 6 * i + (PU_F + 36 + k + 1))
                            ins = act.activation(stage[:, par, half, 0:w], bank(2 * par + half, w), ACT.Sigmoid)
                        ins.then_inc(pair_free, 1)
                        act.wait_ge(pair_free, 6 * i + (2 + PU_F + 36 + k + 1))
                        act.dma_start(zgate.rearrange("(i j s) p t -> i j p s t", j=2, s=2)[i, j, :, :, a:a + w],
                                      stage[:, par, :, 0:w]).then_inc(stored[par], 16)

            def exps(h):
                s = h % 2
                act.wait_ge(arg_ready, h + 1)
                act.activation(Wd[:, s, 0:SEQ], Wd[:, s, 0:SEQ], ACT.Exp)
                act.activation(Wd[0:SAMP, s, SEQ:TOK], Wd[0:SAMP, s, SEQ:TOK], ACT.Exp)
                act.activation(qw[:, s], qw[:, s], ACT.Exp)
                act.activation(ecol[:, s], ecol[:, s], ACT.Exp)
                act.activation(wsc[:, s, 1:2], wsc[:, s, 1:2], ACT.Exp)
                act.activation(nm[:, s], nm[:, s], ACT.Exp).then_inc(exp_ready, 1)

            def keys(w):
                h, c = divmod(w, 9)
                act.wait_ge(ts_full, w + 1)
                if c == 0:
                    act.wait_ge(exp_ready, h + 1)
                if w >= 2:
                    act.wait_ge(cu_full, 8 * ((w - 2) // 9) + min((w - 2) % 9 + 1, 8))
                    act.wait_ge(su_full, 8 * ((w - 1) // 9))
                if c < 8:
                    act.activation(kw[:, w % 2, :], ps[:, 2 + w % 2, 0:P], ACT.Copy,
                                   scale=ecol[:, h % 2, 2, c:c + 1]).then_inc(kw_ready, 1)
                else:
                    act.activation(kw[0:SAMP, w % 2, :], ps[0:SAMP, 2 + w % 2, 0:P], ACT.Copy).then_inc(kw_ready, 1)

            def head_squares(h):
                act.wait_ge(hn_ready, 9 * (h + 1))
                if h > 0:
                    act.wait_ge(hm_out, 16 * h)
                act.activation(ss[:], hn[:, h % 2], ACT.Square).then_inc(sqh_ready, 1)

            def head_scale(h):
                for c, (a, w) in enumerate(CHUNKS):
                    act.wait_ge(ss_full, 3 * h + c + 1)
                    act.activation(ss[:, a:a + w], bank(7, w), ACT.Ln, bias=eps, scale=1.0 / DK).then_inc(rs_read, 1)
                act.wait_ge(rs_read, 3 * h + 3)
                act.activation(ss[:], ss[:], ACT.Exp, scale=-0.5).then_inc(rs_ready, 1)

            exps(0)
            for h in range(H):
                for c in range(9):
                    keys(9 * h + c)
                    if c == 1 and h > 0:
                        head_scale(h - 1)
                    if c == 7 and h + 1 < H:
                        exps(h + 1)
                head_squares(h)
            head_scale(H - 1)

            for u, (g, blk, h0, nh, nk) in enumerate(UNITS):
                act.wait_ge(mx_full, u + 1)
                if u >= 2:
                    act.wait_ge(pt_full, u - 1)
                wd = nk * P
                for i in range(nh):
                    ins = act.activation(ap_[:, u % 2, i * wd:(i + 1) * wd], ps[:, u % 2, i * wd:(i + 1) * wd], ACT.Exp,
                                         bias=amx[:, u % 4, i:i + 1])
                ins.then_inc(p_ready, 1)
            for n in range(NBLK):
                act.wait_ge(ocw_ready, n + 1)
                act.activation(ocw[:, n % 2], ocw[:, n % 2], ACT.Exp).then_inc(oce_ready, 1)
            for b in range(NB):
                act.wait_ge(smx_ready, b + 1)
                if b >= 2:
                    act.wait_ge(st_full, b - 1)
                m = smx[:, b % 2, 3:4]
                act.activation(spx[:, b % 2, 0:152], ps[:, 0, 0:152], ACT.Exp, bias=m)
                act.activation(spx[:, b % 2, 152:664], ps[:, 1, :], ACT.Exp, bias=m)
                act.activation(spx[:, b % 2, 664:1176], ps[:, 2, :], ACT.Exp, bias=m).then_inc(sp_ready, 1)

            for c, (a, w) in enumerate(CHUNKS):
                if c > 0:
                    act.wait_ge(up_full, PU_UP + KT * c)
                for k in range(6):
                    n = 6 * c + k
                    act.wait_ge(mx_in[n % 2], 16 * (n // 2 + 1))
                    act.activation(mx_hi[:, k, 0:w], mxin[:, n % 2, 0:w], ACT.Copy).then_inc(mx_hid, 1)
                for d in range(KT):
                    n = KT * c + d
                    act.wait_ge(mg_ready, n + 1)
                    act.activation(h_hi[:, d, a:a + w], bank(2 * (d % 2) + 1, w), ACT.Copy).then_inc(mg_hid, 1)

            norm(2, lambda c: act.wait_ge(acc_free, 4 + AU_OUT + 18 + 2 * (c + 1)))
            ffn(1)
            norm(3, lambda c: act.wait_ge(acc_free, 4 + AU_END - 16 + 8 * c))
            act.wait_ge(ms_stored, 16)

        @block.vector
        def _(dve):
            steps = [0]

            def link(ins):
                steps[0] += 1
                ins.then_inc(dve_step, 1)
                dve.wait_ge(dve_step, steps[0])

            dve.sem_inc(acc_free, 4)
            dve.sem_inc(pair_free, 2)
            dve.sem_inc(slab_free, 3)
            dve.wait_ge(con_in, 16)
            dve.tensor_copy(idb[:], con[:, C_ID:C_ID + P]).then_inc(idb_ready, 1)

            def norm(n, x_done):
                gains = con[:, C_G + 8 * n:C_G + 8 * n + 8]

                def scaled(c, k):
                    a, w = CHUNKS[c]
                    q = 24 * n + 8 * c + k
                    if k == 0:
                        x_done(c)
                        dve.wait_ge(std_ready, 3 * n + c + 1)
                        dve.reciprocal(rstd[:, c % 2, 0:w], rstd[:, c % 2, 0:w]).then_inc(rstd_ready, 1)
                        dve.wait_ge(rstd_ready, 3 * n + c + 1)
                    if n < 3:
                        if q >= 2:
                            dve.wait_ge(h_ready, q - 1)
                    elif q - 72 >= 2:
                        dve.wait_ge(y_stored[q % 2], 16 * ((q - 72) // 2))
                    ins = dve.scalar_tensor_tensor(htmp[:, q % 2, 0:w], x[:, k, a:a + w], gains[:, k:k + 1],
                                                   rstd[:, c % 2, 0:w], ALU.mult, ALU.mult)
                    ins.then_inc(ht_ready if n < 3 else y_ready, 1)

                def low(c, k):
                    a, w = CHUNKS[c]
                    q = 24 * n + 8 * c + k
                    dve.wait_ge(hhi_ready, q + 1)
                    dve.tensor_tensor(h_lo[:, k, a:a + w], htmp[:, q % 2, 0:w], h_hi[:, k, a:a + w].bitcast(F32),
                                      ALU.subtract).then_inc(h_ready, 1)

                order = [(c, k) for c in range(NC) for k in range(KT)]
                scaled(*order[0])
                for m, (c, k) in enumerate(order):
                    if m + 1 < len(order):
                        scaled(*order[m + 1])
                    if n < 3:
                        low(c, k)

            def ffn(n):
                pu, fu, au = (0, 0, 0) if n == 0 else (PU_FFN2, 6 * FFN_ITERS, AU_FFN2)
                with dve.Fori(0, FFN_ITERS) as i:
                    for j in range(2):
                        for c, (a, w) in enumerate(CHUNKS):
                            k = 3 * j + c
                            par = k % 2
                            up = bank(2 * par + 1, w)
                            dve.wait_ge(silu_done, 6 * i + (fu + k + 1))
                            dve.wait_ge(up_full, 6 * i + (pu + k + 1))
                            dve.tensor_tensor(up, silu[:, par, 0:w], up, ALU.mult).then_inc(mul_done, 1)
                            dve.wait_ge(acthi_done, 6 * i + (fu + k + 1))
                            dve.tensor_tensor(act_lo[:, j, a:a + w], up, act_hi[:, j, a:a + w].bitcast(F32),
                                              ALU.subtract).then_inc(pair_free, 1)
                    dve.wait_ge(acc_free, 24 * i + (au + 4))
                    for c, (a, w) in enumerate(CHUNKS):
                        for d in range(KT):
                            v = 8 * c + d
                            dve.wait_ge(acc_full, 24 * i + (au + v + 1))
                            dve.scalar_tensor_tensor(x[:, d, a:a + w], bank(4 + v % 4, w), 0.5, x[:, d, a:a + w],
                                                     ALU.mult, ALU.add).then_inc(acc_free, 1)

            norm(0, lambda c: dve.wait_ge(x_in[c], 16))
            ffn(0)
            norm(1, lambda c: dve.wait_ge(acc_free, 4 + AU_IF - 16 + 8 * c))

            for c, (a, w) in enumerate(CHUNKS):
                dve.wait_ge(acc_full, AU_IF + c + 1)
                dve.tensor_copy(zif_s[:, c, 0:w], ps[0:8, 4 + c, 0:w]).then_inc(if_staged, 1)
                dve.wait_ge(if_staged, c + 1)
                dve.sem_inc(acc_free, 1)
            dve.memset(svm[:], 1.0)
            link(dve.memset(sva[:], 1.0))
            for s in range(5):
                for t in range(9):
                    n = 9 * s + t
                    v = AU_V + n
                    r = slice(0, P) if t < 8 else slice(SAMP, P)
                    dve.wait_ge(acc_full, v + 1)
                    if n >= 2:
                        dve.wait_ge(v_stored[n % 2], 16 * (n // 2))
                    if s < 2:
                        dst, nh = svm[r, n % 2, :, 0:DK], 2
                    else:
                        dst, nh = sva[r, n % 2, :, 0:HD], H
                    dve.tensor_copy(dst, ps[r, 4 + v % 4, 0:256].rearrange("p (h e) -> p h e", h=nh)).then_inc(v_staged, 1)
                    dve.wait_ge(v_staged, n + 1)
                    dve.sem_inc(acc_free, 1)

            col = lambda c: con[0:32, c:c + 1]
            dve.wait_ge(gates_in, 16 * 16)
            dve.tensor_scalar(zi[:], zi[:], col(C_BI), None, ALU.add)
            link(dve.tensor_scalar(zf[:], zf[:], col(C_BF), None, ALU.add))
            dve.tensor_scalar(gmn[:], zf[:], 0.0, None, ALU.min)
            dve.scalar_tensor_tensor(gna[:], zf[:], -1.0, zf[:], ALU.mult, ALU.min).then_inc(gna_ready, 1)
            dve.memset(scan_b[:], 0.0)
            link(dve.memset(scan_g[:], -3e38))
            dve.wait_ge(gl_ready, 1)
            parts = ((64, 0, P, 7), (196, P, T, 3))
            for o, a, w, _ in parts:
                last = dve.tensor_tensor(scan_b[:, 0, o:o + w], gmn[:, a:a + w], gl[:, a:a + w], ALU.subtract)
            link(last)

            def scan(buf, op):
                for k in range(7):
                    for o, _, w, n in parts:
                        if k < n:
                            last = dve.tensor_tensor(buf[:, (k + 1) % 2, o:o + w], buf[:, k % 2, o:o + w],
                                                     buf[:, k % 2, o - 2 ** k:o - 2 ** k + w], op)
                    link(last)

            scan(scan_b, ALU.add)
            for o, a, w, _ in parts:
                dve.tensor_tensor(scan_g[:, 0, o:o + w], zi[:, a:a + w], scan_b[:, 1, o:o + w], ALU.subtract)
                last = dve.tensor_tensor(gna[:, a:a + w], zi[:, a:a + w], scan_b[:, 1, o:o + w], ALU.subtract)
            link(last)
            scan(scan_g, ALU.max)
            dve.memset(mrow[:, :, 0:1], 0.0).then_inc(blk_ready, 1)
            dve.wait_ge(blk_ready, 1)
            dve.wait_ge(grow_io, 48)
            lr = lrow[:].rearrange("p a (h c) -> p a h c", h=H)
            for c in range(NBLK):
                link(dve.tensor_tensor(mtmp[:, c, :], mrow[:, :, c], lr[:, 1, :, c], ALU.max))
                ins = dve.tensor_tensor(mrow[:, :, c + 1], mtmp[:, c, :], lr[:, 0, :, c], ALU.add)
                link(ins)
            dve.sem_inc(mrow_ready, 1)
            dve.wait_ge(grow_io, 48 + 64)
            for (o, a, w, _), m in zip(parts, (mcol[:], col(C_MS))):
                link(dve.tensor_scalar(zi[:, a:a + w], scan_g[:, 1, o:o + w], m, None, ALU.max))
                dve.tensor_scalar(ge[:, a:a + w], zi[:, a:a + w], -1.0, None, ALU.mult)
                link(dve.tensor_tensor(gmn[:, a:a + w], zi[:, a:a + w], scan_b[:, 1, o:o + w], ALU.add))
                last = dve.tensor_scalar(gl[:, a:a + w], gmn[:, a:a + w], -1.0, None, ALU.mult)
            last.then_inc(gM_ready, 1)

            dve.wait_ge(tab_in, 32)
            for j in range(6):
                for c, (a, w) in enumerate(CHUNKS):
                    u = 18 + 3 * j + c
                    par = u % 2
                    scale = HD ** -0.5 if j < 3 else 1.0
                    A, B = bank(2 * par, w), bank(2 * par + 1, w)
                    dve.wait_ge(stored[par], 16 * (u // 2))
                    dve.wait_ge(up_full, PU_F + u + 1)
                    o1, o2 = stage[:, par, 0, 0:w], stage[:, par, 1, 0:w]
                    stt = dve.scalar_tensor_tensor
                    link(stt(o1, A, scale, cost[:, a:a + w], ALU.mult, ALU.mult))
                    link(stt(o2, A, scale, sint[:, a:a + w], ALU.mult, ALU.mult))
                    stt(A, B, scale, sint[:, a:a + w], ALU.mult, ALU.mult)
                    link(stt(B, B, scale, cost[:, a:a + w], ALU.mult, ALU.mult))
                    dve.tensor_tensor(o1, o1, A, ALU.subtract)
                    dve.tensor_tensor(o2, o2, B, ALU.add).then_inc(rope_ready, 1)

            def args(h):
                s = h % 2
                dve.wait_ge(head_in[s], 128 * (h // 2 + 1))
                blocks = lambda t: t[:, 0:SEQ].rearrange("p (c t) -> p c t", t=P)
                samples = lambda t: t[:, SEQ:TOK].rearrange("p (b t) -> p b t", t=T)
                nMp, nMs = blocks(nM[:, s]), samples(nM[:, s])
                for c in range(NBLK):
                    dve.scalar_tensor_tensor(Wd[:, s, c * P:(c + 1) * P], nMp[:, c, :], gcol[:, c, h:h + 1],
                                             msk[:, M_CAUSAL:M_CAUSAL + P], ALU.add, ALU.add)
                dve.scalar_tensor_tensor(Wd[0:SAMP, s, SEQ:TOK], nM[0:SAMP, s, SEQ:TOK], gcol[0:SAMP, 8, h:h + 1],
                                         msk[0:SAMP, M_SAMPLE:M_SAMPLE + SAMP], ALU.add, ALU.add)
                dve.tensor_tensor(blocks(qw[:, s]), nMp, mpb[:, h, :].unsqueeze(2).to_broadcast([P, 8, P]), ALU.add)
                dve.tensor_tensor(samples(qw[:, s]), nMs, msb[:, h, :].unsqueeze(2).to_broadcast([P, 8, T]), ALU.add)
                dve.tensor_tensor(ecol[:, s, 0, :], mpb[:, h, :], nMp[:, :, P - 1], ALU.add)
                dve.tensor_tensor(ecol[:, s, 1, :], msb[:, h, :], nMs[:, :, T - 1], ALU.add)
                dve.tensor_tensor(ecol[:, s, 2, :], gcol[:, 0:8, h], nMp[:, :, P - 1], ALU.add)
                link(dve.tensor_tensor(own[:, s, :], nMs[0:SAMP, :, T - 1], msk[0:SAMP, M_BLOCK:M_BLOCK + NB], ALU.mult))
                link(dve.tensor_reduce(wsc[:, s, 0:1], own[:, s, :], AX.X, ALU.add))
                dve.tensor_tensor(wsc[:, s, 1:2], wsc[:, s, 0:1], gcol[0:SAMP, 8, h:h + 1], ALU.add).then_inc(arg_ready, 1)

            def queries(h):
                s = h % 2
                dve.wait_ge(exp_ready, h + 1)
                dve.tensor_tensor(qw[:, s], qT[:, s], qw[:, s], ALU.mult).then_inc(qw_ready, 1)

            def sample_parts(h):
                s = h % 2
                dve.wait_ge(qw_ready, h + 1)
                dve.tensor_tensor(qn[:].rearrange("p (b t) -> p b t", t=T),
                                  qw[:, s, SEQ:TOK].rearrange("p (b t) -> p b t", t=T),
                                  Cs[:, s, :, DK:DK + 1].to_broadcast([P, NB, T]), ALU.mult)
                link(dve.tensor_scalar(own[:, s, :], msk[0:SAMP, M_BLOCK:M_BLOCK + NB], wsc[:, s, 1:2], None, ALU.mult))
                for b in range(NB):
                    ins = dve.tensor_scalar(vex[:, b, :], v1[0:SAMP, s, 8, :], own[:, s, b:b + 1], None, ALU.mult)
                ins.then_inc(samp_ready, 1)

            def weights(w):
                h, c = divmod(w, 9)
                n = P if c < 8 else SAMP
                dve.wait_ge(ts_full, w + 1)
                if c == 0:
                    dve.wait_ge(exp_ready, h + 1)
                if w >= 2:
                    dve.wait_ge(nd_full, w - 1)
                dve.tensor_tensor(Pm[0:n, w % 2, 0:n], ps[0:n, w % 2, 0:n], Wd[0:n, h % 2, c * P:c * P + n],
                                  ALU.mult).then_inc(pm_ready, 1)

            def new_state(w):
                h, c = divmod(w, 9)
                n = 8 * h + c
                dve.wait_ge(cu_full, n + 1)
                if w > 0:
                    dve.wait_ge(nd_full, w)
                if n > 0:
                    dve.wait_ge(cp_ready, n)
                if c == 1 and h > 0:
                    dve.wait_ge(cp_out, 16 * h)
                dst = Cp[:, (c + 1) % 2]
                if c == 0:
                    dve.tensor_copy(dst, ps[:, 6, 0:DK + 1]).then_inc(cp_ready, 1)
                else:
                    dve.scalar_tensor_tensor(dst, Cp[:, c % 2], ecol[:, h % 2, 0, c:c + 1], ps[:, 6, 0:DK + 1],
                                             ALU.mult, ALU.add).then_inc(cp_ready, 1)

            def sample_states(h):
                for b in range(NB):
                    n = 8 * h + b
                    dve.wait_ge(su_full, n + 1)
                    dve.scalar_tensor_tensor(Cs[:, h % 2, b], Cs[:, h % 2, b], ecol[:, h % 2, 1, b:b + 1],
                                             ps[:, 6 + b % 2, 0:DK + 1], ALU.mult, ALU.add).then_inc(cs_ready, 1)

            def hidden(w):
                h, c = divmod(w, 9)
                n = P if c < 8 else SAMP
                b = 4 + w % 2
                tok = slice(c * P, c * P + n)
                dve.wait_ge(nd_full, w + 1)
                if w > 0:
                    dve.wait_ge(hn_ready, w)
                link(dve.scalar_tensor_tensor(den[:, 0:n], ps[:, b, P:P + n], -1.0, nm[:, h % 2, tok], ALU.mult, ALU.max))
                link(dve.tensor_tensor(den[:, 0:n], ps[:, b, P:P + n], den[:, 0:n], ALU.max))
                link(dve.reciprocal(den[:, 0:n], den[:, 0:n]))
                dve.tensor_tensor(hn[:, h % 2, tok], ps[:, b, 0:n], den[:, 0:n], ALU.mult).then_inc(hn_ready, 1)

            def finish(h):
                dve.wait_ge(rs_ready, h + 1)
                link(dve.scalar_tensor_tensor(ss[:], hn[:, h % 2], con[:, C_GM + h:C_GM + h + 1], ss[:], ALU.mult, ALU.mult))
                dve.tensor_tensor(ss[:], ss[:], oT[:, h % 2], ALU.mult).then_inc(head_done, 1)

            dve.wait_ge(mix_const, 16 * 8)
            args(0)
            queries(0)
            weights(0)
            for w in range(9 * H):
                h, c = divmod(w, 9)
                if w + 1 < 9 * H:
                    weights(w + 1)
                if c < 8:
                    new_state(w)
                hidden(w)
                if c == 1 and h > 0:
                    finish(h - 1)
                if c == 5 and h + 1 < H:
                    args(h + 1)
                if c == 7:
                    sample_parts(h)
                if c == 8:
                    sample_states(h)
                    if h + 1 < H:
                        queries(h + 1)
            finish(H - 1)

            dve.wait_ge(att_const, 16)
            dve.wait_ge(idb_ready, 1)
            dve.tensor_copy(amb[:], amf[:, 0:384]).then_inc(amb_ready, 1)

            def att_max(u):
                nh = UNITS[u][3]
                dve.wait_ge(as_full, u + 1)
                if u >= 4:
                    dve.wait_ge(o_ready, u - 3)
                dve.tensor_reduce(amx[:, u % 4, 0:nh], ps[:, u % 2, :].rearrange("p (h k) -> p h k", h=nh), AX.X, ALU.max,
                                  negate=True).then_inc(mx_full, 1)

            def att_copy(u):
                dve.wait_ge(pt_full, u + 1)
                if u >= 2:
                    dve.wait_ge(ov_full, u - 1)
                dve.tensor_copy(apt[:, u % 2, :], ps[:, 2 + u % 2, :]).then_inc(pt_ready, 1)

            def att_out(u):
                nh = UNITS[u][3]
                dve.wait_ge(ov_full, u + 1)
                if u >= 2:
                    dve.wait_ge(o_stored[u % 2], 16 * (u // 2))
                dve.tensor_copy(ao[:, u % 2, 0:nh, 0:HD + 1], ps[:, 4 + u % 2, 0:nh * (HD + 1)].rearrange("p (h e) -> p h e", h=nh))
                dve.tensor_copy(ao[:, u % 2, 0:nh, HD + 1], amx[:, u % 4, 0:nh]).then_inc(o_ready, 1)

            NU = len(UNITS)
            att_max(0)
            att_max(1)
            att_copy(0)
            for u in range(NU):
                if u + 2 < NU:
                    att_max(u + 2)
                if u + 1 < NU:
                    att_copy(u + 1)
                att_out(u)

            for n in range(NBLK):
                s = n % 2
                dve.wait_ge(c_in[s], 16 * (n // 2 + 1))
                if n >= 2:
                    dve.wait_ge(ya_ready, n - 1)
                nmax = oc[:, s, :, :, HD + 1]
                link(dve.tensor_tensor(ocm[:, s], nmax[:, 0], nmax[:, 1], ALU.min))
                link(dve.tensor_tensor(ocm[:, s], ocm[:, s], nmax[:, 2], ALU.min))
                dve.tensor_tensor(ocw[:, s], ocm[:, s].unsqueeze(1).to_broadcast([P, G, H]), nmax,
                                  ALU.subtract).then_inc(ocw_ready, 1)
                dve.wait_ge(oce_ready, n + 1)
                for g in range(G):
                    last = dve.tensor_tensor(oc[:, s, g, :, 0:HD + 1], oc[:, s, g, :, 0:HD + 1],
                                             ocw[:, s, g, :].unsqueeze(2).to_broadcast([P, H, HD + 1]), ALU.mult)
                link(last)
                link(dve.tensor_tensor(oacc[:, s], oc[:, s, 0, :, 0:HD + 1], oc[:, s, 1, :, 0:HD + 1], ALU.add))
                dve.tensor_tensor(oacc[:, s], oacc[:, s], oc[:, s, 2, :, 0:HD + 1], ALU.add).then_inc(oc_read, 1)
                dve.wait_ge(oc_read, n + 1)
                link(dve.reciprocal(ocm[:, s], oacc[:, s, :, HD]))
                dve.tensor_tensor(yat[:, s].rearrange("p (h e) -> p h e", h=H), oacc[:, s, :, 0:HD],
                                  ocm[:, s].unsqueeze(2).to_broadcast([P, H, HD]), ALU.mult).then_inc(ya_ready, 1)
                dve.wait_ge(yt_full, n + 1)
                if n >= 2:
                    dve.wait_ge(c_out_[s], 16 * (n // 2))
                dve.tensor_copy(yT[:, s].rearrange("p j t -> p (j t)"), ps[:, n % 2, 0:256]).then_inc(yT_ready, 1)

            dve.wait_ge(s_const, 16 * (5 * G + 1))
            dve.tensor_copy(smb[:], spx[:, 1, :])
            for g in range(G):
                for h in range(H):
                    ins = dve.tensor_copy(sqr[:, g, h].rearrange("p b (r t) -> p b r t", t=T),
                                          sqs[:, g, h].rearrange("p (b t) -> p b t", t=T).unsqueeze(2).to_broadcast([HD, NB, 4, T]))
            ins.then_inc(sqr_ready, 1)
            dve.wait_ge(sqr_ready, 1)
            for b in range(NB):
                s = b % 2
                dve.wait_ge(ss2_full, b + 1)
                dve.tensor_reduce(smx[:, s, 0:1], ps[:, 0, 0:152], AX.X, ALU.max)
                dve.tensor_reduce(smx[:, s, 1:2], ps[:, 1, :], AX.X, ALU.max)
                link(dve.tensor_reduce(smx[:, s, 2:3], ps[:, 2, :], AX.X, ALU.max))
                dve.tensor_reduce(smx[:, s, 3:4], smx[:, s, 0:3], AX.X, ALU.max, negate=True).then_inc(smx_ready, 1)
                if b > 0:
                    dve.wait_ge(sot_full, b)
                    dve.tensor_copy(soT[:, :, b - 1, :], ps[0:HD, 7, 0:P].rearrange("p (h r) -> p h r", h=H)[:, :, 0:T]).then_inc(soT_ready, 1)
                dve.wait_ge(st_full, b + 1)
                dve.tensor_copy(spt[:, 0:4, :], ps[:, 3, :].rearrange("p (i t) -> p i t", t=P))
                dve.tensor_copy(spt[:, 4:8, :], ps[:, 4, :].rearrange("p (i t) -> p i t", t=P))
                dve.tensor_copy(spt[:, 8, :], ps[:, 5, 0:P])
                dve.tensor_copy(spt[0:G * T, 9, :], ps[0:G * T, 5, P:2 * P]).then_inc(spt_ready, 1)
                dve.wait_ge(sv_full, b + 1)
                link(dve.reciprocal(smx[:, s, 0:1], ps[:, 6, HD:HD + 1]))
                dve.tensor_scalar(so[:, s, 0:HD], ps[:, 6, 0:HD], smx[:, s, 0:1], None, ALU.mult).then_inc(so_ready, 1)
            dve.wait_ge(sot_full, NB)
            dve.tensor_copy(soT[:, :, NB - 1, :], ps[0:HD, 7, 0:P].rearrange("p (h r) -> p h r", h=H)[:, :, 0:T]).then_inc(soT_ready, 1)

            for c, (a, w) in enumerate(CHUNKS):
                for k in range(6):
                    n = 6 * c + k
                    dve.wait_ge(mx_hid, n + 1)
                    dve.tensor_tensor(mx_lo[:, k, 0:w], mxin[:, n % 2, 0:w], mx_hi[:, k, 0:w].bitcast(F32),
                                      ALU.subtract).then_inc(mx_ready, 1)
                for d in range(KT):
                    n = KT * c + d
                    A, B = bank(2 * (d % 2), w), bank(2 * (d % 2) + 1, w)
                    dve.wait_ge(sg_in[n % 2], 16 * (n // 2 + 1))
                    dve.wait_ge(gate_full, PU_UP + n + 1)
                    if n > 0:
                        dve.wait_ge(mg_ready, n)
                    dve.tensor_tensor(mgt[:, 0:w], A, sgate[:, n % 2, 0, 0:w], ALU.mult)
                    dve.wait_ge(up_full, PU_UP + n + 1)
                    dve.tensor_tensor(B, B, sgate[:, n % 2, 1, 0:w], ALU.mult).then_inc(sg_read, 1)
                    dve.wait_ge(sg_read, n + 1)
                    dve.tensor_tensor(B, B, mgt[:, 0:w], ALU.add).then_inc(mg_ready, 1)
                    dve.wait_ge(mg_hid, n + 1)
                    dve.tensor_tensor(h_lo[:, d, a:a + w], B, h_hi[:, d, a:a + w].bitcast(F32),
                                      ALU.subtract).then_inc(pair_free, 1)
            for s in range(4):
                for c, (a, w) in enumerate(CHUNKS):
                    for dd in range(2):
                        v = AU_OUT + 6 * s + 2 * c + dd
                        d = 2 * s + dd
                        dve.wait_ge(acc_full, v + 1)
                        dve.tensor_tensor(x[:, d, a:a + w], bank(4 + v % 4, w), x[:, d, a:a + w], ALU.add).then_inc(acc_free, 1)

            norm(2, lambda c: dve.wait_ge(acc_free, 4 + AU_OUT + 18 + 2 * (c + 1)))
            ffn(1)
            norm(3, lambda c: dve.wait_ge(acc_free, 4 + AU_END - 16 + 8 * c))


def constants():
    ident = np.eye(P, dtype=np.float32)
    t = np.arange(P)
    masks = np.zeros((P, M_N), np.float32)
    masks[:, M_CAUSAL:M_CAUSAL + P] = np.where(t[:, None] <= t[None, :], 0.0, NEG)
    a = np.arange(SAMP)
    same = a[:, None] // T == a[None, :] // T
    masks[0:SAMP, M_SAMPLE:M_SAMPLE + SAMP] = np.where(same & (a[:, None] <= a[None, :]), 0.0, NEG)
    masks[0:SAMP, M_BLOCK:M_BLOCK + NB] = a[:, None] // T == np.arange(NB)[None, :]
    am = np.zeros((P, A_N), np.float32)
    k = np.arange(2 * P)
    dist = t[:, None] + P - k[None, :]
    am[:, A_BAND:A_BAND + 2 * P] = np.where((dist >= 0) & (dist <= 128), 0.0, NEG)
    am[:, A_PAIR:A_PAIR + P] = np.where((t[:, None] % 2 == t[None, :] % 2) & (t[None, :] <= t[:, None]), 0.0, NEG)
    q = (t % T)[:, None]
    new = np.arange(T)[None, :]
    g2 = np.arange(512)[None, :]
    ok = np.concatenate([t[None, :] >= q,
                         new <= q, (new <= q) & ((q - new) % 4 == 0), new == q,
                         (g2 >= q) & ((g2 - q) % 4 == 0),
                         g2 % 8 == q], 1)
    am[:, A_SAMP:A_N] = np.where(ok, 0.0, NEG)
    half = HD // 2
    inv = np.float32(10000.0) ** (np.float32(-2.0) * np.arange(half, dtype=np.float32) / np.float32(HD))
    pos = np.concatenate([np.arange(SEQ), np.tile(SEQ + np.arange(T), NB)]).astype(np.float32)
    ang = np.tile((inv[:, None] * pos[None, :]).astype(np.float32), (4, 1)).astype(np.float64)
    return ident, masks, am, np.cos(ang).astype(np.float32), np.sin(ang).astype(np.float32)


def kernel(x_prompt, x_sample, state_mlstm_C, state_mlstm_n, state_mlstm_m,
           cache_win128_kv, cache_win512_kv, cache_win2048_kv,
           g_ffn1, w1_gate, w1_up, w1_down, g_mix, w_in, b_igate, b_fgate, g_mhead,
           w_up_m, w_up_a, w_out, g_ffn2, w2_gate, w2_up, w2_down, g_final):
    import concourse.bacc as bacc
    from concourse.bass_utils import run_bass_kernel_spmd

    A = np.asarray
    f32 = np.float32
    ident, masks, am, cos_t, sin_t = constants()
    feat = lambda a, n: A(a).reshape(n, P).T
    x = np.concatenate([A(x_prompt).reshape(SEQ, D), A(x_sample).reshape(SAMP, D)], 0)
    xT = np.ascontiguousarray(x.T.reshape(KT, P, TOK).transpose(1, 0, 2))

    stream = np.zeros((SLABS, P, SLAB), f32)
    tiles = lambda w: A(w).reshape(w.shape[0] // P, P, w.shape[1])

    def ffn(s0, wg, wu, wd):
        both = np.stack([tiles(wg[0]), tiles(wu[0])], 0).reshape(2, KT, P, FFN_ITERS, 2, P)
        v = stream[s0:s0 + 3 * FFN_ITERS].reshape(FFN_ITERS, 3, P, SLAB)
        v[:, 0:2] = both.transpose(3, 4, 2, 0, 1, 5).reshape(FFN_ITERS, 2, P, SLAB)
        v[:, 2] = tiles(wd[0]).reshape(FFN_ITERS, 2, P, D).transpose(0, 2, 1, 3).reshape(FFN_ITERS, P, SLAB)

    ffn(0, A(w1_gate), A(w1_up), A(w1_down))
    ffn(S_FFN2, A(w2_gate), A(w2_up), A(w2_down))
    w = A(w_in)[0]
    o = np.cumsum([0, 512, 512, 512, 4, 4, 512, 768, 768, 768, D, D])
    qm, km, vm_, ig, fg, og, qa, ka, va, gm, ga = (w[:, o[i]:o[i + 1]] for i in range(11))
    wide = lambda m: tiles(m).transpose(1, 0, 2)
    stream[S_IF].reshape(P, KT, 256)[:, :, 0:8] = wide(np.concatenate([ig, fg], 1))
    vs = np.concatenate([vm_, va], 1)
    for i in range(5):
        stream[S_V + i] = wide(vs[:, 256 * i:256 * i + 256]).reshape(P, SLAB)
    pairs = []
    for i in range(2):
        pairs += [m[:, 256 * i:256 * i + 256] for m in (qm, km, og)]
    for m in (qa, ka):
        m = m.reshape(D, G, H, 2, 32).transpose(0, 1, 3, 2, 4)
        pairs += [m[:, g].reshape(D, 256) for g in range(G)]
    for m in (gm, ga):
        pairs += [m[:, 256 * i:256 * i + 256] for i in range(4)]
    for i, m in enumerate(pairs):
        stream[S_F + i] = tiles(m).reshape(KT, P, 2, P).transpose(1, 2, 0, 3).reshape(P, SLAB)
    up = np.concatenate([tiles(A(w_up_m)[0]), tiles(A(w_up_a)[0])], 0)
    for i in range(3):
        stream[S_UP + i] = up[2 * i:2 * i + 2].transpose(1, 0, 2).reshape(P, SLAB)
    for i in range(4):
        stream[S_OUT + i] = wide(A(w_out)[0][:, 256 * i:256 * i + 256]).reshape(P, SLAB)

    cols = np.zeros((P, C_N), f32)
    cols[:, C_ONES:C_ONES + P] = 1.0
    cols[:, C_ID:C_ID + P] = ident
    for i, g in enumerate((g_ffn1, g_mix, g_ffn2, g_final)):
        cols[:, C_G + 8 * i:C_G + 8 * i + 8] = feat(g, KT)
    cols[:, C_GM:C_GM + 4] = feat(g_mhead, H)
    cols[:, C_EPS], cols[:, C_ONE] = EPS, 1.0
    cols[0:32, C_BI] = np.repeat(A(b_igate)[0], 8)
    cols[0:32, C_BF] = np.repeat(A(b_fgate)[0], 8)
    m_in = np.ascontiguousarray(A(state_mlstm_m)[0].T)
    cols[0:32, C_MS] = m_in.reshape(32)
    state_in = np.concatenate([A(state_mlstm_C)[0].transpose(1, 3, 0, 2),
                               A(state_mlstm_n)[0].transpose(1, 2, 0)[..., None]], 3)
    caches = [A(c)[0] for c in (cache_win128_kv, cache_win512_kv, cache_win2048_kv)]
    caches[2] = caches[2].reshape(NB, 64, 16, 2, H, HD)[:, :, 0:8].reshape(NB, 512, 2, H, HD)
    kv = np.concatenate(caches, 1)
    kc_in = kv[:, :, 0].transpose(0, 3, 2, 1)
    vc_in = np.concatenate([kv[:, :, 1], np.ones((NB, 1152, H, 1), f32)], 3)
    vc_in = vc_in.reshape(NB, 9, P, H * (HD + 1)).transpose(0, 2, 1, 3)

    ins = dict(stream=stream, xT=xT, cols=cols, masks=masks, amasks=am, cos_t=cos_t, sin_t=sin_t,
               state_in=state_in, m_in=m_in, kc_in=kc_in, vc_in=vc_in)
    outs = dict(y_out=(P, KT, TOK), c_out=(H, P, DK + 1), m_out=(H, NBLK + 1), cs_out=(H, P, NB, DK + 1),
                ms_out=(32, 1), kr_out=(G, 2, P, TOK), va_out=(TOK, G, H * (HD + 1)))
    nc = bacc.Bacc("TRN2", target_bir_lowering=False, num_devices=1)
    ins = {k: np.ascontiguousarray(v) for k, v in ins.items()}
    args = [nc.dram_tensor(k, v.shape, F32, kind="ExternalInput").ap() for k, v in ins.items()]
    args += [nc.dram_tensor(k, s, F32, kind="ExternalOutput").ap() for k, s in outs.items()]
    program(nc, *args)
    r = run_bass_kernel_spmd(nc, [ins], core_ids=[0]).results[0]

    y = A(r["y_out"]).transpose(2, 1, 0).reshape(TOK, D)
    C = A(r["c_out"]).transpose(0, 2, 1)
    Cs = A(r["cs_out"]).transpose(2, 0, 3, 1)
    k = A(r["kr_out"]).reshape(G, 2, H, 32, TOK).transpose(4, 0, 2, 1, 3).reshape(TOK, G, H, HD)
    v = A(r["va_out"]).reshape(TOK, G, H, HD + 1)[..., 0:HD]
    kvs = np.stack([k, v], 2)
    wins = (128, 512, SEQ)
    prompt = tuple(kvs[SEQ - n:SEQ, g][None, None] for g, n in enumerate(wins))
    sample = tuple(kvs[SEQ:, g].reshape(1, NB, T, 2, H, HD) for g in range(G))
    return (y[0:SEQ].reshape(1, SEQ, D), y[SEQ:].reshape(NB, T, D),
            C[None, None, :, 0:DK], C[None, None, :, DK], A(r["m_out"])[None, None, :, NBLK], *prompt,
            Cs[None, :, :, 0:DK], Cs[None, :, :, DK], A(r["ms_out"]).reshape(H, NB).T[None], *sample)
```

```python
from contextlib import ExitStack

import numpy as np

import concourse.bass as bass
from concourse import mybir

F32 = mybir.dt.float32
F32R = mybir.dt.float32r
BF16 = mybir.dt.bfloat16
ALU = mybir.AluOpType
ACT = mybir.ActivationFunctionType
AX = mybir.AxisListType

P = 128
D = 1024
KT = D // P
SEQ, NB, T = 1024, 8, 8
SAMP = NB * T
TOK = SEQ + SAMP
F = 2816
FFN_ITERS = F // (2 * P)
CHUNKS = ((0, 384), (384, 384), (768, TOK - 768))
NC = len(CHUNKS)
H = 4
DK = 128
HD = 64
G = 3
NBLK = SEQ // P
EPS = 1e-6
NEG = -1e30

SLAB = 2048
S_IF = 3 * FFN_ITERS
S_V = S_IF + 1
S_F = S_V + 5
S_UP = S_F + 20
S_OUT = S_UP + 3
S_FFN2 = S_OUT + 4
SLABS = S_FFN2 + 3 * FFN_ITERS
PU_F = 6 * FFN_ITERS
PU_UP = PU_F + 20 * NC
PU_FFN2 = PU_UP + KT * NC
AU_IF = 24 * FFN_ITERS
AU_V = AU_IF + NC
AU_OUT = AU_V + 5 * 9
AU_FFN2 = AU_OUT + KT * NC
AU_END = AU_FFN2 + 24 * FFN_ITERS

C_ONES, C_ID, C_G, C_GM, C_EPS, C_ONE, C_BI, C_BF, C_MS, C_N = 0, 128, 256, 288, 292, 293, 294, 295, 296, 297
M_CAUSAL, M_SAMPLE, M_BLOCK, M_N = 0, 128, 192, 200
A_BAND, A_PAIR, A_ID, A_SAMP, A_N = 0, 256, 384, 512, 512 + 1176
SROW = H * T
KEYS_S = 128 + 512 + 512 + 24
SC_WIDTH = (152, 512, 512)
SC_KEY = (0, 152, 664)


def attention_units():
    out = []
    for g, blocks in ((0, NBLK), (1, NBLK), (2, NBLK)):
        for blk in range(blocks):
            first = (blk == 0, blk % 2 == 0, True)[g]
            out += [(g, blk, 0, 4, 1)] if first else [(g, blk, 0, 2, 2), (g, blk, 2, 2, 2)]
    return out


UNITS = attention_units()
NU = len(UNITS)
HEAD_IN = 16 * 6
LATE_IN = 16 * 2
ATT_IN = (16 * 5, 16 * 8, 16 * (5 + 5))


def program(nc, stream, xT, cols, masks, amasks, cos_t, sin_t, state_in, m_in, kc_in, vc_in,
            y_out, c_out, m_out, cs_out, ms_out, kr_out, va_out):
    dram = lambda name, shape: nc.dram_tensor(name, shape, F32).ap()
    zqko = dram("zqko", (12, P, TOK))
    zgate = dram("zgate", (16, P, TOK))
    qr = dram("qr", (G, 2, P, TOK))
    x_kept = dram("x_kept", (P, KT, TOK))
    vm = dram("vm", (TOK, H, DK + 1))
    zif = dram("zif", (8, TOK))
    lastrow = dram("lastrow", (2, 32))
    rows = dram("rows", (3, H, TOK))
    mix = dram("mix", (6, P, TOK))
    o_att = dram("o_att", (SEQ, G, H, HD + 2))

    ctx = ExitStack()
    with ctx:
        at = [16512]

        def place(name, shape, dt=F32, offset=None):
            size = int(np.prod(shape[1:])) * (2 if dt == BF16 else 4)
            size = -(-size // 32) * 32
            o = at[0] if offset is None else offset
            t = nc.alloc_sbuf_tensor_at(name, shape, dt, offset=o)
            if offset is None:
                at[0] += size
            return t

        def overlay(base):
            o = [base]

            def put(name, shape, dt=F32):
                t = place(name, shape, dt, o[0])
                o[0] += -(-int(np.prod(shape[1:])) * (2 if dt == BF16 else 4) // 32) * 32
                assert o[0] <= 229344, (name, o[0])
                return t
            return put

        x = place("x", [P, KT, TOK])
        raw = place("raw", [P, 3, SLAB])
        whi = place("whi", [P, 3, SLAB], F32R)
        wlo = place("wlo", [P, 3, SLAB], F32R)
        con = place("con", [P, C_N])
        idb = place("idb", [P, P], BF16)
        MIX = at[0]
        h_hi = place("h_hi", [P, KT, TOK], F32R)
        h_lo = place("h_lo", [P, KT, TOK], F32R)
        ACTS = at[0]
        act_hi = place("act_hi", [P, 2, TOK], F32R)
        act_lo = place("act_lo", [P, 2, TOK], F32R)
        TEMP = at[0]
        put = overlay(TEMP)
        sq = put("sq", [P, 2, 384])
        htmp = put("htmp", [P, 2, 384])
        rstd = put("rstd", [P, 2, 384])
        put = overlay(TEMP)
        stage = put("stage", [P, 2, 2, 384])
        svm = put("svm", [P, 2, 2, DK + 1])
        sva = put("sva", [P, 2, H, HD + 1])
        at[0] = TEMP + 10496
        silu = place("silu", [P, 2, 384])
        zif_s = place("zif_s", [8, NC, 384], F32, at[0] - 3072)
        assert at[0] <= 229344
        put = overlay(ACTS)
        cost = put("cost", [P, TOK])
        sint = put("sint", [P, TOK])
        W32 = P + T
        zi = put("zi", [32, W32])
        zf = put("zf", [32, W32])
        gna = put("gna", [32, W32])
        gmn = put("gmn", [32, W32])
        ge = put("ge", [32, W32])
        gl = put("gl", [32, W32])
        scan_b = put("scan_b", [32, 2, 204])
        scan_g = put("scan_g", [32, 2, 204])
        lrow = put("lrow", [1, 2, 32])
        mrow = put("mrow", [1, H, NBLK + 1])
        mtmp = put("mtmp", [1, NBLK, H])
        mcol = put("mcol", [32, 1])
        put = overlay(MIX)
        qT = put("qT", [P, 2, TOK])
        kT = put("kT", [P, 2, TOK])
        oT = put("oT", [P, 2, TOK])
        nM = put("nM", [P, 2, TOK])
        nm = put("nm", [P, 2, TOK])
        v1 = put("v1", [P, 2, 9, DK + 1])
        Wd = put("Wd", [P, 2, TOK])
        qw = put("qw", [P, 2, TOK])
        hn = put("hn", [P, 2, TOK])
        ss = put("ss", [P, TOK])
        Cs = put("Cs", [P, 2, NB, DK + 1])
        Cp = put("Cp", [P, 2, DK + 1])
        kw = put("kw", [P, 2, DK])
        Pm = put("Pm", [P, 2, P])
        vex = put("vex", [SAMP, NB, DK + 1])
        den = put("den", [P, P])
        msk = put("msk", [P, M_N])
        gcol = put("gcol", [P, 9, H])
        mpb = put("mpb", [P, H, 8])
        msb = put("msb", [P, H, NB])
        ecol = put("ecol", [P, 2, 3, 8])
        own = put("own", [SAMP, 2, 8])
        wsc = put("wsc", [SAMP, 2, 2])
        qn = put("qn", [P, SAMP])
        put = overlay(16512)
        aqk = put("aqk", [HD, 2, 2, H, SEQ])
        aq, ak = aqk[:, :, 0], aqk[:, :, 1]
        av = put("av", [P, 2, NBLK, H * (HD + 1)])
        ap_ = put("ap_", [P, 2, 512])
        apt = put("apt", [P, 2, 512])
        ao = put("ao", [P, 2, H, HD + 2])
        amx = put("amx", [P, 4, 4])
        amf = put("amf", [P, A_SAMP])
        amb = put("amb", [P, 384], BF16)
        put = overlay(MIX)
        kc = put("kc", [P, 3, 2, 1152])
        vc = put("vc", [P, 3, 9, H * (HD + 1)])
        sqs = put("sqs", [P, G, 2, SAMP])
        sks = put("sks", [P, G, 2, SAMP])
        vnw = put("vnw", [G * T, NB, H * (HD + 1)])
        sqb = put("sqb", [P, G, 2, NB, SROW])
        spx = put("spx", [SROW, 2, KEYS_S])
        soT = put("soT", [HD, H, NB, T])
        spt = put("spt", [P, 10, SROW])
        smb = put("smb", [SROW, KEYS_S], BF16)
        smx = put("smx", [SROW, 2, 4])
        so = put("so", [SROW, 2, H, HD])
        oc = put("oc", [P, 2, G, H, HD + 2])
        ocw = put("ocw", [P, 2, G, H])
        ocm = put("ocm", [P, 2, H])
        oacc = put("oacc", [P, 2, H, HD + 1])
        yat = put("yat", [P, 2, H * HD])
        yT = put("yT", [P, 2, 2, P])
        put = overlay(ACTS)
        mx_hi = put("mx_hi", [P, 6, 384], F32R)
        mx_lo = put("mx_lo", [P, 6, 384], F32R)
        mxin = put("mxin", [P, 2, 384])
        sgate = put("sgate", [P, 2, 2, 384])
        mgt = put("mgt", [P, 384])
        ps = nc.alloc_psum_tensor("ps", [P, 8, 512], F32)
        bank = lambda b, w: ps[:, b, 0:w]
        sem = lambda name: ctx.enter_context(nc.semaphore(name))
        acc_free = sem("acc_free")
        acc_full = sem("acc_full")
        acthi_done = sem("acthi_done")
        amb_ready = sem("amb_ready")
        arg_ready = sem("arg_ready")
        as_full = sem("as_full")
        att_const = sem("att_const")
        att_in = [sem(f"att_in{i}") for i in range(2)]
        blk_ready = sem("blk_ready")
        c_in = [sem(f"c_in{i}") for i in range(2)]
        c_out_ = [sem(f"c_out_{i}") for i in range(2)]
        con_in = sem("con_in")
        cp_out = sem("cp_out")
        cp_ready = sem("cp_ready")
        cs_outd = sem("cs_outd")
        cs_ready = sem("cs_ready")
        cu_full = sem("cu_full")
        dve_step = sem("dve_step")
        exp_ready = sem("exp_ready")
        gM_ready = sem("gM_ready")
        gate_full = sem("gate_full")
        gates_in = sem("gates_in")
        ge_ready = sem("ge_ready")
        gl_ready = sem("gl_ready")
        gna_ready = sem("gna_ready")
        grow_io = sem("grow_io")
        grows_out = sem("grows_out")
        h_ready = sem("h_ready")
        head_done = sem("head_done")
        head_in = [sem(f"head_in{i}") for i in range(2)]
        late_in = [sem(f"late_in{i}") for i in range(2)]
        x_saved = sem("x_saved")
        x_back = sem("x_back")
        hhi_ready = sem("hhi_ready")
        hi_split = sem("hi_split")
        hm_out = sem("hm_out")
        hn_ready = sem("hn_ready")
        ht_ready = sem("ht_ready")
        idb_ready = sem("idb_ready")
        if_staged = sem("if_staged")
        if_stored = sem("if_stored")
        kw_ready = sem("kw_ready")
        mg_hid = sem("mg_hid")
        mg_ready = sem("mg_ready")
        mix_const = sem("mix_const")
        mrow_ready = sem("mrow_ready")
        ms_stored = sem("ms_stored")
        mul_done = sem("mul_done")
        mx_full = sem("mx_full")
        mx_hid = sem("mx_hid")
        mx_in = [sem(f"mx_in{i}") for i in range(2)]
        mx_ready = sem("mx_ready")
        nd_full = sem("nd_full")
        o_ready = sem("o_ready")
        o_stored = [sem(f"o_stored{i}") for i in range(2)]
        oc_read = sem("oc_read")
        oce_ready = sem("oce_ready")
        ocw_ready = sem("ocw_ready")
        ov_full = sem("ov_full")
        p_ready = sem("p_ready")
        pair_free = sem("pair_free")
        pm_ready = sem("pm_ready")
        pt_full = sem("pt_full")
        pt_ready = sem("pt_ready")
        qw_ready = sem("qw_ready")
        raw_in = [sem(f"raw_in{i}") for i in range(3)]
        rope_ready = sem("rope_ready")
        rs_read = sem("rs_read")
        rs_ready = sem("rs_ready")
        rstd_ready = sem("rstd_ready")
        s_const = sem("s_const")
        s_in = [sem(f"s_in{i}") for i in range(3)]
        s_out = sem("s_out")
        samp_ready = sem("samp_ready")
        sg_in = [sem(f"sg_in{i}") for i in range(2)]
        sg_read = sem("sg_read")
        silu_done = sem("silu_done")
        slab_free = sem("slab_free")
        slab_ready = sem("slab_ready")
        smx_ready = sem("smx_ready")
        soT_ready = sem("soT_ready")
        so_ready = sem("so_ready")
        sot_full = sem("sot_full")
        sp_ready = sem("sp_ready")
        spt_ready = sem("spt_ready")
        sq_free = sem("sq_free")
        sq_ready = sem("sq_ready")
        sqh_ready = sem("sqh_ready")
        sqb_ready = sem("sqb_ready")
        ss2_full = sem("ss2_full")
        ss_full = sem("ss_full")
        st_full = sem("st_full")
        std_ready = sem("std_ready")
        stored = [sem(f"stored{i}") for i in range(2)]
        su_full = sem("su_full")
        sv_full = sem("sv_full")
        tab_in = sem("tab_in")
        ts_full = sem("ts_full")
        up_full = sem("up_full")
        v_staged = sem("v_staged")
        v_stored = [sem(f"v_stored{i}") for i in range(2)]
        x_in = [sem(f"x_in{i}") for i in range(3)]
        yT_ready = sem("yT_ready")
        y_ready = sem("y_ready")
        y_stored = [sem(f"y_stored{i}") for i in range(2)]
        ya_ready = sem("ya_ready")
        yt_full = sem("yt_full")
        block = ctx.enter_context(nc.Block())
        def ch(t, c):
            a, w = CHUNKS[c]
            return t[..., a:a + w]

        @block.sync
        def _(sp):
            def slab(s, j):
                sp.dma_start(raw[:, j, :], stream[s]).then_inc(raw_in[j], 16)

            def slab_behind(s, j):
                sp.wait_ge(slab_ready, s - 2)
                slab(s, j)

            sp.dma_start(con[:], cols).then_inc(con_in, 16)
            sp.dma_start(ch(x[:, :, :], 0), ch(xT, 0)).then_inc(x_in[0], 16)
            slab(0, 0)
            sp.dma_start(ch(x[:, :, :], 1), ch(xT, 1)).then_inc(x_in[1], 16)
            sp.dma_start(ch(x[:, :, :], 2), ch(xT, 2)).then_inc(x_in[2], 16)
            slab(1, 1)
            slab(2, 2)
            LOOPED = S_UP // 3
            with sp.Fori(1, LOOPED) as i:
                for j in range(3):
                    slab_behind(3 * i + j, j)
            for s in range(3 * LOOPED, S_UP):
                slab_behind(s, s % 3)

            def load_keys(g):
                s = g % 2
                for half in range(2):
                    for dst, src in ((aq, qr), (ak, kr_out)):
                        sp.dma_start(dst[32 * half:32 * half + 32, s],
                                     src[g, half, :, 0:SEQ].rearrange("(h p) t -> p h t", h=H)).then_inc(att_in[s], 16)

            sp.wait_ge(x_saved, 16)
            sp.wait_ge(h_ready, 48)
            sp.wait_ge(stored[0], 16 * 18)
            sp.wait_ge(stored[1], 16 * 18)
            load_keys(0)

            sp.wait_ge(up_full, PU_UP)
            sp.wait_ge(stored[0], 16 * 30)
            sp.wait_ge(stored[1], 16 * 30)
            sp.wait_ge(v_stored[0], 16 * 23)
            sp.wait_ge(v_stored[1], 16 * 22)
            sp.wait_ge(grows_out, 16 * (1 + 24))
            sp.dma_start(msk[:], masks).then_inc(mix_const, 16)
            for h in range(H):
                sp.dma_start(gcol[:, 0:8, h], rows[2, h, 0:SEQ].rearrange("(n p) -> p n", p=P),
                             allow_slow_non_contiguous=True).then_inc(mix_const, 16)
            sp.dma_start(gcol[0:SAMP, 8, :], rows[2, :, SEQ:TOK].rearrange("h p -> p h"), allow_slow_non_contiguous=True).then_inc(mix_const, 16)
            sp.dma_start(mpb[:], m_out[:, 0:8].unsqueeze(0).to_broadcast([P, H, 8])).then_inc(mix_const, 16)
            sp.dma_start(msb[:], m_in.unsqueeze(0).to_broadcast([P, H, NB])).then_inc(mix_const, 16)

            def load_head(h):
                s = h % 2
                for dst, src in ((nM[:, s], rows[0, h].unsqueeze(0).to_broadcast([P, TOK])),
                                 (kT[:, s], zqko[4 + h]), (qT[:, s], zqko[h]),
                                 (nm[:, s], rows[1, h].unsqueeze(0).to_broadcast([P, TOK])),
                                 (v1[:, s, 0:8], vm[0:SEQ, h].rearrange("(n p) e -> p n e", p=P)),
                                 (v1[0:SAMP, s, 8], vm[SEQ:TOK, h])):
                    sp.dma_start(dst, src).then_inc(head_in[s], 16)

            def load_late(h):
                s = h % 2
                for dst, src in ((Cs[:, s], state_in[h]), (oT[:, s], zqko[8 + h])):
                    sp.dma_start(dst, src).then_inc(late_in[s], 16)

            def load_values(g):
                s = g % 2
                if g == 0:
                    sp.dma_start(av[:, s], va_out[0:SEQ, g].rearrange("(n p) e -> p n e", p=P)).then_inc(att_in[s], 16)
                elif g == 1:
                    v = va_out[0:SEQ, g].rearrange("(q p r) e -> r p q e", p=P, r=4)
                    for r in range(4):
                        sp.dma_start(av[:, s, 2 * r:2 * r + 2], v[r]).then_inc(att_in[s], 16)
                else:
                    sp.dma_start(av[:, s], va_out[0:SEQ, g].rearrange("(i u) e -> i u e", u=8)).then_inc(att_in[s], 16)

            load_head(0)
            sp.dma_start(amf[:], amasks[:, 0:A_SAMP]).then_inc(att_const, 16)
            load_values(0)
            load_late(0)
            load_keys(1)
            load_values(1)
            load_head(1)
            load_late(1)
            last_of = [max(u for u, x_ in enumerate(UNITS) if x_[0] == g) for g in range(G)]

            def store_outputs(u):
                g, blk, h0, nh, nk = UNITS[u]
                sp.wait_ge(o_ready, u + 1)
                o = o_att[:, g, h0:h0 + nh, :]
                src = ao[:, u % 2, 0:nh]
                if g == 0:
                    sp.dma_start(o[blk * P:(blk + 1) * P], src).then_inc(o_stored[u % 2], 16)
                elif g == 1:
                    r, qb = blk // 2, blk % 2
                    o = o.rearrange("(q p r) h e -> r q p h e", p=P, r=4)
                    sp.dma_start(o[r, qb], src).then_inc(o_stored[u % 2], 16)
                else:
                    sp.dma_start(o.rearrange("(i u) h e -> u i h e", u=8)[blk], src).then_inc(o_stored[u % 2], 16)
                if u == last_of[0]:
                    load_keys(2)
                    load_values(2)

            for w in range(9 * H):
                h, c = divmod(w, 9)
                if h > 0 and c == 0:
                    sp.wait_ge(cp_ready, 8 * h)
                    sp.dma_start(c_out[h - 1], Cp[:, 0]).then_inc(cp_out, 16)
                    sp.wait_ge(hn_ready, 9 * h)
                    sp.wait_ge(cs_ready, 8 * h)
                    sp.dma_start(cs_out[h - 1], Cs[:, (h - 1) % 2]).then_inc(cs_outd, 16)
                    if h + 1 < H and h > 0:
                        load_head(h + 1)
                if w < NU:
                    store_outputs(w)
                if h > 0 and c == 6:
                    sp.wait_ge(head_done, h)
                    sp.dma_start(mix[h - 1], ss[:]).then_inc(hm_out, 16)
                    if h + 1 < H:
                        sp.wait_ge(cs_outd, 16 * h)
                        load_late(h + 1)
            sp.wait_ge(cp_ready, 8 * H)
            sp.dma_start(c_out[H - 1], Cp[:, 0]).then_inc(cp_out, 16)
            sp.wait_ge(cs_ready, 8 * H)
            sp.dma_start(cs_out[H - 1], Cs[:, (H - 1) % 2]).then_inc(cs_outd, 16)
            sp.wait_ge(head_done, H)
            sp.dma_start(mix[H - 1], ss[:]).then_inc(hm_out, 16)
            sp.wait_ge(hm_out, 16 * H)
            sp.wait_ge(cs_outd, 16 * H)
            sp.wait_ge(cp_out, 16 * H)

            sp.dma_start(spx[:, 1, :], amasks[0:SROW, A_SAMP:A_N]).then_inc(s_const, 16)
            for half in range(2):
                for r in range(2):
                    for dst, src in ((sqs, qr), (sks, kr_out)):
                        for g in range(G):
                            sp.dma_start(dst[64 * r + 32 * half:64 * r + 32 * half + 32, g],
                                         src[g, half, :, SEQ:TOK].rearrange("(p r d) t -> r d p t", p=2, r=2)[r]).then_inc(s_const, 16)
            for g in range(G):
                sp.dma_start(vnw[T * g:T * g + T], va_out[SEQ:TOK, g].rearrange("(b t) e -> t b e", t=T)).then_inc(s_const, 16)
            for s in range(2):
                sp.wait_ge(o_stored[s], 16 * len(UNITS[s::2]))
            for n in range(NB):
                if n >= 3:
                    sp.wait_ge(ss2_full, n - 2)
                sp.dma_start(kc[:, n % 3], kc_in[n]).then_inc(s_in[n % 3], 16)
                if n >= 3:
                    sp.wait_ge(sv_full, n - 2)
                sp.dma_start(vc[:, n % 3], vc_in[n]).then_inc(s_in[n % 3], 16)
                if n >= 2:
                    sp.wait_ge(oc_read, n - 1)
                sp.dma_start(oc[:, n % 2], o_att[n * P:(n + 1) * P]).then_inc(c_in[n % 2], 16)
                if n >= 2:
                    sp.wait_ge(yT_ready, n - 1)
                    sp.dma_start(mix[4:6, :, (n - 2) * P:(n - 1) * P].rearrange("j p t -> p j t"),
                                 yT[:, n % 2]).then_inc(c_out_[n % 2], 16)
                if n >= 2 and n < 5:
                    slab_behind(S_UP + n - 2, (S_UP + n - 2) % 3)
                if n == 5:
                    sp.dma_start(x[:], x_kept).then_inc(x_back, 16)
                if n >= 5:
                    slab_behind(S_UP + n - 2, (S_UP + n - 2) % 3)
            for n in range(NBLK - 2, NBLK):
                sp.wait_ge(yT_ready, n + 1)
                sp.dma_start(mix[4:6, :, n * P:(n + 1) * P].rearrange("j p t -> p j t"), yT[:, n % 2]).then_inc(c_out_[n % 2], 16)
            sp.wait_ge(soT_ready, NB)
            for h in range(H):
                sp.dma_start(mix[4 + h // 2, 64 * (h % 2):64 * (h % 2) + 64, SEQ:TOK],
                             soT[:, h].rearrange("d b t -> d (b t)")).then_inc(s_out, 16)
            sp.wait_ge(c_out_[0], 16 * 4)
            sp.wait_ge(c_out_[1], 16 * 4)

            sp.wait_ge(s_out, 16 * H)
            for c in range(NC):
                a, w = CHUNKS[c]
                for k in range(6):
                    n = 6 * c + k
                    if n >= 2:
                        sp.wait_ge(mx_ready, n - 1)
                    sp.dma_start(mxin[:, n % 2, 0:w], mix[k, :, a:a + w]).then_inc(mx_in[n % 2], 16)
                for d in range(KT):
                    n = KT * c + d
                    if n >= 2:
                        sp.wait_ge(sg_read, n - 1)
                    sp.dma_start(sgate[:, n % 2, :, 0:w],
                                 zgate.rearrange("(j d) p t -> d p j t", j=2)[d, :, :, a:a + w]).then_inc(sg_in[n % 2], 16)

            for s in range(S_UP + 6, 3 * (-(-(S_UP + 6) // 3))):
                slab_behind(s, s % 3)
            with sp.Fori(-(-(S_UP + 6) // 3), SLABS // 3) as i:
                for j in range(3):
                    slab_behind(3 * i + j, j)

            for c in range(NC):
                a, w = CHUNKS[c]
                for k in range(KT):
                    q = KT * c + k
                    sp.wait_ge(y_ready, q + 1)
                    sp.dma_start(y_out[:, k, a:a + w], htmp[:, q % 2, 0:w]).then_inc(y_stored[q % 2], 16)
            sp.wait_ge(y_stored[0], 16 * 12)
            sp.wait_ge(y_stored[1], 16 * 12)

        @block.gpsimd
        def _(pool):
            pool.wait_ge(con_in, 16)
            with pool.Fori(0, SLABS // 3) as i:
                for j in range(3):
                    pool.wait_ge(raw_in[j], 16 * i + 16)
                    pool.wait_ge(slab_free, 3 * i + j + 1)
                    pool.tensor_tensor(whi[:, j, :], raw[:, j, :], con[:, C_ONES:C_ONES + 1].to_broadcast([P, SLAB]), ALU.mult).then_inc(hi_split, 1)
                    pool.wait_ge(hi_split, 3 * i + j + 1)
                    pool.tensor_tensor(wlo[:, j, :], raw[:, j, :], whi[:, j, :].bitcast(F32),
                                       ALU.subtract).then_inc(slab_ready, 1)

        @block.tensor
        def _(pe):
            ones = con[:, C_ONES:C_ONES + P]
            ident = con[:, C_ID:C_ID + P]

            def products(out, parts, nk):
                for k in range(nk):
                    w_hi, w_lo, x_hi, x_lo = parts(k)
                    pe.matmul(out, w_hi, x_hi, start=(k == 0), stop=False)
                    pe.matmul(out, w_hi, x_lo, start=False, stop=False)
                    last = pe.matmul(out, w_lo, x_hi, start=False, stop=(k == nk - 1))
                return last

            def norm(n, free):
                pe.wait_ge(acc_free, free)
                for c, (a, w) in enumerate(CHUNKS):
                    for k in range(KT):
                        q = 24 * n + 8 * c + k
                        pe.wait_ge(sq_ready, q + 1)
                        mm = pe.matmul(bank(4 + c, w), ones, sq[:, q % 2, 0:w], start=(k == 0), stop=(k == KT - 1))
                        mm.then_inc(sq_free, 1)

            def release(full, count):
                pe.wait_ge(full, count)
                pe.sem_inc(slab_free, 1)

            def pair_unit(j, c, unit, par):
                a, w = CHUNKS[c]
                pe.wait_ge(pair_free, unit + 1)
                for half, full in ((0, gate_full), (1, up_full)):
                    products(bank(2 * par + half, w), lambda k: (
                        whi[:, j, (8 * half + k) * P:(8 * half + k + 1) * P],
                        wlo[:, j, (8 * half + k) * P:(8 * half + k + 1) * P],
                        h_hi[:, k, a:a + w], h_lo[:, k, a:a + w]), KT).then_inc(full, 1)

            def ffn(n):
                s0, pu, au = (0, 0, 0) if n == 0 else (S_FFN2, PU_FFN2, AU_FFN2)
                norm_n = 2 * n
                with pe.Fori(0, FFN_ITERS) as i:
                    for j in range(2):
                        pe.wait_ge(slab_ready, 3 * i + (s0 + j + 1))
                        for c in range(NC):
                            pe.wait_ge(h_ready, 24 * norm_n + 8 * (c + 1))
                            pair_unit(j, c, 6 * i + (pu + 3 * j + c), (3 * j + c) % 2)
                            if c == 0:
                                release(gate_full, 6 * i + (pu + 3 * j + 1))
                    pe.wait_ge(slab_ready, 3 * i + (s0 + 3))
                    for c, (a, w) in enumerate(CHUNKS):
                        pe.wait_ge(pair_free, 6 * i + (pu + 3 + c + 1 + 2))
                        for d in range(KT):
                            v = 8 * c + d
                            pe.wait_ge(acc_free, 24 * i + (au + v + 1))
                            products(bank(4 + v % 4, w), lambda k: (
                                whi[:, 2, k * D + d * P:k * D + (d + 1) * P], wlo[:, 2, k * D + d * P:k * D + (d + 1) * P],
                                act_hi[:, k, a:a + w], act_lo[:, k, a:a + w]), 2).then_inc(acc_full, 1)
                        if c == 0:
                            release(acc_full, 24 * i + (au + 1))

            pe.wait_ge(con_in, 16)
            norm(0, 4)
            ffn(0)
            norm(1, 4 + AU_IF)

            pe.wait_ge(slab_ready, S_IF + 1)
            for c, (a, w) in enumerate(CHUNKS):
                pe.wait_ge(h_ready, 24 + 8 * (c + 1))
                pe.wait_ge(acc_free, AU_IF + c + 1)
                products(bank(4 + c, w), lambda k: (whi[:, 0, k * 256:k * 256 + P], wlo[:, 0, k * 256:k * 256 + P],
                                                    h_hi[:, k, a:a + w], h_lo[:, k, a:a + w]), KT).then_inc(acc_full, 1)
            release(acc_full, AU_IF + 1)
            for s in range(5):
                j = (S_V + s) % 3
                pe.wait_ge(slab_ready, S_V + s + 1)
                for t in range(9):
                    v = AU_V + 9 * s + t
                    a = min(t * P, TOK - P)
                    pe.wait_ge(acc_free, v + 1)
                    products(bank(4 + v % 4, 256), lambda k: (h_hi[:, k, a:a + P], h_lo[:, k, a:a + P],
                                                              whi[:, j, k * 256:(k + 1) * 256],
                                                              wlo[:, j, k * 256:(k + 1) * 256]), KT).then_inc(acc_full, 1)
                    if t == 2:
                        release(acc_full, AU_V + 9 * s + 1)
            with pe.Fori(0, 3) as i:
                for j in range(6):
                    pe.wait_ge(slab_ready, 6 * i + (S_F + j + 1))
                    for c in range(NC):
                        pair_unit(j % 3, c, 18 * i + (PU_F + 3 * j + c), (3 * j + c) % 2)
                        if c == 0:
                            release(gate_full, 18 * i + (PU_F + 3 * j + 1))
            for j in range(2):
                pe.wait_ge(slab_ready, S_F + 18 + j + 1)
                for c in range(NC):
                    pair_unit(j, c, PU_F + 54 + 3 * j + c, (3 * j + c) % 2)
                    if c == 0:
                        release(gate_full, PU_F + 54 + 3 * j + 1)
            release(up_full, PU_UP)

            def where(w):
                h, c = divmod(w, 9)
                return h, c, (SAMP if c == 8 else P), slice(c * P, c * P + (SAMP if c == 8 else P))

            def scores(w):
                h, c, n, tok = where(w)
                s = h % 2
                if c == 0:
                    pe.wait_ge(head_in[s], HEAD_IN * (h // 2 + 1))
                if w == 0:
                    pe.wait_ge(pair_free, PU_UP + 2)
                    pe.wait_ge(acc_free, 4 + AU_OUT)
                else:
                    pe.wait_ge(kw_ready, w)
                    pe.wait_ge(pm_ready, w)
                if h > 0 and 3 <= c <= 5:
                    pe.wait_ge(rs_read, 3 * (h - 1) + c - 2)
                pe.transpose(ps[0:n, 0, 0:P], kT[:, s, tok], ident)
                pe.matmul(ps[0:n, 1, 0:n], kT[:, s, tok], qT[:, s, tok], start=True, stop=True).then_inc(ts_full, 1)

            def outputs(w):
                h, c, n, tok = where(w)
                s = h % 2
                num, dn = ps[:, 2, 0:n], ps[:, 2, P:P + n]
                pe.wait_ge(pm_ready, w + 1)
                if w >= 1:
                    pe.wait_ge(hn_ready, w)
                if c == 0 and h > 0:
                    pe.wait_ge(cs_ready, 8 * h)
                if c == 1:
                    pe.wait_ge(qw_ready, h + 1)
                if 0 < c < 8:
                    pe.wait_ge(cp_ready, 8 * h + c)
                if c == 8:
                    pe.wait_ge(samp_ready, h + 1)
                more = c > 0
                pe.matmul(num, v1[0:n, s, c, 0:DK], Pm[0:n, w % 2, 0:n], start=True, stop=not more)
                if c == 8:
                    for q in range(NB):
                        pe.matmul(num[:, T * q:T * q + T], Cs[:, s, q, 0:DK], qw[:, s, SEQ + T * q:SEQ + T * q + T],
                                  start=False, stop=(q == NB - 1))
                elif more:
                    pe.matmul(num, Cp[:, c % 2, 0:DK], qw[:, s, tok], start=False, stop=True)
                mm = pe.matmul(dn, ones[0:n], Pm[0:n, w % 2, 0:n], start=True, stop=not more)
                if c == 8:
                    mm = pe.matmul(dn, ones, qn[:], start=False, stop=True)
                elif more:
                    mm = pe.matmul(dn, Cp[:, c % 2, DK:DK + 1].to_broadcast([P, P]), qw[:, s, tok], start=False, stop=True)
                mm.then_inc(nd_full, 1)

            def states(w):
                h, c, n, tok = where(w)
                s = h % 2
                pe.wait_ge(kw_ready, w + 1)
                if c < 8:
                    pe.wait_ge(cp_ready, 8 * h + c)
                    if c == 0 and h > 0:
                        pe.wait_ge(cs_ready, 8 * h)
                    pe.matmul(ps[:, 3, 0:DK + 1], kw[:, w % 2, :], v1[:, s, c, :], start=True, stop=True).then_inc(cu_full, 1)
                else:
                    pe.wait_ge(cp_ready, 8 * h + 8)
                    for q in range(NB):
                        if q == 1:
                            pe.wait_ge(hn_ready, w + 1)
                        if q >= 2:
                            pe.wait_ge(cs_ready, 8 * h + q - 1)
                        pe.matmul(ps[:, 3 - q % 2, 0:DK + 1], kw[0:SAMP, w % 2, :], vex[:, q, :],
                                  start=True, stop=True).then_inc(su_full, 1)

            def norm_head(h, c):
                a, w = CHUNKS[c]
                pe.wait_ge(sqh_ready, h + 1)
                pe.wait_ge(kw_ready, min(9 * (h + 1) + c + 3, 9 * H))
                if h == H - 1 and c > 0:
                    pe.wait_ge(rs_read, 3 * h + c)
                pe.matmul(bank(0, w), ones, ss[:, a:a + w], start=True, stop=True).then_inc(ss_full, 1)

            def tokens(t, g, blk, n=1):
                if g == 0:
                    return t[:, blk * P:(blk + n) * P]
                if g == 1:
                    r, q = divmod(blk, 2)
                    return t.rearrange("p (n r) -> p r n", r=4)[:, r, q * P:(q + n) * P]
                return t.rearrange("p (i u) -> p u i", u=8)[:, blk, :]

            def att_scores(u):
                g, blk, h0, nh, nk = UNITS[u]
                s = g % 2
                if u == 0:
                    pe.wait_ge(amb_ready, 1)
                if u == 0 or UNITS[u - 1][0] != g:
                    pe.wait_ge(att_in[s], ATT_IN[g])
                if u >= 2:
                    pe.wait_ge(p_ready, u - 1)
                b = 4 + u % 2
                mask = (amb[:, 256:384] if g == 2 else amb[:, 256 - 128 * nk:256])
                pe.matmul(ps[:, b, :], idb[:], mask.unsqueeze(1).to_broadcast([P, nh, nk * P]), start=True, stop=False)
                for i in range(nh):
                    q = tokens(aq[:, s, h0 + i, :], g, blk)
                    k = tokens(ak[:, s, h0 + i, :], g, blk - (nk - 1), nk)
                    mm = pe.matmul(ps[:, b, i * nk * P:(i + 1) * nk * P], q, k, start=False, stop=(i == nh - 1))
                mm.then_inc(as_full, 1)

            def att_turn(u):
                pe.wait_ge(p_ready, u + 1)
                if u >= 1:
                    pe.wait_ge(pt_ready, u)
                for i in range(4):
                    mm = pe.transpose(ps[:, 6, i * P:(i + 1) * P], ap_[:, u % 2, i * P:(i + 1) * P], ident)
                mm.then_inc(pt_full, 1)

            def att_values(u):
                g, blk, h0, nh, nk = UNITS[u]
                pe.wait_ge(pt_ready, u + 1)
                if u >= 1:
                    pe.wait_ge(o_ready, u)
                for i in range(nh):
                    for k in range(nk):
                        hh = (h0 + i) * (HD + 1)
                        mm = pe.matmul(ps[:, 7, i * (HD + 1):(i + 1) * (HD + 1)],
                                       apt[:, u % 2, (i * nk + k) * P:(i * nk + k + 1) * P],
                                       av[:, g % 2, blk - (nk - 1) + k, hh:hh + HD + 1], start=(k == 0), stop=(k == nk - 1))
                mm.then_inc(ov_full, 1)

            scores(0)
            att_scores(0)
            for w in range(9 * H):
                h, c = divmod(w, 9)
                if w + 1 < 9 * H:
                    scores(w + 1)
                if w + 1 < NU:
                    att_scores(w + 1)
                if w < NU:
                    att_turn(w)
                if c < 8:
                    states(w)
                    outputs(w)
                else:
                    outputs(w)
                    states(w)
                if w < NU:
                    att_values(w)
                if h > 0 and 1 <= c <= 3:
                    norm_head(h - 1, c - 1)
            for c in range(NC):
                norm_head(H - 1, c)

            def s_scores(b):
                if b == 0:
                    pe.wait_ge(sqb_ready, 1)
                    pe.wait_ge(o_ready, NU)
                    pe.wait_ge(rs_read, 3 * H)
                    pe.wait_ge(cs_ready, NB * H)
                else:
                    pe.wait_ge(sp_ready, b)
                pe.wait_ge(s_in[b % 3], 32 * (b // 3 + 1))
                for i, wd in enumerate(SC_WIDTH):
                    pe.matmul(ps[0:SROW, i, 0:wd], idb[0:SROW, 0:SROW], smb[:, SC_KEY[i]:SC_KEY[i] + wd], start=True, stop=False)
                for p in range(2):
                    last = p == 1
                    pe.matmul(ps[0:SROW, 0, 0:128], sqb[:, 0, p, b, :], kc[:, b % 3, p, 0:128], start=False, stop=False)
                    for g in range(G):
                        pe.matmul(ps[0:SROW, 0, 128 + T * g:128 + T * g + T], sqb[:, g, p, b, :],
                                  sks[:, g, p, T * b:T * b + T], start=False, stop=(last and g == G - 1))
                    pe.matmul(ps[0:SROW, 1, :], sqb[:, 1, p, b, :], kc[:, b % 3, p, 128:640], start=False, stop=last)
                    mm = pe.matmul(ps[0:SROW, 2, :], sqb[:, 2, p, b, :], kc[:, b % 3, p, 640:1152], start=False, stop=last)
                mm.then_inc(ss2_full, 1)

            def s_turn(b):
                pe.wait_ge(sp_ready, b + 1)
                if b >= 1:
                    pe.wait_ge(spt_ready, b)
                for i in range(9):
                    a = 0 if i == 0 else 152 + (i - 1) * P
                    pe.transpose(ps[:, 3, i * SROW:(i + 1) * SROW], spx[:, b % 2, a:a + P], ident[0:SROW, 0:SROW])
                pe.transpose(ps[0:G * T, 3, 9 * SROW:10 * SROW], spx[:, b % 2, 128:152], ident[0:SROW, 0:SROW]).then_inc(st_full, 1)

            def s_values(b):
                pe.wait_ge(spt_ready, b + 1)
                if b >= 1:
                    pe.wait_ge(so_ready, b)
                for i in range(9):
                    pe.matmul(ps[0:SROW, 4, 0:H * (HD + 1)], spt[:, i, :], vc[:, b % 3, i, :], start=(i == 0), stop=False)
                pe.matmul(ps[0:SROW, 4, 0:H * (HD + 1)], spt[0:G * T, 9, :], vnw[:, b, :], start=False, stop=True).then_inc(sv_full, 1)

            def s_out_turn(b):
                pe.wait_ge(so_ready, b + 1)
                if b >= 1:
                    pe.wait_ge(soT_ready, b)
                for h in range(H):
                    mm = pe.matmul(ps[0:HD, 5, T * h:T * h + T], so[:, b % 2, h, :], ident[0:SROW, T * h:T * h + T], start=True, stop=True)
                mm.then_inc(sot_full, 1)

            def c_turn(n):
                pe.wait_ge(ya_ready, n + 1)
                if n >= 2:
                    pe.wait_ge(yT_ready, n - 1)
                for i in range(2):
                    mm = pe.transpose(ps[:, 6 + n % 2, i * P:(i + 1) * P], yat[:, n % 2, i * P:(i + 1) * P], ident)
                mm.then_inc(yt_full, 1)

            s_scores(0)
            for b in range(NB):
                if b > 0:
                    s_values(b - 1)
                s_turn(b)
                if b > 0:
                    s_out_turn(b - 1)
                if b + 1 < NB:
                    s_scores(b + 1)
                c_turn(b)
            s_values(NB - 1)
            s_out_turn(NB - 1)

            pe.wait_ge(slab_ready, S_UP + 3)
            pe.wait_ge(soT_ready, NB)
            jm = [(S_UP + i) % 3 for i in range(3)]
            for c, (a, w) in enumerate(CHUNKS):
                pe.wait_ge(mx_ready, 6 * (c + 1))
                for d in range(KT):
                    unit = PU_UP + KT * c + d
                    par = d % 2
                    pe.wait_ge(pair_free, unit + 1)
                    for k0, nk, full, half in ((0, 4, gate_full, 0), (4, 2, up_full, 1)):
                        products(bank(2 * par + half, w), lambda k: (
                            whi[:, jm[(k0 + k) // 2], (k % 2) * D + d * P:(k % 2) * D + (d + 1) * P],
                            wlo[:, jm[(k0 + k) // 2], (k % 2) * D + d * P:(k % 2) * D + (d + 1) * P],
                            mx_hi[:, k0 + k, 0:w], mx_lo[:, k0 + k, 0:w]), nk).then_inc(full, 1)
            pe.wait_ge(up_full, PU_FFN2)
            pe.sem_inc(slab_free, 3)
            for s in range(4):
                j = (S_OUT + s) % 3
                pe.wait_ge(slab_ready, S_OUT + s + 1)
                for c, (a, w) in enumerate(CHUNKS):
                    pe.wait_ge(pair_free, PU_UP + KT * (c + 1) + 2)
                    for dd in range(2):
                        v = AU_OUT + 6 * s + 2 * c + dd
                        pe.wait_ge(acc_free, v + 1)
                        products(bank(4 + v % 4, w), lambda k: (
                            whi[:, j, k * 256 + dd * P:k * 256 + (dd + 1) * P], wlo[:, j, k * 256 + dd * P:k * 256 + (dd + 1) * P],
                            h_hi[:, k, a:a + w], h_lo[:, k, a:a + w]), KT).then_inc(acc_full, 1)
                    if s > 0 and c == 0:
                        release(acc_full, AU_OUT + 6 * s + 1)

            norm(2, 4 + AU_FFN2)
            ffn(1)
            norm(3, 4 + AU_END)

        @block.scalar
        def _(act):
            eps = con[:, C_EPS:C_EPS + 1]

            def norm(n, x_done):
                def squares(c):
                    a, w = CHUNKS[c]
                    x_done(c)
                    for k in range(KT):
                        q = 24 * n + 8 * c + k
                        if q >= 2:
                            act.wait_ge(sq_free, q - 1)
                        act.activation(sq[:, q % 2, 0:w], x[:, k, a:a + w], ACT.Square).then_inc(sq_ready, 1)
                    act.wait_ge(sq_free, 24 * n + 8 * (c + 1))
                    if c == 2:
                        act.wait_ge(*((ht_ready, 24 * n + 8) if n < 3 else (y_ready, 8)))
                    act.activation(rstd[:, c % 2, 0:w], bank(4 + c, w), ACT.Sqrt, bias=eps, scale=1.0 / D).then_inc(std_ready, 1)

                def highs(c):
                    a, w = CHUNKS[c]
                    for k in range(KT):
                        q = 24 * n + 8 * c + k
                        act.wait_ge(ht_ready, q + 1)
                        act.activation(h_hi[:, k, a:a + w], htmp[:, q % 2, 0:w], ACT.Copy).then_inc(hhi_ready, 1)

                squares(0)
                squares(1)
                if n < 3:
                    highs(0)
                squares(2)
                if n < 3:
                    highs(1)
                    highs(2)

            def ffn(n):
                pu, fu = (0, 0) if n == 0 else (PU_FFN2, 6 * FFN_ITERS)
                with act.Fori(0, FFN_ITERS) as i:
                    for j in range(2):
                        for c, (a, w) in enumerate(CHUNKS):
                            k = 3 * j + c
                            par = k % 2
                            act.wait_ge(gate_full, 6 * i + (pu + k + 1))
                            act.activation(silu[:, par, 0:w], bank(2 * par, w), ACT.Silu).then_inc(silu_done, 1)
                            act.wait_ge(mul_done, 6 * i + (fu + k + 1))
                            act.activation(act_hi[:, j, a:a + w], bank(2 * par + 1, w), ACT.Copy).then_inc(acthi_done, 1)

            def x0(c):
                act.wait_ge(x_in[c], 16)
            act.wait_ge(con_in, 16)
            norm(0, x0)
            ffn(0)
            norm(1, lambda c: act.wait_ge(acc_free, 4 + AU_IF - 16 + 8 * c))

            act.wait_ge(acc_free, 4 + AU_IF)
            act.dma_start(x_kept, x[:]).then_inc(x_saved, 16)
            act.dma_start(cost[:], cos_t).then_inc(tab_in, 16)
            act.dma_start(sint[:], sin_t).then_inc(tab_in, 16)
            for c, (a, w) in enumerate(CHUNKS):
                act.wait_ge(if_staged, c + 1)
                act.dma_start(zif[:, a:a + w], zif_s[:, c, 0:w]).then_inc(if_stored, 16)
            act.wait_ge(if_stored, 48)
            for dst, h0 in ((zi, 0), (zf, H)):
                for h in range(H):
                    r = slice(8 * h, 8 * h + 8)
                    act.dma_start(dst[r, 0:P], zif[h0 + h, 0:SEQ].rearrange("(c t) -> c t", t=P)).then_inc(gates_in, 16)
                    act.dma_start(dst[r, P:W32], zif[h0 + h, SEQ:TOK].rearrange("(b t) -> b t", t=T)).then_inc(gates_in, 16)
            for s in range(5):
                for t in range(9):
                    n = 9 * s + t
                    rws, tok = (slice(0, P), slice(t * P, (t + 1) * P)) if t < 8 else (slice(SAMP, P), slice(SEQ, TOK))
                    act.wait_ge(v_staged, n + 1)
                    if s < 2:
                        act.dma_start(vm[tok, 2 * s:2 * s + 2, :], svm[rws, n % 2]).then_inc(v_stored[n % 2], 16)
                    else:
                        act.dma_start(va_out[tok, s - 2, :], sva[rws, n % 2].rearrange("p h e -> p (h e)")).then_inc(v_stored[n % 2], 16)

            def store(u, dst):
                act.dma_start(dst, stage[:, u % 2, :, 0:dst.shape[-1]]).then_inc(stored[u % 2], 16)

            def plain(u, kind, pair, c):
                a, w = CHUNKS[c]
                par = u % 2
                if u >= 2:
                    act.wait_ge(stored[par], 16 * (u // 2))
                for half, full in ((0, gate_full), (1, up_full)):
                    act.wait_ge(full, PU_F + u + 1)
                    ins = act.activation(stage[:, par, half, 0:w], bank(2 * par + half, w),
                                         ACT.Sigmoid if kind == 2 else ACT.Copy, scale=DK ** -0.5 if kind == 1 else 1.0)
                ins.then_inc(pair_free, 1)
                act.wait_ge(pair_free, 2 + PU_F + u + 1)
                store(u, zqko[4 * kind + 2 * pair:4 * kind + 2 * pair + 2, :, a:a + w].rearrange("j p t -> p j t"))

            for j in range(3):
                for c in range(NC):
                    plain(3 * j + c, j, 0, c)

            act.wait_ge(gna_ready, 1)
            act.activation(ge[:], gna[:], ACT.Exp).then_inc(ge_ready, 1)
            act.wait_ge(ge_ready, 1)
            act.activation(gl[:], ge[:], ACT.Ln, bias=con[0:32, C_ONE:C_ONE + 1]).then_inc(gl_ready, 1)
            for j in range(3):
                for c in range(NC):
                    plain(9 + 3 * j + c, j, 1, c)
            act.wait_ge(blk_ready, 1)
            act.dma_start(lastrow[0].unsqueeze(1), scan_b[:, 1, 191:192]).then_inc(grow_io, 16)
            act.dma_start(lastrow[1].unsqueeze(1), scan_g[:, 1, 191:192]).then_inc(grow_io, 16)
            act.wait_ge(grow_io, 32)
            act.dma_start(lrow[:], lastrow.unsqueeze(0)).then_inc(grow_io, 16)
            act.wait_ge(mrow_ready, 1)
            act.dma_start(m_out.unsqueeze(0), mrow[:]).then_inc(grows_out, 16)
            act.wait_ge(grows_out, 16)
            for h in range(H):
                act.dma_start(mcol[8 * h:8 * h + 8, :], m_out[h, 0:8].unsqueeze(1)).then_inc(grow_io, 16)
            act.wait_ge(gM_ready, 1)
            for n, t in enumerate((ge, gl, gna)):
                for h in range(H):
                    r = slice(8 * h, 8 * h + 8)
                    act.dma_start(rows[n, h, 0:SEQ].rearrange("(c t) -> c t", t=P), t[r, 0:P]).then_inc(grows_out, 16)
                    act.dma_start(rows[n, h, SEQ:TOK].rearrange("(b t) -> b t", t=T), t[r, P:W32]).then_inc(grows_out, 16)
            act.dma_start(ms_out, gmn[:, P + T - 1:P + T]).then_inc(ms_stored, 16)

            for j in range(6):
                for c, (a, w) in enumerate(CHUNKS):
                    u = 18 + 3 * j + c
                    act.wait_ge(rope_ready, 3 * j + c + 1)
                    act.sem_inc(pair_free, 1)
                    dst = (qr if j < 3 else kr_out)[j % 3]
                    store(u, dst[:, :, a:a + w].rearrange("s p t -> p s t"))
            with act.Fori(0, 4) as i:
                for j in range(2):
                    for c, (a, w) in enumerate(CHUNKS):
                        k = 3 * j + c
                        par = k % 2
                        act.wait_ge(stored[par], 48 * i + 16 * (18 + k // 2))
                        for half, full in ((0, gate_full), (1, up_full)):
                            act.wait_ge(full, 6 * i + (PU_F + 36 + k + 1))
                            ins = act.activation(stage[:, par, half, 0:w], bank(2 * par + half, w), ACT.Sigmoid)
                        ins.then_inc(pair_free, 1)
                        act.wait_ge(pair_free, 6 * i + (2 + PU_F + 36 + k + 1))
                        act.dma_start(zgate.rearrange("(i j s) p t -> i j p s t", j=2, s=2)[i, j, :, :, a:a + w],
                                      stage[:, par, :, 0:w]).then_inc(stored[par], 16)

            def exps(h):
                s = h % 2
                act.wait_ge(arg_ready, h + 1)
                act.activation(Wd[:, s, 0:SEQ], Wd[:, s, 0:SEQ], ACT.Exp)
                act.activation(Wd[0:SAMP, s, SEQ:TOK], Wd[0:SAMP, s, SEQ:TOK], ACT.Exp)
                act.activation(qw[:, s], qw[:, s], ACT.Exp)
                act.activation(ecol[:, s], ecol[:, s], ACT.Exp)
                act.activation(wsc[:, s, 1:2], wsc[:, s, 1:2], ACT.Exp)
                act.activation(nm[:, s], nm[:, s], ACT.Exp).then_inc(exp_ready, 1)

            def keys(w):
                h, c = divmod(w, 9)
                act.wait_ge(ts_full, w + 1)
                if c == 0:
                    act.wait_ge(exp_ready, h + 1)
                if w >= 2:
                    act.wait_ge(cu_full, 8 * ((w - 2) // 9) + min((w - 2) % 9 + 1, 8))
                    act.wait_ge(su_full, 8 * ((w - 1) // 9))
                if c < 8:
                    act.activation(kw[:, w % 2, :], ps[:, 0, 0:P], ACT.Copy,
                                   scale=ecol[:, h % 2, 2, c:c + 1]).then_inc(kw_ready, 1)
                else:
                    act.activation(kw[0:SAMP, w % 2, :], ps[0:SAMP, 0, 0:P], ACT.Copy).then_inc(kw_ready, 1)

            def head_squares(h):
                act.wait_ge(hn_ready, 9 * (h + 1))
                if h > 0:
                    act.wait_ge(hm_out, 16 * h)
                act.activation(ss[:], hn[:, h % 2], ACT.Square).then_inc(sqh_ready, 1)

            def head_scale(h, c):
                a, w = CHUNKS[c]
                act.wait_ge(ss_full, 3 * h + c + 1)
                act.activation(ss[:, a:a + w], bank(0, w), ACT.Ln, bias=eps, scale=1.0 / DK).then_inc(rs_read, 1)
                if c == 2:
                    act.wait_ge(rs_read, 3 * h + 3)
                    act.activation(ss[:], ss[:], ACT.Exp, scale=-0.5).then_inc(rs_ready, 1)

            def att_exps(u):
                g, blk, h0, nh, nk = UNITS[u]
                act.wait_ge(mx_full, u + 1)
                if u >= 2:
                    act.wait_ge(pt_full, u - 1)
                wd = nk * P
                for i in range(nh):
                    ins = act.activation(ap_[:, u % 2, i * wd:(i + 1) * wd], ps[:, 4 + u % 2, i * wd:(i + 1) * wd], ACT.Exp,
                                         bias=amx[:, u % 4, i:i + 1])
                ins.then_inc(p_ready, 1)

            def att_copy(u):
                act.wait_ge(pt_full, u + 1)
                if u >= 2:
                    act.wait_ge(ov_full, u - 1)
                act.activation(apt[:, u % 2, :], ps[:, 6, :], ACT.Copy).then_inc(pt_ready, 1)

            exps(0)
            keys(0)
            att_exps(0)
            for w in range(9 * H):
                h, c = divmod(w, 9)
                if w + 1 < 9 * H:
                    keys(w + 1)
                if w < NU:
                    att_copy(w)
                if w + 1 < NU:
                    att_exps(w + 1)
                if h > 0 and c == 0:
                    head_squares(h - 1)
                if h > 0 and 1 <= c <= 3:
                    head_scale(h - 1, c - 1)
                if c == 6 and h + 1 < H:
                    exps(h + 1)
            head_squares(H - 1)
            for c in range(NC):
                head_scale(H - 1, c)

            for b in range(NB):
                act.wait_ge(smx_ready, b + 1)
                if b >= 2:
                    act.wait_ge(st_full, b - 1)
                for i, wd in enumerate(SC_WIDTH):
                    ins = act.activation(spx[:, b % 2, SC_KEY[i]:SC_KEY[i] + wd], ps[0:SROW, i, 0:wd], ACT.Exp,
                                         bias=smx[:, b % 2, 3:4])
                ins.then_inc(sp_ready, 1)
                act.wait_ge(ocw_ready, b + 1)
                act.activation(ocw[:, b % 2], ocw[:, b % 2], ACT.Exp).then_inc(oce_ready, 1)

            for c, (a, w) in enumerate(CHUNKS):
                if c > 0:
                    act.wait_ge(up_full, PU_UP + KT * c)
                for k in range(6):
                    n = 6 * c + k
                    act.wait_ge(mx_in[n % 2], 16 * (n // 2 + 1))
                    act.activation(mx_hi[:, k, 0:w], mxin[:, n % 2, 0:w], ACT.Copy).then_inc(mx_hid, 1)
                for d in range(KT):
                    n = KT * c + d
                    act.wait_ge(mg_ready, n + 1)
                    act.activation(h_hi[:, d, a:a + w], bank(2 * (d % 2) + 1, w), ACT.Copy).then_inc(mg_hid, 1)

            norm(2, lambda c: act.wait_ge(acc_free, 4 + AU_OUT + 18 + 2 * (c + 1)))
            ffn(1)
            norm(3, lambda c: act.wait_ge(acc_free, 4 + AU_END - 16 + 8 * c))
            act.wait_ge(ms_stored, 16)

        @block.vector
        def _(dve):
            steps = [0]

            def link(ins):
                steps[0] += 1
                ins.then_inc(dve_step, 1)
                dve.wait_ge(dve_step, steps[0])

            dve.sem_inc(acc_free, 4)
            dve.sem_inc(pair_free, 2)
            dve.sem_inc(slab_free, 2)
            dve.wait_ge(con_in, 16)
            dve.tensor_copy(idb[:], con[:, C_ID:C_ID + P]).then_inc(idb_ready, 1)

            def norm(n, x_done):
                gains = con[:, C_G + 8 * n:C_G + 8 * n + 8]

                def scaled(c, k):
                    a, w = CHUNKS[c]
                    q = 24 * n + 8 * c + k
                    if k == 0:
                        x_done(c)
                        dve.wait_ge(std_ready, 3 * n + c + 1)
                        dve.reciprocal(rstd[:, c % 2, 0:w], rstd[:, c % 2, 0:w]).then_inc(rstd_ready, 1)
                        dve.wait_ge(rstd_ready, 3 * n + c + 1)
                    if n < 3:
                        if q >= 2:
                            dve.wait_ge(h_ready, q - 1)
                    elif q - 72 >= 2:
                        dve.wait_ge(y_stored[q % 2], 16 * ((q - 72) // 2))
                    ins = dve.scalar_tensor_tensor(htmp[:, q % 2, 0:w], x[:, k, a:a + w], gains[:, k:k + 1],
                                                   rstd[:, c % 2, 0:w], ALU.mult, ALU.mult)
                    ins.then_inc(ht_ready if n < 3 else y_ready, 1)

                def low(c, k):
                    a, w = CHUNKS[c]
                    q = 24 * n + 8 * c + k
                    dve.wait_ge(hhi_ready, q + 1)
                    dve.tensor_tensor(h_lo[:, k, a:a + w], htmp[:, q % 2, 0:w], h_hi[:, k, a:a + w].bitcast(F32),
                                      ALU.subtract).then_inc(h_ready, 1)

                order = [(c, k) for c in range(NC) for k in range(KT)]
                scaled(*order[0])
                for m, (c, k) in enumerate(order):
                    if m + 1 < len(order):
                        scaled(*order[m + 1])
                    if n < 3:
                        low(c, k)

            def ffn(n):
                pu, fu, au = (0, 0, 0) if n == 0 else (PU_FFN2, 6 * FFN_ITERS, AU_FFN2)
                with dve.Fori(0, FFN_ITERS) as i:
                    for j in range(2):
                        for c, (a, w) in enumerate(CHUNKS):
                            k = 3 * j + c
                            par = k % 2
                            up = bank(2 * par + 1, w)
                            dve.wait_ge(silu_done, 6 * i + (fu + k + 1))
                            dve.wait_ge(up_full, 6 * i + (pu + k + 1))
                            dve.tensor_tensor(up, silu[:, par, 0:w], up, ALU.mult).then_inc(mul_done, 1)
                            dve.wait_ge(acthi_done, 6 * i + (fu + k + 1))
                            dve.tensor_tensor(act_lo[:, j, a:a + w], up, act_hi[:, j, a:a + w].bitcast(F32),
                                              ALU.subtract).then_inc(pair_free, 1)
                    dve.wait_ge(acc_free, 24 * i + (au + 4))
                    for c, (a, w) in enumerate(CHUNKS):
                        for d in range(KT):
                            v = 8 * c + d
                            dve.wait_ge(acc_full, 24 * i + (au + v + 1))
                            dve.scalar_tensor_tensor(x[:, d, a:a + w], bank(4 + v % 4, w), 0.5, x[:, d, a:a + w],
                                                     ALU.mult, ALU.add).then_inc(acc_free, 1)

            norm(0, lambda c: dve.wait_ge(x_in[c], 16))
            ffn(0)
            norm(1, lambda c: dve.wait_ge(acc_free, 4 + AU_IF - 16 + 8 * c))

            for c, (a, w) in enumerate(CHUNKS):
                dve.wait_ge(acc_full, AU_IF + c + 1)
                dve.tensor_copy(zif_s[:, c, 0:w], ps[0:8, 4 + c, 0:w]).then_inc(if_staged, 1)
                dve.wait_ge(if_staged, c + 1)
                dve.sem_inc(acc_free, 1)
            dve.memset(svm[:], 1.0)
            link(dve.memset(sva[:], 1.0))
            for s in range(5):
                for t in range(9):
                    n = 9 * s + t
                    v = AU_V + n
                    r = slice(0, P) if t < 8 else slice(SAMP, P)
                    dve.wait_ge(acc_full, v + 1)
                    if n >= 2:
                        dve.wait_ge(v_stored[n % 2], 16 * (n // 2))
                    if s < 2:
                        dst, nh = svm[r, n % 2, :, 0:DK], 2
                    else:
                        dst, nh = sva[r, n % 2, :, 0:HD], H
                    dve.tensor_copy(dst, ps[r, 4 + v % 4, 0:256].rearrange("p (h e) -> p h e", h=nh)).then_inc(v_staged, 1)
                    dve.wait_ge(v_staged, n + 1)
                    dve.sem_inc(acc_free, 1)

            col = lambda c: con[0:32, c:c + 1]
            dve.wait_ge(gates_in, 16 * 16)
            dve.tensor_scalar(zi[:], zi[:], col(C_BI), None, ALU.add)
            link(dve.tensor_scalar(zf[:], zf[:], col(C_BF), None, ALU.add))
            dve.tensor_scalar(gmn[:], zf[:], 0.0, None, ALU.min)
            dve.scalar_tensor_tensor(gna[:], zf[:], -1.0, zf[:], ALU.mult, ALU.min).then_inc(gna_ready, 1)
            dve.memset(scan_b[:], 0.0)
            link(dve.memset(scan_g[:], -3e38))
            dve.wait_ge(gl_ready, 1)
            parts = ((64, 0, P, 7), (196, P, T, 3))
            for o, a, w, _ in parts:
                last = dve.tensor_tensor(scan_b[:, 0, o:o + w], gmn[:, a:a + w], gl[:, a:a + w], ALU.subtract)
            link(last)

            def scan(buf, op):
                for k in range(7):
                    for o, _, w, n in parts:
                        if k < n:
                            last = dve.tensor_tensor(buf[:, (k + 1) % 2, o:o + w], buf[:, k % 2, o:o + w],
                                                     buf[:, k % 2, o - 2 ** k:o - 2 ** k + w], op)
                    link(last)

            scan(scan_b, ALU.add)
            for o, a, w, _ in parts:
                dve.tensor_tensor(scan_g[:, 0, o:o + w], zi[:, a:a + w], scan_b[:, 1, o:o + w], ALU.subtract)
                last = dve.tensor_tensor(gna[:, a:a + w], zi[:, a:a + w], scan_b[:, 1, o:o + w], ALU.subtract)
            link(last)
            scan(scan_g, ALU.max)
            dve.memset(mrow[:, :, 0:1], 0.0).then_inc(blk_ready, 1)
            dve.wait_ge(blk_ready, 1)
            dve.wait_ge(grow_io, 48)
            lr = lrow[:].rearrange("p a (h c) -> p a h c", h=H)
            for c in range(NBLK):
                link(dve.tensor_tensor(mtmp[:, c, :], mrow[:, :, c], lr[:, 1, :, c], ALU.max))
                ins = dve.tensor_tensor(mrow[:, :, c + 1], mtmp[:, c, :], lr[:, 0, :, c], ALU.add)
                link(ins)
            dve.sem_inc(mrow_ready, 1)
            dve.wait_ge(grow_io, 48 + 64)
            for (o, a, w, _), m in zip(parts, (mcol[:], col(C_MS))):
                link(dve.tensor_scalar(zi[:, a:a + w], scan_g[:, 1, o:o + w], m, None, ALU.max))
                dve.tensor_scalar(ge[:, a:a + w], zi[:, a:a + w], -1.0, None, ALU.mult)
                link(dve.tensor_tensor(gmn[:, a:a + w], zi[:, a:a + w], scan_b[:, 1, o:o + w], ALU.add))
                last = dve.tensor_scalar(gl[:, a:a + w], gmn[:, a:a + w], -1.0, None, ALU.mult)
            last.then_inc(gM_ready, 1)

            dve.wait_ge(tab_in, 32)
            for j in range(6):
                for c, (a, w) in enumerate(CHUNKS):
                    u = 18 + 3 * j + c
                    par = u % 2
                    scale = HD ** -0.5 if j < 3 else 1.0
                    A, B = bank(2 * par, w), bank(2 * par + 1, w)
                    dve.wait_ge(stored[par], 16 * (u // 2))
                    dve.wait_ge(up_full, PU_F + u + 1)
                    o1, o2 = stage[:, par, 0, 0:w], stage[:, par, 1, 0:w]
                    stt = dve.scalar_tensor_tensor
                    link(stt(o1, A, scale, cost[:, a:a + w], ALU.mult, ALU.mult))
                    link(stt(o2, A, scale, sint[:, a:a + w], ALU.mult, ALU.mult))
                    stt(A, B, scale, sint[:, a:a + w], ALU.mult, ALU.mult)
                    link(stt(B, B, scale, cost[:, a:a + w], ALU.mult, ALU.mult))
                    dve.tensor_tensor(o1, o1, A, ALU.subtract)
                    dve.tensor_tensor(o2, o2, B, ALU.add).then_inc(rope_ready, 1)

            def args(h):
                s = h % 2
                dve.wait_ge(head_in[s], HEAD_IN * (h // 2 + 1))
                blocks = lambda t: t[:, 0:SEQ].rearrange("p (c t) -> p c t", t=P)
                samples = lambda t: t[:, SEQ:TOK].rearrange("p (b t) -> p b t", t=T)
                nMp, nMs = blocks(nM[:, s]), samples(nM[:, s])
                for c in range(NBLK):
                    dve.scalar_tensor_tensor(Wd[:, s, c * P:(c + 1) * P], nMp[:, c, :], gcol[:, c, h:h + 1],
                                             msk[:, M_CAUSAL:M_CAUSAL + P], ALU.add, ALU.add)
                dve.scalar_tensor_tensor(Wd[0:SAMP, s, SEQ:TOK], nM[0:SAMP, s, SEQ:TOK], gcol[0:SAMP, 8, h:h + 1],
                                         msk[0:SAMP, M_SAMPLE:M_SAMPLE + SAMP], ALU.add, ALU.add)
                dve.tensor_tensor(blocks(qw[:, s]), nMp, mpb[:, h, :].unsqueeze(2).to_broadcast([P, 8, P]), ALU.add)
                dve.tensor_tensor(samples(qw[:, s]), nMs, msb[:, h, :].unsqueeze(2).to_broadcast([P, 8, T]), ALU.add)
                dve.tensor_tensor(ecol[:, s, 0, :], mpb[:, h, :], nMp[:, :, P - 1], ALU.add)
                dve.tensor_tensor(ecol[:, s, 1, :], msb[:, h, :], nMs[:, :, T - 1], ALU.add)
                dve.tensor_tensor(ecol[:, s, 2, :], gcol[:, 0:8, h], nMp[:, :, P - 1], ALU.add)
                link(dve.tensor_tensor(own[:, s, :], nMs[0:SAMP, :, T - 1], msk[0:SAMP, M_BLOCK:M_BLOCK + NB], ALU.mult))
                link(dve.tensor_reduce(wsc[:, s, 0:1], own[:, s, :], AX.X, ALU.add))
                dve.tensor_tensor(wsc[:, s, 1:2], wsc[:, s, 0:1], gcol[0:SAMP, 8, h:h + 1], ALU.add).then_inc(arg_ready, 1)

            def queries(h):
                s = h % 2
                dve.wait_ge(exp_ready, h + 1)
                dve.tensor_tensor(qw[:, s], qT[:, s], qw[:, s], ALU.mult).then_inc(qw_ready, 1)

            def sample_parts(h):
                s = h % 2
                dve.wait_ge(qw_ready, h + 1)
                dve.wait_ge(late_in[s], LATE_IN * (h // 2 + 1))
                dve.tensor_tensor(qn[:].rearrange("p (b t) -> p b t", t=T),
                                  qw[:, s, SEQ:TOK].rearrange("p (b t) -> p b t", t=T),
                                  Cs[:, s, :, DK:DK + 1].to_broadcast([P, NB, T]), ALU.mult)
                link(dve.tensor_scalar(own[:, s, :], msk[0:SAMP, M_BLOCK:M_BLOCK + NB], wsc[:, s, 1:2], None, ALU.mult))
                for b in range(NB):
                    ins = dve.tensor_scalar(vex[:, b, :], v1[0:SAMP, s, 8, :], own[:, s, b:b + 1], None, ALU.mult)
                ins.then_inc(samp_ready, 1)

            def weights(w):
                h, c = divmod(w, 9)
                n = P if c < 8 else SAMP
                dve.wait_ge(ts_full, w + 1)
                if c == 0:
                    dve.wait_ge(exp_ready, h + 1)
                if w >= 2:
                    dve.wait_ge(nd_full, w - 1)
                dve.tensor_tensor(Pm[0:n, w % 2, 0:n], ps[0:n, 1, 0:n], Wd[0:n, h % 2, c * P:c * P + n],
                                  ALU.mult).then_inc(pm_ready, 1)

            def new_state(w):
                h, c = divmod(w, 9)
                n = 8 * h + c
                dve.wait_ge(cu_full, n + 1)
                if w > 0:
                    dve.wait_ge(nd_full, w)
                if n > 0:
                    dve.wait_ge(cp_ready, n)
                if c == 1 and h > 0:
                    dve.wait_ge(cp_out, 16 * h)
                dst = Cp[:, (c + 1) % 2]
                if c == 0:
                    dve.tensor_copy(dst, ps[:, 3, 0:DK + 1]).then_inc(cp_ready, 1)
                else:
                    dve.scalar_tensor_tensor(dst, Cp[:, c % 2], ecol[:, h % 2, 0, c:c + 1], ps[:, 3, 0:DK + 1],
                                             ALU.mult, ALU.add).then_inc(cp_ready, 1)

            def sample_states(h):
                for b in range(NB):
                    n = 8 * h + b
                    dve.wait_ge(su_full, n + 1)
                    dve.scalar_tensor_tensor(Cs[:, h % 2, b], Cs[:, h % 2, b], ecol[:, h % 2, 1, b:b + 1],
                                             ps[:, 3 - b % 2, 0:DK + 1], ALU.mult, ALU.add).then_inc(cs_ready, 1)

            def hidden(w):
                h, c = divmod(w, 9)
                n = P if c < 8 else SAMP
                b = 2
                tok = slice(c * P, c * P + n)
                dve.wait_ge(nd_full, w + 1)
                if w > 0:
                    dve.wait_ge(hn_ready, w)
                link(dve.scalar_tensor_tensor(den[:, 0:n], ps[:, b, P:P + n], -1.0, nm[:, h % 2, tok], ALU.mult, ALU.max))
                link(dve.tensor_tensor(den[:, 0:n], ps[:, b, P:P + n], den[:, 0:n], ALU.max))
                link(dve.reciprocal(den[:, 0:n], den[:, 0:n]))
                dve.tensor_tensor(hn[:, h % 2, tok], ps[:, b, 0:n], den[:, 0:n], ALU.mult).then_inc(hn_ready, 1)

            def finish(h):
                dve.wait_ge(rs_ready, h + 1)
                link(dve.scalar_tensor_tensor(ss[:], hn[:, h % 2], con[:, C_GM + h:C_GM + h + 1], ss[:], ALU.mult, ALU.mult))
                dve.tensor_tensor(ss[:], ss[:], oT[:, h % 2], ALU.mult).then_inc(head_done, 1)

            def att_max(u):
                nh = UNITS[u][3]
                dve.wait_ge(as_full, u + 1)
                if u >= 4:
                    dve.wait_ge(o_ready, u - 3)
                dve.tensor_reduce(amx[:, u % 4, 0:nh], ps[:, 4 + u % 2, :].rearrange("p (h k) -> p h k", h=nh), AX.X, ALU.max,
                                  negate=True).then_inc(mx_full, 1)

            def att_out(u):
                nh = UNITS[u][3]
                dve.wait_ge(ov_full, u + 1)
                if u >= 2:
                    dve.wait_ge(o_stored[u % 2], 16 * (u // 2))
                dve.tensor_copy(ao[:, u % 2, 0:nh, 0:HD + 1], ps[:, 7, 0:nh * (HD + 1)].rearrange("p (h e) -> p h e", h=nh))
                dve.tensor_copy(ao[:, u % 2, 0:nh, HD + 1], amx[:, u % 4, 0:nh]).then_inc(o_ready, 1)

            dve.wait_ge(mix_const, 16 * 8)
            args(0)
            queries(0)
            dve.wait_ge(att_const, 16)
            dve.wait_ge(idb_ready, 1)
            dve.tensor_copy(amb[:], amf[:, 0:384]).then_inc(amb_ready, 1)
            weights(0)
            att_max(0)
            for w in range(9 * H):
                h, c = divmod(w, 9)
                if w + 1 < 9 * H:
                    weights(w + 1)
                if w + 1 < NU:
                    att_max(w + 1)
                if c < 8:
                    new_state(w)
                hidden(w)
                if c == 7:
                    sample_parts(h)
                if c == 8:
                    sample_states(h)
                    if h + 1 < H:
                        queries(h + 1)
                if w < NU:
                    att_out(w)
                if c == 4 and h > 0:
                    finish(h - 1)
                if c == 5 and h + 1 < H:
                    args(h + 1)
            finish(H - 1)

            dve.wait_ge(s_const, 16 * (1 + 9 * G))
            dve.tensor_copy(smb[:], spx[:, 1, :])
            link(dve.memset(sqb[:], 0.0))
            for r in range(2):
                for p in range(2):
                    h, rw = 2 * p + r, slice(64 * r, 64 * r + 64)
                    ins = dve.tensor_copy(sqb[rw, :, p, :, T * h:T * h + T],
                                          sqs[rw, :, p, :].rearrange("d g (b t) -> d g b t", t=T))
            ins.then_inc(sqb_ready, 1)

            def s_max(b):
                s = b % 2
                dve.wait_ge(ss2_full, b + 1)
                for i, wd in enumerate(SC_WIDTH):
                    last = dve.tensor_reduce(smx[:, s, i:i + 1], ps[0:SROW, i, 0:wd], AX.X, ALU.max)
                link(last)
                dve.tensor_reduce(smx[:, s, 3:4], smx[:, s, 0:3], AX.X, ALU.max, negate=True).then_inc(smx_ready, 1)

            def s_turned(b):
                dve.wait_ge(st_full, b + 1)
                if b > 0:
                    dve.wait_ge(sv_full, b)
                dve.tensor_copy(spt[:, 0:9, :], ps[:, 3, 0:9 * SROW].rearrange("p (i t) -> p i t", t=SROW))
                dve.tensor_copy(spt[0:G * T, 9, :], ps[0:G * T, 3, 9 * SROW:10 * SROW]).then_inc(spt_ready, 1)

            def s_outputs(b):
                dve.wait_ge(sv_full, b + 1)
                link(dve.reciprocal(smx[:, b % 2, 0:1], ps[0:SROW, 4, HD:HD + 1]))
                dve.tensor_scalar(so[:, b % 2], ps[0:SROW, 4, 0:H * (HD + 1)].rearrange("p (h e) -> p h e", h=H)[:, :, 0:HD],
                                  smx[:, b % 2, 0:1], None, ALU.mult).then_inc(so_ready, 1)

            def s_out(b):
                dve.wait_ge(sot_full, b + 1)
                dve.tensor_copy(soT[:, :, b, :], ps[0:HD, 5, 0:SROW].rearrange("p (h t) -> p h t", h=H)).then_inc(soT_ready, 1)

            def group_weights(n):
                s = n % 2
                dve.wait_ge(c_in[s], 16 * (n // 2 + 1))
                if n >= 2:
                    dve.wait_ge(ya_ready, n - 1)
                nmax = oc[:, s, :, :, HD + 1]
                link(dve.tensor_tensor(ocm[:, s], nmax[:, 0], nmax[:, 1], ALU.min))
                link(dve.tensor_tensor(ocm[:, s], ocm[:, s], nmax[:, 2], ALU.min))
                dve.tensor_tensor(ocw[:, s], ocm[:, s].unsqueeze(1).to_broadcast([P, G, H]), nmax,
                                  ALU.subtract).then_inc(ocw_ready, 1)

            def combine(n):
                s = n % 2
                dve.wait_ge(oce_ready, n + 1)
                for g in range(G):
                    last = dve.tensor_tensor(oc[:, s, g, :, 0:HD + 1], oc[:, s, g, :, 0:HD + 1],
                                             ocw[:, s, g, :].unsqueeze(2).to_broadcast([P, H, HD + 1]), ALU.mult)
                link(last)
                link(dve.tensor_tensor(oacc[:, s], oc[:, s, 0, :, 0:HD + 1], oc[:, s, 1, :, 0:HD + 1], ALU.add))
                dve.tensor_tensor(oacc[:, s], oacc[:, s], oc[:, s, 2, :, 0:HD + 1], ALU.add).then_inc(oc_read, 1)
                dve.wait_ge(oc_read, n + 1)
                link(dve.reciprocal(ocm[:, s], oacc[:, s, :, HD]))
                if n >= 2:
                    dve.wait_ge(yt_full, n - 1)
                dve.tensor_tensor(yat[:, s].rearrange("p (h e) -> p h e", h=H), oacc[:, s, :, 0:HD],
                                  ocm[:, s].unsqueeze(2).to_broadcast([P, H, HD]), ALU.mult).then_inc(ya_ready, 1)

            def c_out(n):
                s = n % 2
                dve.wait_ge(yt_full, n + 1)
                if n >= 2:
                    dve.wait_ge(c_out_[s], 16 * (n // 2))
                dve.tensor_copy(yT[:, s].rearrange("p j t -> p (j t)"), ps[:, 6 + s, 0:256]).then_inc(yT_ready, 1)

            group_weights(0)
            s_max(0)
            for b in range(NB):
                if b > 0:
                    s_outputs(b - 1)
                s_turned(b)
                combine(b)
                if b + 1 < NB:
                    group_weights(b + 1)
                    s_max(b + 1)
                if b > 0:
                    s_out(b - 1)
                c_out(b)
            s_outputs(NB - 1)
            s_out(NB - 1)

            for c, (a, w) in enumerate(CHUNKS):
                for k in range(6):
                    n = 6 * c + k
                    dve.wait_ge(mx_hid, n + 1)
                    dve.tensor_tensor(mx_lo[:, k, 0:w], mxin[:, n % 2, 0:w], mx_hi[:, k, 0:w].bitcast(F32),
                                      ALU.subtract).then_inc(mx_ready, 1)
                for d in range(KT):
                    n = KT * c + d
                    A, B = bank(2 * (d % 2), w), bank(2 * (d % 2) + 1, w)
                    dve.wait_ge(sg_in[n % 2], 16 * (n // 2 + 1))
                    dve.wait_ge(gate_full, PU_UP + n + 1)
                    if n > 0:
                        dve.wait_ge(mg_ready, n)
                    dve.tensor_tensor(mgt[:, 0:w], A, sgate[:, n % 2, 0, 0:w], ALU.mult)
                    dve.wait_ge(up_full, PU_UP + n + 1)
                    dve.tensor_tensor(B, B, sgate[:, n % 2, 1, 0:w], ALU.mult).then_inc(sg_read, 1)
                    dve.wait_ge(sg_read, n + 1)
                    dve.tensor_tensor(B, B, mgt[:, 0:w], ALU.add).then_inc(mg_ready, 1)
                    dve.wait_ge(mg_hid, n + 1)
                    dve.tensor_tensor(h_lo[:, d, a:a + w], B, h_hi[:, d, a:a + w].bitcast(F32),
                                      ALU.subtract).then_inc(pair_free, 1)
            dve.wait_ge(x_back, 16)
            for s in range(4):
                for c, (a, w) in enumerate(CHUNKS):
                    for dd in range(2):
                        v = AU_OUT + 6 * s + 2 * c + dd
                        d = 2 * s + dd
                        dve.wait_ge(acc_full, v + 1)
                        dve.tensor_tensor(x[:, d, a:a + w], bank(4 + v % 4, w), x[:, d, a:a + w], ALU.add).then_inc(acc_free, 1)

            norm(2, lambda c: dve.wait_ge(acc_free, 4 + AU_OUT + 18 + 2 * (c + 1)))
            ffn(1)
            norm(3, lambda c: dve.wait_ge(acc_free, 4 + AU_END - 16 + 8 * c))


def constants():
    ident = np.eye(P, dtype=np.float32)
    t = np.arange(P)
    masks = np.zeros((P, M_N), np.float32)
    masks[:, M_CAUSAL:M_CAUSAL + P] = np.where(t[:, None] <= t[None, :], 0.0, NEG)
    a = np.arange(SAMP)
    same = a[:, None] // T == a[None, :] // T
    masks[0:SAMP, M_SAMPLE:M_SAMPLE + SAMP] = np.where(same & (a[:, None] <= a[None, :]), 0.0, NEG)
    masks[0:SAMP, M_BLOCK:M_BLOCK + NB] = a[:, None] // T == np.arange(NB)[None, :]
    am = np.zeros((P, A_N), np.float32)
    k = np.arange(2 * P)
    dist = t[:, None] + P - k[None, :]
    am[:, A_BAND:A_BAND + 2 * P] = np.where((dist >= 0) & (dist <= 128), 0.0, NEG)
    am[:, A_PAIR:A_PAIR + P] = np.where((t[:, None] % 2 == t[None, :] % 2) & (t[None, :] <= t[:, None]), 0.0, NEG)
    q = (t % T)[:, None]
    new = np.arange(T)[None, :]
    g2 = np.arange(512)[None, :]
    ok = np.concatenate([t[None, :] >= q,
                         new <= q, (new <= q) & ((q - new) % 4 == 0), new == q,
                         (g2 >= q) & ((g2 - q) % 4 == 0),
                         g2 % 8 == q], 1)
    am[:, A_SAMP:A_N] = np.where(ok, 0.0, NEG)
    half = HD // 2
    inv = np.float32(10000.0) ** (np.float32(-2.0) * np.arange(half, dtype=np.float32) / np.float32(HD))
    pos = np.concatenate([np.arange(SEQ), np.tile(SEQ + np.arange(T), NB)]).astype(np.float32)
    ang = np.tile((inv[:, None] * pos[None, :]).astype(np.float32), (4, 1)).astype(np.float64)
    return ident, masks, am, np.cos(ang).astype(np.float32), np.sin(ang).astype(np.float32)


def kernel(x_prompt, x_sample, state_mlstm_C, state_mlstm_n, state_mlstm_m,
           cache_win128_kv, cache_win512_kv, cache_win2048_kv,
           g_ffn1, w1_gate, w1_up, w1_down, g_mix, w_in, b_igate, b_fgate, g_mhead,
           w_up_m, w_up_a, w_out, g_ffn2, w2_gate, w2_up, w2_down, g_final):
    import concourse.bacc as bacc
    from concourse.bass_utils import run_bass_kernel_spmd

    A = np.asarray
    f32 = np.float32
    ident, masks, am, cos_t, sin_t = constants()
    feat = lambda a, n: A(a).reshape(n, P).T
    x = np.concatenate([A(x_prompt).reshape(SEQ, D), A(x_sample).reshape(SAMP, D)], 0)
    xT = np.ascontiguousarray(x.T.reshape(KT, P, TOK).transpose(1, 0, 2))

    stream = np.zeros((SLABS, P, SLAB), f32)
    tiles = lambda w: A(w).reshape(w.shape[0] // P, P, w.shape[1])

    def ffn(s0, wg, wu, wd):
        both = np.stack([tiles(wg[0]), tiles(wu[0])], 0).reshape(2, KT, P, FFN_ITERS, 2, P)
        v = stream[s0:s0 + 3 * FFN_ITERS].reshape(FFN_ITERS, 3, P, SLAB)
        v[:, 0:2] = both.transpose(3, 4, 2, 0, 1, 5).reshape(FFN_ITERS, 2, P, SLAB)
        v[:, 2] = tiles(wd[0]).reshape(FFN_ITERS, 2, P, D).transpose(0, 2, 1, 3).reshape(FFN_ITERS, P, SLAB)

    ffn(0, A(w1_gate), A(w1_up), A(w1_down))
    ffn(S_FFN2, A(w2_gate), A(w2_up), A(w2_down))
    w = A(w_in)[0]
    o = np.cumsum([0, 512, 512, 512, 4, 4, 512, 768, 768, 768, D, D])
    qm, km, vm_, ig, fg, og, qa, ka, va, gm, ga = (w[:, o[i]:o[i + 1]] for i in range(11))
    wide = lambda m: tiles(m).transpose(1, 0, 2)
    stream[S_IF].reshape(P, KT, 256)[:, :, 0:8] = wide(np.concatenate([ig, fg], 1))
    vs = np.concatenate([vm_, va], 1)
    for i in range(5):
        stream[S_V + i] = wide(vs[:, 256 * i:256 * i + 256]).reshape(P, SLAB)
    pairs = []
    for i in range(2):
        pairs += [m[:, 256 * i:256 * i + 256] for m in (qm, km, og)]
    for m in (qa, ka):
        m = m.reshape(D, G, H, 2, 32).transpose(0, 1, 3, 2, 4)
        pairs += [m[:, g].reshape(D, 256) for g in range(G)]
    for m in (gm, ga):
        pairs += [m[:, 256 * i:256 * i + 256] for i in range(4)]
    for i, m in enumerate(pairs):
        stream[S_F + i] = tiles(m).reshape(KT, P, 2, P).transpose(1, 2, 0, 3).reshape(P, SLAB)
    up = np.concatenate([tiles(A(w_up_m)[0]), tiles(A(w_up_a)[0])], 0)
    for i in range(3):
        stream[S_UP + i] = up[2 * i:2 * i + 2].transpose(1, 0, 2).reshape(P, SLAB)
    for i in range(4):
        stream[S_OUT + i] = wide(A(w_out)[0][:, 256 * i:256 * i + 256]).reshape(P, SLAB)

    cols = np.zeros((P, C_N), f32)
    cols[:, C_ONES:C_ONES + P] = 1.0
    cols[:, C_ID:C_ID + P] = ident
    for i, g in enumerate((g_ffn1, g_mix, g_ffn2, g_final)):
        cols[:, C_G + 8 * i:C_G + 8 * i + 8] = feat(g, KT)
    cols[:, C_GM:C_GM + 4] = feat(g_mhead, H)
    cols[:, C_EPS], cols[:, C_ONE] = EPS, 1.0
    cols[0:32, C_BI] = np.repeat(A(b_igate)[0], 8)
    cols[0:32, C_BF] = np.repeat(A(b_fgate)[0], 8)
    m_in = np.ascontiguousarray(A(state_mlstm_m)[0].T)
    cols[0:32, C_MS] = m_in.reshape(32)
    state_in = np.concatenate([A(state_mlstm_C)[0].transpose(1, 3, 0, 2),
                               A(state_mlstm_n)[0].transpose(1, 2, 0)[..., None]], 3)
    caches = [A(c)[0] for c in (cache_win128_kv, cache_win512_kv, cache_win2048_kv)]
    caches[2] = caches[2].reshape(NB, 64, 16, 2, H, HD)[:, :, 0:8].reshape(NB, 512, 2, H, HD)
    kv = np.concatenate(caches, 1)
    kc_in = kv[:, :, 0].reshape(NB, 1152, 2, 2, HD).transpose(0, 3, 4, 2, 1).reshape(NB, P, 2, 1152)
    vc_in = np.concatenate([kv[:, :, 1], np.ones((NB, 1152, H, 1), f32)], 3)
    vc_in = vc_in.reshape(NB, 9, P, H * (HD + 1)).transpose(0, 2, 1, 3)

    ins = dict(stream=stream, xT=xT, cols=cols, masks=masks, amasks=am, cos_t=cos_t, sin_t=sin_t,
               state_in=state_in, m_in=m_in, kc_in=kc_in, vc_in=vc_in)
    outs = dict(y_out=(P, KT, TOK), c_out=(H, P, DK + 1), m_out=(H, NBLK + 1), cs_out=(H, P, NB, DK + 1),
                ms_out=(32, 1), kr_out=(G, 2, P, TOK), va_out=(TOK, G, H * (HD + 1)))
    nc = bacc.Bacc("TRN2", target_bir_lowering=False, num_devices=1)
    ins = {k: np.ascontiguousarray(v) for k, v in ins.items()}
    args = [nc.dram_tensor(k, v.shape, F32, kind="ExternalInput").ap() for k, v in ins.items()]
    args += [nc.dram_tensor(k, s, F32, kind="ExternalOutput").ap() for k, s in outs.items()]
    program(nc, *args)
    r = run_bass_kernel_spmd(nc, [ins], core_ids=[0]).results[0]

    y = A(r["y_out"]).transpose(2, 1, 0).reshape(TOK, D)
    C = A(r["c_out"]).transpose(0, 2, 1)
    Cs = A(r["cs_out"]).transpose(2, 0, 3, 1)
    k = A(r["kr_out"]).reshape(G, 2, H, 32, TOK).transpose(4, 0, 2, 1, 3).reshape(TOK, G, H, HD)
    v = A(r["va_out"]).reshape(TOK, G, H, HD + 1)[..., 0:HD]
    kvs = np.stack([k, v], 2)
    wins = (128, 512, SEQ)
    prompt = tuple(kvs[SEQ - n:SEQ, g][None, None] for g, n in enumerate(wins))
    sample = tuple(kvs[SEQ:, g].reshape(1, NB, T, 2, H, HD) for g in range(G))
    return (y[0:SEQ].reshape(1, SEQ, D), y[SEQ:].reshape(NB, T, D),
            C[None, None, :, 0:DK], C[None, None, :, DK], A(r["m_out"])[None, None, :, NBLK], *prompt,
            Cs[None, :, :, 0:DK], Cs[None, :, :, DK], A(r["ms_out"]).reshape(H, NB).T[None], *sample)
```

```python
from contextlib import ExitStack

import numpy as np

import concourse.bass as bass
from concourse import mybir

F32 = mybir.dt.float32
F32R = mybir.dt.float32r
BF16 = mybir.dt.bfloat16
ALU = mybir.AluOpType
ACT = mybir.ActivationFunctionType
AX = mybir.AxisListType

P = 128
D = 1024
KT = D // P
SEQ, NB, T = 1024, 8, 8
SAMP = NB * T
TOK = SEQ + SAMP
F = 2816
FFN_ITERS = F // (2 * P)
CHUNKS = ((0, 384), (384, 384), (768, TOK - 768))
NC = len(CHUNKS)
H = 4
DK = 128
HD = 64
G = 3
NBLK = SEQ // P
EPS = 1e-6
NEG = -1e30

SLAB = 2048
S_IF = 3 * FFN_ITERS
S_V = S_IF + 1
S_F = S_V + 5
S_UP = S_F + 20
S_OUT = S_UP + 3
S_FFN2 = S_OUT + 4
SLABS = S_FFN2 + 3 * FFN_ITERS
PU_F = 6 * FFN_ITERS
PU_UP = PU_F + 20 * NC
PU_FFN2 = PU_UP + KT * NC
AU_IF = 24 * FFN_ITERS
AU_V = AU_IF + NC
AU_OUT = AU_V + 5 * 9
AU_FFN2 = AU_OUT + KT * NC
AU_END = AU_FFN2 + 24 * FFN_ITERS



def v_unit(s, t):
    return AU_IF + 9 * s + t + (NC if s else 0)


def sums_bank(h, c):
    return 0 if h < H - 1 else 4 + c


def if_unit(c):
    return AU_IF + 9 + c


SUM_BANK = (0, 2, 3)
PAIRS_BEFORE = (0, PU_F, PU_FFN2, PU_FFN2 + 6 * FFN_ITERS)

C_ONES, C_ID, C_G, C_GM, C_EPS, C_ONE, C_BI, C_BF, C_MS, C_N = 0, 128, 256, 288, 292, 293, 294, 295, 296, 297
M_CAUSAL, M_SAMPLE, M_BLOCK, M_N = 0, 128, 192, 200
A_BAND, A_PAIR, A_ID, A_SAMP, A_N = 0, 256, 384, 512, 512 + 1176
SROW = H * T
KEYS_S = 128 + 512 + 512 + 24
SC_WIDTH = (152, 512, 512)
SC_KEY = (0, 152, 664)


def attention_units():
    out = []
    for g, blocks in ((0, NBLK), (1, NBLK), (2, NBLK)):
        for blk in range(blocks):
            first = (blk == 0, blk % 2 == 0, True)[g]
            out += [(g, blk, 0, 4, 1)] if first else [(g, blk, 0, 2, 2), (g, blk, 2, 2, 2)]
    return out


UNITS = attention_units()
NU = len(UNITS)
HEAD_IN = 16 * 6
LATE_IN = 16 * 2
S_CONST = 16 * (1 + 9 * G)
ATT_IN = (16 * 4, 16 * 4, 16 * 8)
AV_IN = (16, 16 * 4, 16 * 2)
LEAD = 3


def program(nc, stream, xT, cols, masks, amasks, cos_t, sin_t, state_in, m_in, kc_in, vc_in,
            y_out, c_out, m_out, cs_out, ms_out, kr_out, va_out):
    dram = lambda name, shape: nc.dram_tensor(name, shape, F32).ap()
    zqko = dram("zqko", (12, P, TOK))
    zgate = dram("zgate", (16, P, TOK))
    qr = dram("qr", (G, 2, P, TOK))
    x_kept = dram("x_kept", (P, KT, TOK))
    vm = dram("vm", (TOK, H, DK + 1))
    zif = dram("zif", (8, TOK))
    lastrow = dram("lastrow", (2, 32))
    rows = dram("rows", (3, H, TOK))
    mix = dram("mix", (6, P, TOK))
    o_att = dram("o_att", (SEQ, G, H, HD + 2))

    ctx = ExitStack()
    with ctx:
        at = [16512]

        def place(name, shape, dt=F32, offset=None):
            size = int(np.prod(shape[1:])) * (2 if dt == BF16 else 4)
            size = -(-size // 32) * 32
            o = at[0] if offset is None else offset
            t = nc.alloc_sbuf_tensor_at(name, shape, dt, offset=o)
            if offset is None:
                at[0] += size
            return t

        def overlay(base):
            o = [base]

            def put(name, shape, dt=F32):
                t = place(name, shape, dt, o[0])
                o[0] += -(-int(np.prod(shape[1:])) * (2 if dt == BF16 else 4) // 32) * 32
                assert o[0] <= 229344, (name, o[0])
                return t
            return put

        x = place("x", [P, KT, TOK])
        RAW = at[0]
        raw = place("raw", [P, 3, SLAB])
        whi = place("whi", [P, 3, SLAB], F32R)
        wlo = place("wlo", [P, 3, SLAB], F32R)
        con = place("con", [P, C_N])
        idb = place("idb", [P, P], BF16)
        MIX = at[0]
        h_hi = place("h_hi", [P, KT, TOK], F32R)
        h_lo = place("h_lo", [P, KT, TOK], F32R)
        ACTS = at[0]
        act_hi = place("act_hi", [P, 2, TOK], F32R)
        act_lo = place("act_lo", [P, 2, TOK], F32R)
        TEMP = at[0]
        put = overlay(TEMP)
        sq = put("sq", [P, 2, 384])
        htmp = put("htmp", [P, 2, 384])
        rstd = put("rstd", [P, 2, 384])
        put = overlay(TEMP)
        stage = put("stage", [P, 2, 2, 384])
        svm = put("svm", [P, 2, 2, DK + 1])
        sva = put("sva", [P, 2, H, HD + 1])
        at[0] = TEMP + 10496
        silu = place("silu", [P, 2, 384])
        zif_s = place("zif_s", [8, NC, 384], F32, TEMP)
        assert at[0] <= 229344
        at[0] = TEMP + 10496 + 3072
        msk = place("msk", [P, M_N])
        gcol = place("gcol", [P, 9, H])
        mpb = place("mpb", [P, H, 8])
        msb = place("msb", [P, H, NB])
        amb = place("amb", [P, 384], BF16)
        assert at[0] <= 229344
        put = overlay(ACTS)
        cost = put("cost", [P, TOK])
        sint = put("sint", [P, TOK])
        W32 = P + T
        zi = put("zi", [32, W32])
        zf = put("zf", [32, W32])
        gna = put("gna", [32, W32])
        gmn = put("gmn", [32, W32])
        ge = put("ge", [32, W32])
        gl = put("gl", [32, W32])
        scan_b = put("scan_b", [32, 2, 204])
        scan_g = put("scan_g", [32, 2, 204])
        lrow = put("lrow", [1, 2, 32])
        mrow = put("mrow", [1, H, NBLK + 1])
        mtmp = put("mtmp", [1, NBLK, H])
        mcol = put("mcol", [32, 1])
        amf = put("amf", [P, 384])
        put = overlay(MIX)
        qT, kT, nM, nm, v1, Wd, qw, hn, oT, Cs = ([] for _ in range(10))
        for s in range(2):
            for t, name in ((qT, "qT"), (kT, "kT"), (nM, "nM"), (nm, "nm"), (Wd, "Wd"), (qw, "qw")):
                t.append(put(f"{name}{s}", [P, TOK]))
            v1.append(put(f"v1_{s}", [P, 9, DK + 1]))
            for t, name in ((hn, "hn"), (oT, "oT")):
                t.append(put(f"{name}{s}", [P, TOK]))
            Cs.append(put(f"Cs{s}", [P, NB, DK + 1]))
        ss = put("ss", [P, TOK])
        Cp = put("Cp", [P, 2, DK + 1])
        kw = put("kw", [P, 2, DK])
        Pm = put("Pm", [P, 2, P])
        vex = put("vex", [SAMP, NB, DK + 1])
        den = put("den", [P, P])
        ecol = put("ecol", [P, 2, 3, 8])
        own = put("own", [SAMP, 2, 8])
        wsc = put("wsc", [SAMP, 2, 2])
        qn = put("qn", [P, SAMP])
        put = overlay(16512)
        aqk = put("aqk", [HD, 2, 2, H, SEQ])
        aq, ak = aqk[:, :, 0], aqk[:, :, 1]
        av = put("av", [P, 2, NBLK, H * (HD + 1)])
        ap_ = put("ap_", [P, 2, 512])
        apt = put("apt", [P, 2, 512])
        ao = put("ao", [P, 2, H, HD + 2])
        amx = put("amx", [P, 4, 4])
        put = overlay(MIX)
        kc = [put("kc0", [P, 2, 1152])]
        vc = [put("vc0", [P, 9, H * (HD + 1)])]
        sqs = put("sqs", [P, G, 2, SAMP])
        sks = put("sks", [P, G, 2, SAMP])
        vnw = put("vnw", [G * T, NB, H * (HD + 1)])
        smk = put("smk", [SROW, KEYS_S])
        soT = put("soT", [HD, H, NB, T])
        kc += [put(f"kc{i}", [P, 2, 1152]) for i in (1, 2)]
        vc += [put("vc1", [P, 9, H * (HD + 1)])]
        put = overlay(16512)
        spx = put("spx", [SROW, 2, KEYS_S])
        sqb = put("sqb", [P, G, 2, NB, SROW])
        spt = put("spt", [P, 10, SROW])
        smb = put("smb", [SROW, KEYS_S], BF16)
        smx = put("smx", [SROW, 2, 4])
        so = put("so", [SROW, 2, H, HD])
        oc = put("oc", [P, 2, G, H, HD + 2])
        ocw = put("ocw", [P, 2, G, H])
        ocm = put("ocm", [P, 2, H])
        oacc = put("oacc", [P, 2, H, HD + 1])
        yat = put("yat", [P, 2, H * HD])
        yT = put("yT", [P, 2, 2, P])
        put = overlay(ACTS)
        mx_hi = [put("mx_hi0", [P, 6, 384], F32R)]
        mx_lo = [put("mx_lo0", [P, 6, 384], F32R)]
        mxin = put("mxin", [P, 4, 384])
        sgate = put("sgate", [P, 2, 2, 384])
        mgt = put("mgt", [P, 384])
        put = overlay(RAW - 2 * 6 * 384 * 4)
        mx_hi.append(put("mx_hi1", [P, 6, 384], F32R))
        mx_lo.append(put("mx_lo1", [P, 6, 384], F32R))
        ps = nc.alloc_psum_tensor("ps", [P, 8, 512], F32)
        bank = lambda b, w: ps[:, b, 0:w]

        sem = lambda name: ctx.enter_context(nc.semaphore(name))
        acc_free = sem("acc_free")
        acc_full = sem("acc_full")
        acthi_done = sem("acthi_done")
        amb_ready = sem("amb_ready")
        arg_ready = sem("arg_ready")
        as_full = sem("as_full")
        att_const = sem("att_const")
        att_in = [sem(f"att_in{i}") for i in range(2)]
        blk_ready = sem("blk_ready")
        c_in = [sem(f"c_in{i}") for i in range(2)]
        mix_stored = [sem(f"mix_stored{i}") for i in range(2)]
        con_in = sem("con_in")
        cp_stored = sem("cp_stored")
        cp_ready = sem("cp_ready")
        cs_stored = sem("cs_stored")
        cs_ready = sem("cs_ready")
        cu_full = sem("cu_full")
        dve_step = sem("dve_step")
        exp_ready = sem("exp_ready")
        gM_ready = sem("gM_ready")
        gate_full = sem("gate_full")
        gates_in = sem("gates_in")
        ge_ready = sem("ge_ready")
        gl_ready = sem("gl_ready")
        gna_ready = sem("gna_ready")
        grow_io = sem("grow_io")
        grows_out = sem("grows_out")
        h_ready = sem("h_ready")
        head_done = sem("head_done")
        head_in = [sem(f"head_in{i}") for i in range(2)]
        late_in = [sem(f"late_in{i}") for i in range(2)]
        x_saved = sem("x_saved")
        gt_full = sem("gt_full")
        gcol_ready = sem("gcol_ready")
        wd_ready = sem("wd_ready")
        ln_ready = sem("ln_ready")
        av_in = [sem(f"av_in{i}") for i in range(2)]
        x_back = sem("x_back")
        x_rest_back = sem("x_rest_back")
        hhi_ready = sem("hhi_ready")
        hi_split = sem("hi_split")
        hidden_stored = sem("hidden_stored")
        hn_ready = sem("hn_ready")
        ht_ready = sem("ht_ready")
        idb_ready = sem("idb_ready")
        if_staged = sem("if_staged")
        if_stored = sem("if_stored")
        kw_ready = sem("kw_ready")
        mg_hid = sem("mg_hid")
        mg_ready = sem("mg_ready")
        mix_const = sem("mix_const")
        mrow_ready = sem("mrow_ready")
        ms_stored = sem("ms_stored")
        mul_done = sem("mul_done")
        mx_full = sem("mx_full")
        mx_hid = sem("mx_hid")
        mx_in = [sem(f"mx_in{i}") for i in range(4)]
        mx_ready = sem("mx_ready")
        nd_full = sem("nd_full")
        o_ready = sem("o_ready")
        o_stored = [sem(f"o_stored{i}") for i in range(2)]
        oc_read = sem("oc_read")
        oce_ready = sem("oce_ready")
        ocw_ready = sem("ocw_ready")
        ov_full = sem("ov_full")
        p_ready = sem("p_ready")
        pair_free = sem("pair_free")
        pm_ready = sem("pm_ready")
        pt_full = sem("pt_full")
        pt_ready = sem("pt_ready")
        qw_ready = sem("qw_ready")
        raw_in = [sem(f"raw_in{i}") for i in range(3)]
        rope_ready = sem("rope_ready")
        rs_read = sem("rs_read")
        rs_ready = sem("rs_ready")
        rstd_ready = sem("rstd_ready")
        s_const = sem("s_const")
        s_in = [sem(f"s_in{i}") for i in range(3)]
        sv_in = [sem(f"sv_in{i}") for i in range(2)]
        sample_stored = sem("sample_stored")
        samp_ready = sem("samp_ready")
        sg_in = [sem(f"sg_in{i}") for i in range(2)]
        sg_read = sem("sg_read")
        silu_done = sem("silu_done")
        slab_free = sem("slab_free")
        slab_ready = sem("slab_ready")
        smx_ready = sem("smx_ready")
        soT_ready = sem("soT_ready")
        so_ready = sem("so_ready")
        sot_full = sem("sot_full")
        sp_ready = sem("sp_ready")
        spt_ready = sem("spt_ready")
        sq_free = sem("sq_free")
        sq_ready = sem("sq_ready")
        sqh_ready = sem("sqh_ready")
        sqb_ready = sem("sqb_ready")
        sample_scored = sem("sample_scored")
        ss_full = sem("ss_full")
        st_full = sem("st_full")
        std_ready = sem("std_ready")
        stored = [sem(f"stored{i}") for i in range(2)]
        su_full = sem("su_full")
        sv_full = sem("sv_full")
        tab_in = sem("tab_in")
        ts_full = sem("ts_full")
        up_full = sem("up_full")
        v_staged = sem("v_staged")
        v_stored = [sem(f"v_stored{i}") for i in range(2)]
        x_in = [sem(f"x_in{i}") for i in range(3)]
        yT_ready = sem("yT_ready")
        y_ready = sem("y_ready")
        y_stored = [sem(f"y_stored{i}") for i in range(2)]
        ya_ready = sem("ya_ready")
        yt_full = sem("yt_full")

        block = ctx.enter_context(nc.Block())

        def ch(t, c):
            a, w = CHUNKS[c]
            return t[..., a:a + w]

        @block.sync
        def _(sp):
            def slab(s, j):
                sp.dma_start(raw[:, j, :], stream[s]).then_inc(raw_in[j], 16)

            def slab_behind(s, j):
                sp.wait_ge(slab_ready, s - 2)
                slab(s, j)

            sp.dma_start(con[:], cols).then_inc(con_in, 16)
            sp.dma_start(ch(x[:, :, :], 0), ch(xT, 0)).then_inc(x_in[0], 16)
            slab(0, 0)
            sp.dma_start(ch(x[:, :, :], 1), ch(xT, 1)).then_inc(x_in[1], 16)
            sp.dma_start(ch(x[:, :, :], 2), ch(xT, 2)).then_inc(x_in[2], 16)
            slab(1, 1)
            slab(2, 2)
            LOOPED = S_UP // 3
            with sp.Fori(1, S_F // 3) as i:
                for j in range(3):
                    slab_behind(3 * i + j, j)
            sp.wait_ge(acc_free, 4 + AU_IF)
            for j in range(3):
                slab_behind(S_F + j, j)
                a, w = CHUNKS[j]
                sp.dma_start(x_kept[:, :, a:a + w], x[:, :, a:a + w]).then_inc(x_saved, 16)
            with sp.Fori(S_F // 3 + 1, LOOPED) as i:
                for j in range(3):
                    slab_behind(3 * i + j, j)
            for s in range(3 * LOOPED, S_UP):
                slab_behind(s, s % 3)

            def load_keys(g):
                s = g % 2
                for half in range(2):
                    for dst, src in ((aq, qr), (ak, kr_out)):
                        sp.dma_start(dst[32 * half:32 * half + 32, s],
                                     src[g, half, :, 0:SEQ].rearrange("(h p) t -> p h t", h=H)).then_inc(att_in[s], 16)

            sp.wait_ge(x_saved, 48)
            sp.wait_ge(h_ready, 48)
            sp.wait_ge(stored[0], 16 * 18)
            sp.wait_ge(stored[1], 16 * 18)
            load_keys(0)

            sp.wait_ge(up_full, PU_UP)
            sp.wait_ge(stored[0], 16 * 30)
            sp.wait_ge(stored[1], 16 * 30)
            sp.wait_ge(v_stored[0], 16 * 23)
            sp.wait_ge(v_stored[1], 16 * 22)
            sp.wait_ge(grows_out, 16 * (1 + 24))
            sp.wait_ge(amb_ready, 1)
            sp.dma_start(gcol[0:SAMP, 8, :], rows[2, :, SEQ:TOK].rearrange("h p -> p h"), allow_slow_non_contiguous=True).then_inc(mix_const, 16)

            def load_head(h):
                s = h % 2
                for dst, src in ((nM[s][:], rows[0, h].unsqueeze(0).to_broadcast([P, TOK])),
                                 (kT[s][:], zqko[4 + h]), (qT[s][:], zqko[h]),
                                 (nm[s][:], rows[1, h].unsqueeze(0).to_broadcast([P, TOK])),
                                 (v1[s][:, 0:8], vm[0:SEQ, h].rearrange("(n p) e -> p n e", p=P)),
                                 (v1[s][0:SAMP, 8], vm[SEQ:TOK, h])):
                    sp.dma_start(dst, src).then_inc(head_in[s], 16)

            def load_late(h):
                s = h % 2
                for dst, src in ((Cs[s][:], state_in[h]), (oT[s][:], zqko[8 + h])):
                    sp.dma_start(dst, src).then_inc(late_in[s], 16)

            def load_values(g):
                s = g % 2
                if g == 0:
                    sp.dma_start(av[:, s], va_out[0:SEQ, g].rearrange("(n p) e -> p n e", p=P)).then_inc(av_in[s], 16)
                elif g == 1:
                    v = va_out[0:SEQ, g].rearrange("(q p r) e -> r p q e", p=P, r=4)
                    for r in range(4):
                        sp.dma_start(av[:, s, 2 * r:2 * r + 2], v[r]).then_inc(av_in[s], 16)
                else:
                    sp.dma_start(av[:, s], va_out[0:SEQ, g].rearrange("(i u) e -> i u e", u=8)).then_inc(av_in[s], 16)

            last_of = [max(u for u, x_ in enumerate(UNITS) if x_[0] == g) for g in range(G)]

            def store_outputs(u):
                g, blk, h0, nh, nk = UNITS[u]
                sp.wait_ge(o_ready, u + 1)
                o = o_att[:, g, h0:h0 + nh, :]
                src = ao[:, u % 2, 0:nh]
                if g == 0:
                    sp.dma_start(o[blk * P:(blk + 1) * P], src).then_inc(o_stored[u % 2], 16)
                elif g == 1:
                    r, qb = blk // 2, blk % 2
                    o = o.rearrange("(q p r) h e -> r q p h e", p=P, r=4)
                    sp.dma_start(o[r, qb], src).then_inc(o_stored[u % 2], 16)
                else:
                    sp.dma_start(o.rearrange("(i u) h e -> u i h e", u=8)[blk], src).then_inc(o_stored[u % 2], 16)
                if u == last_of[0]:
                    load_keys(2)
                    load_values(2)

            def load_keys_s(n):
                if n >= 3:
                    sp.wait_ge(sample_scored, n - 2)
                sp.dma_start(kc[n % 3][:], kc_in[n]).then_inc(s_in[n % 3], 16)

            def load_values_s(n):
                if n >= 2:
                    sp.wait_ge(sv_full, n - 1)
                sp.dma_start(vc[n % 2][:], vc_in[n]).then_inc(sv_in[n % 2], 16)

            def load_sample():
                load_keys_s(0)
                for half in range(2):
                    for r in range(2):
                        for dst, src in ((sqs, qr), (sks, kr_out)):
                            for g in range(G):
                                sp.dma_start(dst[64 * r + 32 * half:64 * r + 32 * half + 32, g],
                                             src[g, half, :, SEQ:TOK].rearrange("(p r d) t -> r d p t", p=2, r=2)[r]).then_inc(s_const, 16)
                for g in range(G):
                    sp.dma_start(vnw[T * g:T * g + T], va_out[SEQ:TOK, g].rearrange("(b t) e -> t b e", t=T)).then_inc(s_const, 16)
                load_values_s(0)

            load_head(0)
            load_values(0)
            load_late(0)
            behind = (lambda: load_keys(1), lambda: load_values(1), lambda: load_head(1))
            for u in range(LEAD):
                store_outputs(u)
                behind[u]()
            load_late(1)
            for w in range(9 * H):
                h, c = divmod(w, 9)
                if h > 0 and c == 0:
                    sp.wait_ge(cp_ready, 8 * h)
                    sp.dma_start(c_out[h - 1], Cp[:, 0]).then_inc(cp_stored, 16)
                    sp.wait_ge(hn_ready, 9 * h)
                    sp.wait_ge(cs_ready, 8 * h)
                    sp.dma_start(cs_out[h - 1], Cs[(h - 1) % 2][:]).then_inc(cs_stored, 16)
                    if h + 1 < H:
                        load_head(h + 1)
                    else:
                        load_sample()
                if w + LEAD < NU:
                    store_outputs(w + LEAD)
                if h > 0 and c == 5:
                    sp.wait_ge(head_done, h)
                    sp.dma_start(mix[h - 1], ss[:]).then_inc(hidden_stored, 16)
                    if h + 1 < H:
                        sp.wait_ge(cs_stored, 16 * h)
                        load_late(h + 1)
                    else:
                        sp.wait_ge(cs_stored, 16 * h)
                        sp.dma_start(smk[:], amasks[0:SROW, A_SAMP:A_N]).then_inc(s_const, 16)
            for s in range(2):
                sp.wait_ge(o_stored[s], 16 * len(UNITS[s::2]))
            for n in range(2):
                sp.dma_start(oc[:, n], o_att[n * P:(n + 1) * P]).then_inc(c_in[n], 16)
            sp.wait_ge(cp_ready, 8 * H)
            sp.dma_start(c_out[H - 1], Cp[:, 0]).then_inc(cp_stored, 16)
            sp.wait_ge(cs_ready, 8 * H)
            sp.dma_start(cs_out[H - 1], Cs[(H - 1) % 2][:]).then_inc(cs_stored, 16)
            sp.wait_ge(head_done, H)
            sp.dma_start(mix[H - 1], ss[:]).then_inc(hidden_stored, 16)
            sp.wait_ge(hidden_stored, 16 * H)
            sp.wait_ge(cs_stored, 16 * H)
            sp.wait_ge(cp_stored, 16 * H)

            def load_branch(c, k):
                a, w = CHUNKS[c]
                n = 6 * c + k
                if n >= 4:
                    sp.wait_ge(mx_ready, n - 3)
                sp.dma_start(mxin[:, n % 4, 0:w], mix[k, :, a:a + w]).then_inc(mx_in[n % 4], 16)

            for n in range(NB):
                if n > 0:
                    load_keys_s(n)
                    load_values_s(n)
                if n >= 2:
                    sp.wait_ge(oc_read, n - 1)
                    sp.dma_start(oc[:, n % 2], o_att[n * P:(n + 1) * P]).then_inc(c_in[n % 2], 16)
                if n >= 2:
                    sp.wait_ge(yT_ready, n - 1)
                    sp.dma_start(mix[4:6, :, (n - 2) * P:(n - 1) * P].rearrange("j p t -> p j t"),
                                 yT[:, n % 2]).then_inc(mix_stored[n % 2], 16)
                    slab_behind(S_UP + n - 2, (S_UP + n - 2) % 3)
                if n == 5:
                    sp.wait_ge(mix_stored[0], 16 * 2)
                    sp.wait_ge(mix_stored[1], 16 * 2)
                    for k in range(4):
                        load_branch(0, k)

            load_branch(0, 4)
            load_branch(0, 5)
            for n in range(NBLK - 2, NBLK):
                sp.wait_ge(yT_ready, n + 1)
                sp.dma_start(mix[4:6, :, n * P:(n + 1) * P].rearrange("j p t -> p j t"), yT[:, n % 2]).then_inc(mix_stored[n % 2], 16)
            sp.wait_ge(soT_ready, NB)
            for h in range(H):
                sp.dma_start(mix[4 + h // 2, 64 * (h % 2):64 * (h % 2) + 64, SEQ:TOK],
                             soT[:, h].rearrange("d b t -> d (b t)")).then_inc(sample_stored, 16)
            sp.wait_ge(mix_stored[0], 16 * 4)
            sp.wait_ge(mix_stored[1], 16 * 4)

            sp.wait_ge(sample_stored, 16 * H)
            for c in range(NC):
                a, w = CHUNKS[c]
                for d in range(KT):
                    n = KT * c + d
                    if n >= 2:
                        sp.wait_ge(sg_read, n - 1)
                    sp.dma_start(sgate[:, n % 2, :, 0:w],
                                 zgate.rearrange("(j d) p t -> d p j t", j=2)[d, :, :, a:a + w]).then_inc(sg_in[n % 2], 16)
                    if c + 1 < NC and d >= 2:
                        load_branch(c + 1, d - 2)
                    if n == 2:
                        sp.dma_start(x[:, 0:3], x_kept[:, 0:3]).then_inc(x_back, 16)
                    if n == KT * NC - 1:
                        sp.wait_ge(up_full, PU_UP + KT * 2)
                        sp.dma_start(x[:, 3:KT], x_kept[:, 3:KT]).then_inc(x_rest_back, 16)

            for s in range(S_UP + 6, 3 * (-(-(S_UP + 6) // 3))):
                slab_behind(s, s % 3)
            with sp.Fori(-(-(S_UP + 6) // 3), SLABS // 3) as i:
                for j in range(3):
                    slab_behind(3 * i + j, j)

            for c in range(NC):
                a, w = CHUNKS[c]
                for k in range(KT):
                    q = KT * c + k
                    sp.wait_ge(y_ready, q + 1)
                    sp.dma_start(y_out[:, k, a:a + w], htmp[:, q % 2, 0:w]).then_inc(y_stored[q % 2], 16)
            sp.wait_ge(y_stored[0], 16 * 12)
            sp.wait_ge(y_stored[1], 16 * 12)

        @block.gpsimd
        def _(pool):
            pool.wait_ge(con_in, 16)
            with pool.Fori(0, SLABS // 3) as i:
                for j in range(3):
                    pool.wait_ge(raw_in[j], 16 * i + 16)
                    pool.wait_ge(slab_free, 3 * i + j + 1)
                    pool.tensor_tensor(whi[:, j, :], raw[:, j, :], con[:, C_ONES:C_ONES + 1].to_broadcast([P, SLAB]), ALU.mult).then_inc(hi_split, 1)
                    pool.wait_ge(hi_split, 3 * i + j + 1)
                    pool.tensor_tensor(wlo[:, j, :], raw[:, j, :], whi[:, j, :].bitcast(F32),
                                       ALU.subtract).then_inc(slab_ready, 1)

        @block.tensor
        def _(pe):
            ones = con[:, C_ONES:C_ONES + P]
            ident = con[:, C_ID:C_ID + P]

            def products(out, parts, nk, h_before=None):
                for k in range(nk):
                    if h_before is not None:
                        pe.wait_ge(h_ready, h_before + k + 1)
                    w_hi, w_lo, x_hi, x_lo = parts(k)
                    pe.matmul(out, w_hi, x_hi, start=(k == 0), stop=False)
                    pe.matmul(out, w_hi, x_lo, start=False, stop=False)
                    last = pe.matmul(out, w_lo, x_hi, start=False, stop=(k == nk - 1))
                return last

            def norm_sums(n, c):
                a, w = CHUNKS[c]
                if c == 0:
                    pe.wait_ge(pair_free, PAIRS_BEFORE[n] + 2)
                for k in range(KT):
                    q = 24 * n + 8 * c + k
                    pe.wait_ge(sq_ready, q + 1)
                    pe.matmul(bank(SUM_BANK[c], w), ones, sq[:, q % 2, 0:w], start=(k == 0), stop=(k == KT - 1)).then_inc(sq_free, 1)

            def release(full, count):
                pe.wait_ge(full, count)
                pe.sem_inc(slab_free, 1)

            def pair_unit(j, c, unit, par, h_before=None):
                a, w = CHUNKS[c]
                pe.wait_ge(pair_free, unit + 1)
                for k in range(KT):
                    if h_before is not None:
                        pe.wait_ge(h_ready, h_before + k + 1)
                    for half, full in ((0, gate_full), (1, up_full)):
                        w_hi = whi[:, j, (8 * half + k) * P:(8 * half + k + 1) * P]
                        w_lo = wlo[:, j, (8 * half + k) * P:(8 * half + k + 1) * P]
                        out = bank(2 * par + half, w)
                        pe.matmul(out, w_hi, h_hi[:, k, a:a + w], start=(k == 0), stop=False)
                        pe.matmul(out, w_hi, h_lo[:, k, a:a + w], start=False, stop=False)
                        mm = pe.matmul(out, w_lo, h_hi[:, k, a:a + w], start=False, stop=(k == KT - 1))
                        if k == KT - 1:
                            mm.then_inc(full, 1)

            def ffn(n):
                s0, pu, au = (0, 0, 0) if n == 0 else (S_FFN2, PU_FFN2, AU_FFN2)
                norm_n = 2 * n

                def step(i, last):
                    for j in range(2):
                        pe.wait_ge(slab_ready, 3 * i + (s0 + j + 1))
                        for c in range(NC):
                            if c == 1:
                                pe.wait_ge(std_ready, 3 * norm_n + 3)
                            pair_unit(j, c, 6 * i + (pu + 3 * j + c), (3 * j + c) % 2,
                                      24 * norm_n + 8 * c if j == 0 else None)
                            if c == 1:
                                release(gate_full, 6 * i + (pu + 3 * j + 1))
                    pe.wait_ge(slab_ready, 3 * i + (s0 + 3))
                    for c, (a, w) in enumerate(CHUNKS):
                        pe.wait_ge(pair_free, 6 * i + (pu + 3 + c + 1 + 2))
                        for d in range(KT):
                            v = 8 * c + d
                            pe.wait_ge(acc_free, 24 * i + (au + v + 1))
                            products(bank(4 + v % 4, w), lambda k: (
                                whi[:, 2, k * D + d * P:k * D + (d + 1) * P], wlo[:, 2, k * D + d * P:k * D + (d + 1) * P],
                                act_hi[:, k, a:a + w], act_lo[:, k, a:a + w]), 2).then_inc(acc_full, 1)
                        if c == 0:
                            release(acc_full, 24 * i + (au + 1))
                        elif last:
                            norm_sums(norm_n + 1, c - 1)

                with pe.Fori(0, FFN_ITERS - 1) as i:
                    step(i, False)
                step(FFN_ITERS - 1, True)
                norm_sums(norm_n + 1, 2)

            pe.wait_ge(con_in, 16)
            for c in range(NC):
                norm_sums(0, c)
            ffn(0)

            for s in range(5):
                j = (S_V + s) % 3
                pe.wait_ge(slab_ready, S_V + s + 1)
                for t in range(9):
                    v = v_unit(s, t)
                    a = min(t * P, TOK - P)
                    pe.wait_ge(acc_free, v + 1)
                    products(bank(4 + v % 4, 256), lambda k: (h_hi[:, k, a:a + P], h_lo[:, k, a:a + P],
                                                              whi[:, j, k * 256:(k + 1) * 256],
                                                              wlo[:, j, k * 256:(k + 1) * 256]), KT,
                             24 + 8 * (a // 384) if s == 0 else None).then_inc(acc_full, 1)
                    if t == 2:
                        release(acc_full, v_unit(s, 0) + 1)
                        if s == 1:
                            release(acc_full, v_unit(s, 0) + 1)
                if s == 0:
                    for c, (a, w) in enumerate(CHUNKS):
                        v = if_unit(c)
                        pe.wait_ge(acc_free, v + 1)
                        products(bank(4 + v % 4, w), lambda k: (
                            whi[:, S_IF % 3, k * 256:k * 256 + P], wlo[:, S_IF % 3, k * 256:k * 256 + P],
                            h_hi[:, k, a:a + w], h_lo[:, k, a:a + w]), KT).then_inc(acc_full, 1)
            pe.wait_ge(std_ready, 6)
            with pe.Fori(0, 3) as i:
                for j in range(6):
                    pe.wait_ge(slab_ready, 6 * i + (S_F + j + 1))
                    for c in range(NC):
                        pair_unit(j % 3, c, 18 * i + (PU_F + 3 * j + c), (3 * j + c) % 2)
                        if c == 1:
                            release(gate_full, 18 * i + (PU_F + 3 * j + 1))
            pe.wait_ge(gM_ready, 1)
            pe.transpose(ps[:, 4, 0:32], gna[:, 0:P], ident[0:32, 0:32]).then_inc(gt_full, 1)
            for j in range(2):
                pe.wait_ge(slab_ready, S_F + 18 + j + 1)
                for c in range(NC):
                    pair_unit(j, c, PU_F + 54 + 3 * j + c, (3 * j + c) % 2)
                    if c == 1:
                        release(gate_full, PU_F + 54 + 3 * j + 1)
            release(up_full, PU_UP)

            def where(w):
                h, c = divmod(w, 9)
                return h, c, (SAMP if c == 8 else P), slice(c * P, c * P + (SAMP if c == 8 else P))

            def scores(w):
                h, c, n, tok = where(w)
                s = h % 2
                if c == 0:
                    pe.wait_ge(head_in[s], HEAD_IN * (h // 2 + 1))
                if w == 0:
                    pe.wait_ge(pair_free, PU_UP + 2)
                    pe.wait_ge(acc_free, 4 + AU_OUT)
                else:
                    pe.wait_ge(kw_ready, w)
                    pe.wait_ge(pm_ready, w)
                if h > 0 and 3 <= c <= 5:
                    pe.wait_ge(rs_read, 3 * (h - 1) + c - 2)
                pe.transpose(ps[0:n, 0, 0:P], kT[s][:, tok], ident)
                pe.matmul(ps[0:n, 1, 0:n], kT[s][:, tok], qT[s][:, tok], start=True, stop=True).then_inc(ts_full, 1)

            def outputs(w):
                h, c, n, tok = where(w)
                s = h % 2
                num, dn = ps[:, 2, 0:n], ps[:, 2, P:P + n]
                pe.wait_ge(pm_ready, w + 1)
                if w >= 1:
                    pe.wait_ge(hn_ready, w)
                if c == 0 and h > 0:
                    pe.wait_ge(cs_ready, 8 * h)
                if c == 1:
                    pe.wait_ge(qw_ready, h + 1)
                if 0 < c < 8:
                    pe.wait_ge(cp_ready, 8 * h + c)
                if c == 8:
                    pe.wait_ge(samp_ready, h + 1)
                more = c > 0
                pe.matmul(num, v1[s][0:n, c, 0:DK], Pm[0:n, w % 2, 0:n], start=True, stop=not more)
                if c == 8:
                    for q in range(NB):
                        pe.matmul(num[:, T * q:T * q + T], Cs[s][:, q, 0:DK], qw[s][:, SEQ + T * q:SEQ + T * q + T],
                                  start=False, stop=(q == NB - 1))
                elif more:
                    pe.matmul(num, Cp[:, c % 2, 0:DK], qw[s][:, tok], start=False, stop=True)
                mm = pe.matmul(dn, ones[0:n], Pm[0:n, w % 2, 0:n], start=True, stop=not more)
                if c == 8:
                    mm = pe.matmul(dn, ones, qn[:], start=False, stop=True)
                elif more:
                    mm = pe.matmul(dn, Cp[:, c % 2, DK:DK + 1].to_broadcast([P, P]), qw[s][:, tok], start=False, stop=True)
                mm.then_inc(nd_full, 1)

            def states(w):
                h, c, n, tok = where(w)
                s = h % 2
                pe.wait_ge(kw_ready, w + 1)
                if c < 8:
                    pe.wait_ge(cp_ready, 8 * h + c)
                    if c == 0 and h > 0:
                        pe.wait_ge(cs_ready, 8 * h)
                    pe.matmul(ps[:, 3, 0:DK + 1], kw[:, w % 2, :], v1[s][:, c, :], start=True, stop=True).then_inc(cu_full, 1)
                else:
                    pe.wait_ge(cp_ready, 8 * h + 8)
                    for q in range(NB):
                        if q == 1:
                            pe.wait_ge(hn_ready, w + 1)
                        if q >= 2:
                            pe.wait_ge(cs_ready, 8 * h + q - 1)
                        pe.matmul(ps[:, 3 - q % 2, 0:DK + 1], kw[0:SAMP, w % 2, :], vex[:, q, :],
                                  start=True, stop=True).then_inc(su_full, 1)

            def norm_head(h, c):
                a, w = CHUNKS[c]
                pe.wait_ge(sqh_ready, h + 1)
                if h < H - 1:
                    pe.wait_ge(kw_ready, 9 * (h + 1) + c + 3)
                else:
                    pe.wait_ge(p_ready, NU)
                    pe.wait_ge(pt_ready, NU)
                pe.matmul(bank(sums_bank(h, c), w), ones, ss[:, a:a + w], start=True, stop=True).then_inc(ss_full, 1)

            def tokens(t, g, blk, n=1):
                if g == 0:
                    return t[:, blk * P:(blk + n) * P]
                if g == 1:
                    r, q = divmod(blk, 2)
                    return t.rearrange("p (n r) -> p r n", r=4)[:, r, q * P:(q + n) * P]
                return t.rearrange("p (i u) -> p u i", u=8)[:, blk, :]

            def att_scores(u):
                g, blk, h0, nh, nk = UNITS[u]
                s = g % 2
                if u == 0:
                    pe.wait_ge(amb_ready, 1)
                if u == 0 or UNITS[u - 1][0] != g:
                    pe.wait_ge(att_in[s], ATT_IN[g])
                if u >= 2:
                    pe.wait_ge(p_ready, u - 1)
                b = 4 + u % 2
                mask = (amb[:, 256:384] if g == 2 else amb[:, 256 - 128 * nk:256])
                pe.matmul(ps[:, b, :], idb[:], mask.unsqueeze(1).to_broadcast([P, nh, nk * P]), start=True, stop=False)
                for i in range(nh):
                    q = tokens(aq[:, s, h0 + i, :], g, blk)
                    k = tokens(ak[:, s, h0 + i, :], g, blk - (nk - 1), nk)
                    mm = pe.matmul(ps[:, b, i * nk * P:(i + 1) * nk * P], q, k, start=False, stop=(i == nh - 1))
                mm.then_inc(as_full, 1)

            def att_turn(u):
                pe.wait_ge(p_ready, u + 1)
                if u >= 1:
                    pe.wait_ge(pt_ready, u)
                for i in range(4):
                    mm = pe.transpose(ps[:, 6, i * P:(i + 1) * P], ap_[:, u % 2, i * P:(i + 1) * P], ident)
                mm.then_inc(pt_full, 1)

            def att_values(u):
                g, blk, h0, nh, nk = UNITS[u]
                pe.wait_ge(pt_ready, u + 1)
                if u >= 1:
                    pe.wait_ge(o_ready, u)
                if u == 0 or UNITS[u - 1][0] != g:
                    pe.wait_ge(av_in[g % 2], AV_IN[g])
                for i in range(nh):
                    for k in range(nk):
                        hh = (h0 + i) * (HD + 1)
                        mm = pe.matmul(ps[:, 7, i * (HD + 1):(i + 1) * (HD + 1)],
                                       apt[:, u % 2, (i * nk + k) * P:(i * nk + k + 1) * P],
                                       av[:, g % 2, blk - (nk - 1) + k, hh:hh + HD + 1], start=(k == 0), stop=(k == nk - 1))
                mm.then_inc(ov_full, 1)

            att_scores(0)
            for u in range(LEAD):
                att_scores(u + 1)
                att_turn(u)
                if u == 0:
                    scores(0)
                att_values(u)
            for w in range(9 * H):
                h, c = divmod(w, 9)
                u = w + LEAD
                if w + 1 < 9 * H:
                    scores(w + 1)
                if u + 1 < NU:
                    att_scores(u + 1)
                if u < NU:
                    att_turn(u)
                if c < 8:
                    states(w)
                    outputs(w)
                else:
                    outputs(w)
                    states(w)
                if u < NU:
                    att_values(u)
                if h > 0 and 1 <= c <= 3:
                    norm_head(h - 1, c - 1)
            for c in range(NC):
                norm_head(H - 1, c)

            def s_scores(b):
                if b == 0:
                    pe.wait_ge(sqb_ready, 1)
                    pe.wait_ge(o_ready, NU)
                    pe.wait_ge(kw_ready, 9 * H)
                    pe.wait_ge(cs_ready, NB * H)
                else:
                    pe.wait_ge(sp_ready, b)
                pe.wait_ge(s_const, S_CONST)
                pe.wait_ge(s_in[b % 3], 16 * (b // 3 + 1))
                for i, wd in enumerate(SC_WIDTH):
                    pe.matmul(ps[0:SROW, i, 0:wd], idb[0:SROW, 0:SROW], smb[:, SC_KEY[i]:SC_KEY[i] + wd], start=True, stop=False)
                for p in range(2):
                    last = p == 1
                    pe.matmul(ps[0:SROW, 0, 0:128], sqb[:, 0, p, b, :], kc[b % 3][:, p, 0:128], start=False, stop=False)
                    for g in range(G):
                        pe.matmul(ps[0:SROW, 0, 128 + T * g:128 + T * g + T], sqb[:, g, p, b, :],
                                  sks[:, g, p, T * b:T * b + T], start=False, stop=(last and g == G - 1))
                    pe.matmul(ps[0:SROW, 1, :], sqb[:, 1, p, b, :], kc[b % 3][:, p, 128:640], start=False, stop=last)
                    mm = pe.matmul(ps[0:SROW, 2, :], sqb[:, 2, p, b, :], kc[b % 3][:, p, 640:1152], start=False, stop=last)
                mm.then_inc(sample_scored, 1)

            def s_turn(b):
                pe.wait_ge(sp_ready, b + 1)
                if b >= 1:
                    pe.wait_ge(spt_ready, b)
                for i in range(9):
                    a = 0 if i == 0 else 152 + (i - 1) * P
                    pe.transpose(ps[:, 3, i * SROW:(i + 1) * SROW], spx[:, b % 2, a:a + P], ident[0:SROW, 0:SROW])
                pe.transpose(ps[0:G * T, 3, 9 * SROW:10 * SROW], spx[:, b % 2, 128:152], ident[0:SROW, 0:SROW]).then_inc(st_full, 1)

            def s_values(b):
                if b == 0:
                    pe.wait_ge(rs_read, 3 * H)
                pe.wait_ge(spt_ready, b + 1)
                pe.wait_ge(sv_in[b % 2], 16 * (b // 2 + 1))
                if b >= 1:
                    pe.wait_ge(so_ready, b)
                for i in range(9):
                    pe.matmul(ps[0:SROW, 4, 0:H * (HD + 1)], spt[:, i, :], vc[b % 2][:, i, :], start=(i == 0), stop=False)
                pe.matmul(ps[0:SROW, 4, 0:H * (HD + 1)], spt[0:G * T, 9, :], vnw[:, b, :], start=False, stop=True).then_inc(sv_full, 1)

            def s_out_turn(b):
                pe.wait_ge(so_ready, b + 1)
                if b >= 1:
                    pe.wait_ge(soT_ready, b)
                for h in range(H):
                    mm = pe.matmul(ps[0:HD, 5, T * h:T * h + T], so[:, b % 2, h, :], ident[0:SROW, T * h:T * h + T], start=True, stop=True)
                mm.then_inc(sot_full, 1)

            def c_turn(n):
                pe.wait_ge(ya_ready, n + 1)
                if n >= 2:
                    pe.wait_ge(yT_ready, n - 1)
                for i in range(2):
                    mm = pe.transpose(ps[:, 6 + n % 2, i * P:(i + 1) * P], yat[:, n % 2, i * P:(i + 1) * P], ident)
                mm.then_inc(yt_full, 1)

            s_scores(0)
            for b in range(NB):
                if b > 0:
                    s_values(b - 1)
                s_turn(b)
                if b > 0:
                    s_out_turn(b - 1)
                if b + 1 < NB:
                    s_scores(b + 1)
                c_turn(b)
            s_values(NB - 1)
            s_out_turn(NB - 1)

            pe.wait_ge(slab_ready, S_UP + 3)
            pe.wait_ge(soT_ready, NB)
            jm = [(S_UP + i) % 3 for i in range(3)]
            for c, (a, w) in enumerate(CHUNKS):
                pe.wait_ge(mx_ready, 6 * (c + 1))
                for d in range(KT):
                    unit = PU_UP + KT * c + d
                    par = d % 2
                    pe.wait_ge(pair_free, unit + 1)
                    for k0, nk, full, half in ((0, 4, gate_full, 0), (4, 2, up_full, 1)):
                        products(bank(2 * par + half, w), lambda k: (
                            whi[:, jm[(k0 + k) // 2], (k % 2) * D + d * P:(k % 2) * D + (d + 1) * P],
                            wlo[:, jm[(k0 + k) // 2], (k % 2) * D + d * P:(k % 2) * D + (d + 1) * P],
                            mx_hi[c % 2][:, k0 + k, 0:w], mx_lo[c % 2][:, k0 + k, 0:w]), nk).then_inc(full, 1)
            pe.wait_ge(up_full, PU_FFN2)
            pe.sem_inc(slab_free, 3)
            for s in range(4):
                j = (S_OUT + s) % 3
                pe.wait_ge(slab_ready, S_OUT + s + 1)
                for c, (a, w) in enumerate(CHUNKS):
                    pe.wait_ge(pair_free, PU_UP + KT * (c + 1) + 2)
                    for dd in range(2):
                        v = AU_OUT + 6 * s + 2 * c + dd
                        pe.wait_ge(acc_free, v + 1)
                        products(bank(4 + v % 4, w), lambda k: (
                            whi[:, j, k * 256 + dd * P:k * 256 + (dd + 1) * P], wlo[:, j, k * 256 + dd * P:k * 256 + (dd + 1) * P],
                            h_hi[:, k, a:a + w], h_lo[:, k, a:a + w]), KT).then_inc(acc_full, 1)
                    if s > 0 and c == 0:
                        release(acc_full, AU_OUT + 6 * s + 1)
                    if s == 3 and c > 0:
                        norm_sums(2, c - 1)

            norm_sums(2, 2)
            ffn(1)

        @block.scalar
        def _(act):
            eps = con[:, C_EPS:C_EPS + 1]

            def norm(n, x_done):
                def squares(c):
                    a, w = CHUNKS[c]
                    x_done(c)
                    for k in range(KT):
                        q = 24 * n + 8 * c + k
                        if q >= 2:
                            act.wait_ge(sq_free, q - 1)
                        act.activation(sq[:, q % 2, 0:w], x[:, k, a:a + w], ACT.Square).then_inc(sq_ready, 1)
                    act.wait_ge(sq_free, 24 * n + 8 * (c + 1))
                    if c == 2:
                        act.wait_ge(*((ht_ready, 24 * n + 8) if n < 3 else (y_ready, 8)))
                    act.activation(rstd[:, c % 2, 0:w], bank(SUM_BANK[c], w), ACT.Sqrt, bias=eps, scale=1.0 / D).then_inc(std_ready, 1)

                def highs(c):
                    a, w = CHUNKS[c]
                    for k in range(KT):
                        q = 24 * n + 8 * c + k
                        act.wait_ge(ht_ready, q + 1)
                        act.activation(h_hi[:, k, a:a + w], htmp[:, q % 2, 0:w], ACT.Copy).then_inc(hhi_ready, 1)

                squares(0)
                if n in (0, 2):
                    squares(1)
                    highs(0)
                else:
                    if n == 1:
                        highs(0)
                    squares(1)
                squares(2)
                if n < 3:
                    highs(1)
                    highs(2)

            def ffn(n):
                pu, fu = (0, 0) if n == 0 else (PU_FFN2, 6 * FFN_ITERS)
                with act.Fori(0, FFN_ITERS) as i:
                    for j in range(2):
                        for c, (a, w) in enumerate(CHUNKS):
                            k = 3 * j + c
                            par = k % 2
                            act.wait_ge(gate_full, 6 * i + (pu + k + 1))
                            act.activation(silu[:, par, 0:w], bank(2 * par, w), ACT.Silu).then_inc(silu_done, 1)
                            act.wait_ge(mul_done, 6 * i + (fu + k + 1))
                            act.activation(act_hi[:, j, a:a + w], bank(2 * par + 1, w), ACT.Copy).then_inc(acthi_done, 1)

            def x0(c):
                act.wait_ge(x_in[c], 16)
            act.wait_ge(con_in, 16)
            norm(0, x0)
            ffn(0)
            norm(1, lambda c: act.wait_ge(acc_free, 4 + AU_IF - 16 + 8 * c))

            act.wait_ge(acc_free, 4 + AU_IF)
            act.dma_start(cost[:], cos_t).then_inc(tab_in, 16)
            act.dma_start(sint[:], sin_t).then_inc(tab_in, 16)
            act.dma_start(msk[:], masks).then_inc(mix_const, 16)
            act.dma_start(msb[:], m_in.unsqueeze(0).to_broadcast([P, H, NB])).then_inc(mix_const, 16)
            act.dma_start(amf[:], amasks[:, 0:384]).then_inc(att_const, 16)
            for s in range(5):
                for t in range(9):
                    n = 9 * s + t
                    rws, tok = (slice(0, P), slice(t * P, (t + 1) * P)) if t < 8 else (slice(SAMP, P), slice(SEQ, TOK))
                    act.wait_ge(v_staged, n + 1)
                    if s < 2:
                        act.dma_start(vm[tok, 2 * s:2 * s + 2, :], svm[rws, n % 2]).then_inc(v_stored[n % 2], 16)
                    else:
                        act.dma_start(va_out[tok, s - 2, :], sva[rws, n % 2].rearrange("p h e -> p (h e)")).then_inc(v_stored[n % 2], 16)
                if s == 0:
                    for c, (a, w) in enumerate(CHUNKS):
                        act.wait_ge(if_staged, c + 1)
                        act.dma_start(zif[:, a:a + w], zif_s[:, c, 0:w]).then_inc(if_stored, 16)
                    act.wait_ge(if_stored, 48)
                    for dst, h0 in ((zi, 0), (zf, H)):
                        for h in range(H):
                            r = slice(8 * h, 8 * h + 8)
                            act.dma_start(dst[r, 0:P], zif[h0 + h, 0:SEQ].rearrange("(c t) -> c t", t=P)).then_inc(gates_in, 16)
                            act.dma_start(dst[r, P:W32], zif[h0 + h, SEQ:TOK].rearrange("(b t) -> b t", t=T)).then_inc(gates_in, 16)

            def store(u, dst):
                act.dma_start(dst, stage[:, u % 2, :, 0:dst.shape[-1]]).then_inc(stored[u % 2], 16)

            def plain(u, kind, pair, c):
                a, w = CHUNKS[c]
                par = u % 2
                if u >= 2:
                    act.wait_ge(stored[par], 16 * (u // 2))
                for half, full in ((0, gate_full), (1, up_full)):
                    act.wait_ge(full, PU_F + u + 1)
                    ins = act.activation(stage[:, par, half, 0:w], bank(2 * par + half, w),
                                         ACT.Sigmoid if kind == 2 else ACT.Copy, scale=DK ** -0.5 if kind == 1 else 1.0)
                ins.then_inc(pair_free, 1)
                act.wait_ge(pair_free, 2 + PU_F + u + 1)
                store(u, zqko[4 * kind + 2 * pair:4 * kind + 2 * pair + 2, :, a:a + w].rearrange("j p t -> p j t"))

            for j in range(3):
                for c in range(NC):
                    plain(3 * j + c, j, 0, c)

            act.wait_ge(gna_ready, 1)
            act.activation(ge[:], gna[:], ACT.Exp).then_inc(ge_ready, 1)
            act.wait_ge(ge_ready, 1)
            act.activation(gl[:], ge[:], ACT.Ln, bias=con[0:32, C_ONE:C_ONE + 1]).then_inc(gl_ready, 1)
            for j in range(3):
                for c in range(NC):
                    plain(9 + 3 * j + c, j, 1, c)
            act.wait_ge(blk_ready, 1)
            act.dma_start(lastrow[0].unsqueeze(1), scan_b[:, 1, 191:192]).then_inc(grow_io, 16)
            act.dma_start(lastrow[1].unsqueeze(1), scan_g[:, 1, 191:192]).then_inc(grow_io, 16)
            act.wait_ge(grow_io, 32)
            act.dma_start(lrow[:], lastrow.unsqueeze(0)).then_inc(grow_io, 16)
            for j in range(6):
                for c, (a, w) in enumerate(CHUNKS):
                    u = 18 + 3 * j + c
                    act.wait_ge(rope_ready, 3 * j + c + 1)
                    act.sem_inc(pair_free, 1)
                    dst = (qr if j < 3 else kr_out)[j % 3]
                    store(u, dst[:, :, a:a + w].rearrange("s p t -> p s t"))
            def gate_unit(i, j, c):
                a, w = CHUNKS[c]
                k = 3 * j + c
                par = k % 2
                act.wait_ge(stored[par], 48 * i + 16 * (18 + k // 2))
                for half, full in ((0, gate_full), (1, up_full)):
                    act.wait_ge(full, 6 * i + (PU_F + 36 + k + 1))
                    ins = act.activation(stage[:, par, half, 0:w], bank(2 * par + half, w), ACT.Sigmoid)
                ins.then_inc(pair_free, 1)
                act.wait_ge(pair_free, 6 * i + (2 + PU_F + 36 + k + 1))
                act.dma_start(zgate.rearrange("(i j s) p t -> i j p s t", j=2, s=2)[i, j, :, :, a:a + w],
                              stage[:, par, :, 0:w]).then_inc(stored[par], 16)

            gate_unit(0, 0, 0)
            act.wait_ge(mrow_ready, 1)
            act.dma_start(m_out.unsqueeze(0), mrow[:]).then_inc(grows_out, 16)
            gate_unit(0, 0, 1)
            act.wait_ge(grows_out, 16)
            for h in range(H):
                act.dma_start(mcol[8 * h:8 * h + 8, :], m_out[h, 0:8].unsqueeze(1)).then_inc(grow_io, 16)
            act.dma_start(mpb[:], m_out[:, 0:8].unsqueeze(0).to_broadcast([P, H, 8])).then_inc(mix_const, 16)
            gate_unit(0, 0, 2)
            gate_unit(0, 1, 0)
            act.wait_ge(gM_ready, 1)
            for n, t in enumerate((ge, gl, gna)):
                for h in range(H):
                    r = slice(8 * h, 8 * h + 8)
                    act.dma_start(rows[n, h, 0:SEQ].rearrange("(c t) -> c t", t=P), t[r, 0:P]).then_inc(grows_out, 16)
                    act.dma_start(rows[n, h, SEQ:TOK].rearrange("(b t) -> b t", t=T), t[r, P:W32]).then_inc(grows_out, 16)
            act.dma_start(ms_out, gmn[:, P + T - 1:P + T]).then_inc(ms_stored, 16)
            gate_unit(0, 1, 1)
            gate_unit(0, 1, 2)
            with act.Fori(1, 4) as i:
                for j in range(2):
                    for c in range(NC):
                        gate_unit(i, j, c)

            def exps(h):
                s = h % 2
                act.wait_ge(arg_ready, h + 1)
                act.activation(ecol[:, s], ecol[:, s], ACT.Exp)
                act.activation(Wd[s][:, 0:SEQ], Wd[s][:, 0:SEQ], ACT.Exp)
                act.activation(Wd[s][0:SAMP, SEQ:TOK], Wd[s][0:SAMP, SEQ:TOK], ACT.Exp).then_inc(wd_ready, 1)
                if h > 0:
                    late_exps(h)

            def late_exps(h):
                s = h % 2
                act.activation(nm[s][:], nm[s][:], ACT.Exp)
                act.activation(wsc[:, s, 1:2], wsc[:, s, 1:2], ACT.Exp)
                act.activation(qw[s][:], qw[s][:], ACT.Exp).then_inc(exp_ready, 1)

            def keys(w):
                h, c = divmod(w, 9)
                act.wait_ge(ts_full, w + 1)
                if c == 0:
                    act.wait_ge(wd_ready, h + 1)
                if w >= 2:
                    act.wait_ge(cu_full, 8 * ((w - 2) // 9) + min((w - 2) % 9 + 1, 8))
                    act.wait_ge(su_full, 8 * ((w - 1) // 9))
                if c < 8:
                    act.activation(kw[:, w % 2, :], ps[:, 0, 0:P], ACT.Copy,
                                   scale=ecol[:, h % 2, 2, c:c + 1]).then_inc(kw_ready, 1)
                else:
                    act.activation(kw[0:SAMP, w % 2, :], ps[0:SAMP, 0, 0:P], ACT.Copy).then_inc(kw_ready, 1)

            def head_squares(h):
                act.wait_ge(hn_ready, 9 * (h + 1))
                if h > 0:
                    act.wait_ge(hidden_stored, 16 * h)
                act.activation(ss[:], hn[h % 2][:], ACT.Square).then_inc(sqh_ready, 1)

            def head_scale(h, c):
                a, w = CHUNKS[c]
                act.wait_ge(ss_full, 3 * h + c + 1)
                act.activation(ss[:, a:a + w], bank(sums_bank(h, c), w), ACT.Copy).then_inc(rs_read, 1)
                if c == 2:
                    act.wait_ge(rs_read, 3 * h + 3)
                    act.activation(ss[:], ss[:], ACT.Ln, bias=eps, scale=1.0 / DK).then_inc(ln_ready, 1)
                    act.wait_ge(ln_ready, h + 1)
                    act.activation(ss[:], ss[:], ACT.Exp, scale=-0.5).then_inc(rs_ready, 1)

            def att_exps(u):
                g, blk, h0, nh, nk = UNITS[u]
                act.wait_ge(mx_full, u + 1)
                if u >= 2:
                    act.wait_ge(pt_full, u - 1)
                wd = nk * P
                for i in range(nh):
                    ins = act.activation(ap_[:, u % 2, i * wd:(i + 1) * wd], ps[:, 4 + u % 2, i * wd:(i + 1) * wd], ACT.Exp,
                                         bias=amx[:, u % 4, i:i + 1])
                ins.then_inc(p_ready, 1)

            def att_copy(u):
                act.wait_ge(pt_full, u + 1)
                if u >= 2:
                    act.wait_ge(ov_full, u - 1)
                act.activation(apt[:, u % 2, :], ps[:, 6, :], ACT.Copy).then_inc(pt_ready, 1)

            att_exps(0)
            for u in range(LEAD):
                att_copy(u)
                att_exps(u + 1)
                if u == 0:
                    exps(0)
                    keys(0)
                    late_exps(0)
            for w in range(9 * H):
                h, c = divmod(w, 9)
                if w + 1 < 9 * H:
                    keys(w + 1)
                u = w + LEAD
                if u < NU:
                    att_copy(u)
                if u + 1 < NU:
                    att_exps(u + 1)
                if h > 0 and c == 0:
                    head_squares(h - 1)
                if h > 0 and 1 <= c <= 3:
                    head_scale(h - 1, c - 1)
                if c == 6 and h + 1 < H:
                    exps(h + 1)
            head_squares(H - 1)
            for c in range(NC):
                head_scale(H - 1, c)

            def branch_high(c, k):
                n = 6 * c + k
                w = CHUNKS[c][1]
                act.wait_ge(mx_in[n % 4], 16 * (n // 4 + 1))
                act.activation(mx_hi[c % 2][:, k, 0:w], mxin[:, n % 4, 0:w], ACT.Copy).then_inc(mx_hid, 1)

            for b in range(NB):
                act.wait_ge(smx_ready, b + 1)
                if b >= 2:
                    act.wait_ge(st_full, b - 1)
                for i, wd in enumerate(SC_WIDTH):
                    ins = act.activation(spx[:, b % 2, SC_KEY[i]:SC_KEY[i] + wd], ps[0:SROW, i, 0:wd], ACT.Exp,
                                         bias=smx[:, b % 2, 3:4])
                ins.then_inc(sp_ready, 1)
                act.wait_ge(ocw_ready, b + 1)
                act.activation(ocw[:, b % 2], ocw[:, b % 2], ACT.Exp).then_inc(oce_ready, 1)
            for k in range(6):
                branch_high(0, k)

            act.wait_ge(soT_ready, NB)
            act.wait_ge(mix_stored[0], 16 * 4)
            act.wait_ge(mix_stored[1], 16 * 4)
            for c, (a, w) in enumerate(CHUNKS):
                for d in range(KT):
                    n = KT * c + d
                    act.wait_ge(mg_ready, n + 1)
                    act.activation(h_hi[:, d, a:a + w], bank(2 * (d % 2) + 1, w), ACT.Copy).then_inc(mg_hid, 1)
                    if c + 1 < NC and d >= 2:
                        branch_high(c + 1, d - 2)

            norm(2, lambda c: act.wait_ge(acc_free, 4 + AU_OUT + 18 + 2 * (c + 1)))
            ffn(1)
            norm(3, lambda c: act.wait_ge(acc_free, 4 + AU_END - 16 + 8 * c))
            act.wait_ge(ms_stored, 16)

        @block.vector
        def _(dve):
            steps = [0]

            def link(ins):
                steps[0] += 1
                ins.then_inc(dve_step, 1)
                dve.wait_ge(dve_step, steps[0])

            dve.sem_inc(acc_free, 4)
            dve.sem_inc(pair_free, 2)
            dve.sem_inc(slab_free, 2)
            dve.wait_ge(con_in, 16)
            dve.tensor_copy(idb[:], con[:, C_ID:C_ID + P]).then_inc(idb_ready, 1)

            def norm(n, x_done):
                gains = con[:, C_G + 8 * n:C_G + 8 * n + 8]

                def scaled(c, k):
                    a, w = CHUNKS[c]
                    q = 24 * n + 8 * c + k
                    if k == 0:
                        x_done(c)
                        dve.wait_ge(std_ready, 3 * n + c + 1)
                        dve.reciprocal(rstd[:, c % 2, 0:w], rstd[:, c % 2, 0:w]).then_inc(rstd_ready, 1)
                        dve.wait_ge(rstd_ready, 3 * n + c + 1)
                    if n < 3:
                        if q >= 2:
                            dve.wait_ge(h_ready, q - 1)
                    elif q - 72 >= 2:
                        dve.wait_ge(y_stored[q % 2], 16 * ((q - 72) // 2))
                    ins = dve.scalar_tensor_tensor(htmp[:, q % 2, 0:w], x[:, k, a:a + w], gains[:, k:k + 1],
                                                   rstd[:, c % 2, 0:w], ALU.mult, ALU.mult)
                    ins.then_inc(ht_ready if n < 3 else y_ready, 1)

                def low(c, k):
                    a, w = CHUNKS[c]
                    q = 24 * n + 8 * c + k
                    dve.wait_ge(hhi_ready, q + 1)
                    dve.tensor_tensor(h_lo[:, k, a:a + w], htmp[:, q % 2, 0:w], h_hi[:, k, a:a + w].bitcast(F32),
                                      ALU.subtract).then_inc(h_ready, 1)

                order = [(c, k) for c in range(NC) for k in range(KT)]

                def step(m):
                    if m == 0:
                        scaled(*order[0])
                    if m + 1 < len(order):
                        scaled(*order[m + 1])
                    if n < 3:
                        low(*order[m])
                return step

            def ffn(n, norm_step):
                pu, fu, au = (0, 0, 0) if n == 0 else (PU_FFN2, 6 * FFN_ITERS, AU_FFN2)
                def accumulate(i, v):
                    c, d = divmod(v, KT)
                    a, w = CHUNKS[c]
                    dve.wait_ge(acc_full, 24 * i + (au + v + 1))
                    dve.scalar_tensor_tensor(x[:, d, a:a + w], bank(4 + v % 4, w), 0.5, x[:, d, a:a + w],
                                             ALU.mult, ALU.add).then_inc(acc_free, 1)

                def activations(i):
                    for j in range(2):
                        for c, (a, w) in enumerate(CHUNKS):
                            k = 3 * j + c
                            par = k % 2
                            up = bank(2 * par + 1, w)
                            dve.wait_ge(silu_done, 6 * i + (fu + k + 1))
                            dve.wait_ge(up_full, 6 * i + (pu + k + 1))
                            dve.tensor_tensor(up, silu[:, par, 0:w], up, ALU.mult).then_inc(mul_done, 1)
                            dve.wait_ge(acthi_done, 6 * i + (fu + k + 1))
                            dve.tensor_tensor(act_lo[:, j, a:a + w], up, act_hi[:, j, a:a + w].bitcast(F32),
                                              ALU.subtract).then_inc(pair_free, 1)
                    dve.wait_ge(acc_free, 24 * i + (au + 4))

                with dve.Fori(0, FFN_ITERS - 1) as i:
                    activations(i)
                    for v in range(24):
                        accumulate(i, v)
                activations(FFN_ITERS - 1)
                for v in range(17):
                    accumulate(FFN_ITERS - 1, v)
                for m in range(7):
                    accumulate(FFN_ITERS - 1, 17 + m)
                    norm_step(m)
                for m in range(7, 24):
                    norm_step(m)

            step = norm(0, lambda c: dve.wait_ge(x_in[c], 16))
            for m in range(24):
                step(m)
            ffn(0, norm(1, lambda c: dve.wait_ge(acc_free, 4 + AU_IF - 16 + 8 * c)))

            dve.memset(svm[:], 1.0)
            link(dve.memset(sva[:], 1.0))
            for s in range(5):
                for t in range(9):
                    n = 9 * s + t
                    v = v_unit(s, t)
                    r = slice(0, P) if t < 8 else slice(SAMP, P)
                    dve.wait_ge(acc_full, v + 1)
                    if n >= 2:
                        dve.wait_ge(v_stored[n % 2], 16 * (n // 2))
                    if s < 2:
                        dst, nh = svm[r, n % 2, :, 0:DK], 2
                    else:
                        dst, nh = sva[r, n % 2, :, 0:HD], H
                    dve.tensor_copy(dst, ps[r, 4 + v % 4, 0:256].rearrange("p (h e) -> p h e", h=nh)).then_inc(v_staged, 1)
                    dve.wait_ge(v_staged, n + 1)
                    dve.sem_inc(acc_free, 1)
                if s == 0:
                    for c, (a, w) in enumerate(CHUNKS):
                        v = if_unit(c)
                        dve.wait_ge(acc_full, v + 1)
                        dve.tensor_copy(zif_s[:, c, 0:w], ps[0:8, 4 + v % 4, 0:w]).then_inc(if_staged, 1)
                        dve.wait_ge(if_staged, c + 1)
                        dve.sem_inc(acc_free, 1)

            col = lambda c: con[0:32, c:c + 1]
            dve.wait_ge(gates_in, 16 * 16)
            dve.tensor_scalar(zi[:], zi[:], col(C_BI), None, ALU.add)
            link(dve.tensor_scalar(zf[:], zf[:], col(C_BF), None, ALU.add))
            dve.tensor_scalar(gmn[:], zf[:], 0.0, None, ALU.min)
            dve.scalar_tensor_tensor(gna[:], zf[:], -1.0, zf[:], ALU.mult, ALU.min).then_inc(gna_ready, 1)
            dve.memset(scan_b[:], 0.0)
            link(dve.memset(scan_g[:], -3e38))
            dve.wait_ge(gl_ready, 1)
            parts = ((64, 0, P, 7), (196, P, T, 3))
            for o, a, w, _ in parts:
                last = dve.tensor_tensor(scan_b[:, 0, o:o + w], gmn[:, a:a + w], gl[:, a:a + w], ALU.subtract)
            link(last)

            def scan(buf, op):
                for k in range(7):
                    for o, _, w, n in parts:
                        if k < n:
                            last = dve.tensor_tensor(buf[:, (k + 1) % 2, o:o + w], buf[:, k % 2, o:o + w],
                                                     buf[:, k % 2, o - 2 ** k:o - 2 ** k + w], op)
                    link(last)

            scan(scan_b, ALU.add)
            for o, a, w, _ in parts:
                dve.tensor_tensor(scan_g[:, 0, o:o + w], zi[:, a:a + w], scan_b[:, 1, o:o + w], ALU.subtract)
                last = dve.tensor_tensor(gna[:, a:a + w], zi[:, a:a + w], scan_b[:, 1, o:o + w], ALU.subtract)
            link(last)
            scan(scan_g, ALU.max)
            dve.memset(mrow[:, :, 0:1], 0.0).then_inc(blk_ready, 1)
            dve.wait_ge(blk_ready, 1)
            dve.wait_ge(tab_in, 32)
            for j in range(6):
                for c, (a, w) in enumerate(CHUNKS):
                    u = 18 + 3 * j + c
                    par = u % 2
                    scale = HD ** -0.5 if j < 3 else 1.0
                    A, B = bank(2 * par, w), bank(2 * par + 1, w)
                    dve.wait_ge(stored[par], 16 * (u // 2))
                    dve.wait_ge(up_full, PU_F + u + 1)
                    o1, o2 = stage[:, par, 0, 0:w], stage[:, par, 1, 0:w]
                    stt = dve.scalar_tensor_tensor
                    link(stt(o1, A, scale, cost[:, a:a + w], ALU.mult, ALU.mult))
                    link(stt(o2, A, scale, sint[:, a:a + w], ALU.mult, ALU.mult))
                    stt(A, B, scale, sint[:, a:a + w], ALU.mult, ALU.mult)
                    link(stt(B, B, scale, cost[:, a:a + w], ALU.mult, ALU.mult))
                    dve.tensor_tensor(o1, o1, A, ALU.subtract)
                    dve.tensor_tensor(o2, o2, B, ALU.add).then_inc(rope_ready, 1)

            dve.wait_ge(grow_io, 48)
            lr = lrow[:].rearrange("p a (h c) -> p a h c", h=H)
            for c in range(NBLK):
                link(dve.tensor_tensor(mtmp[:, c, :], mrow[:, :, c], lr[:, 1, :, c], ALU.max))
                ins = dve.tensor_tensor(mrow[:, :, c + 1], mtmp[:, c, :], lr[:, 0, :, c], ALU.add)
                link(ins)
            dve.sem_inc(mrow_ready, 1)
            dve.wait_ge(grow_io, 48 + 64)
            for (o, a, w, _), m in zip(parts, (mcol[:], col(C_MS))):
                link(dve.tensor_scalar(zi[:, a:a + w], scan_g[:, 1, o:o + w], m, None, ALU.max))
                dve.tensor_scalar(ge[:, a:a + w], zi[:, a:a + w], -1.0, None, ALU.mult)
                link(dve.tensor_tensor(gmn[:, a:a + w], zi[:, a:a + w], scan_b[:, 1, o:o + w], ALU.add))
                last = dve.tensor_scalar(gl[:, a:a + w], gmn[:, a:a + w], -1.0, None, ALU.mult)
            last.then_inc(gM_ready, 1)

            def args(h):
                s = h % 2
                dve.wait_ge(head_in[s], HEAD_IN * (h // 2 + 1))
                blocks = lambda t: t[:, 0:SEQ].rearrange("p (c t) -> p c t", t=P)
                samples = lambda t: t[:, SEQ:TOK].rearrange("p (b t) -> p b t", t=T)
                nMp, nMs = blocks(nM[s][:]), samples(nM[s][:])
                for c in range(NBLK):
                    dve.scalar_tensor_tensor(Wd[s][:, c * P:(c + 1) * P], nMp[:, c, :], gcol[:, c, h:h + 1],
                                             msk[:, M_CAUSAL:M_CAUSAL + P], ALU.add, ALU.add)
                dve.scalar_tensor_tensor(Wd[s][0:SAMP, SEQ:TOK], nM[s][0:SAMP, SEQ:TOK], gcol[0:SAMP, 8, h:h + 1],
                                         msk[0:SAMP, M_SAMPLE:M_SAMPLE + SAMP], ALU.add, ALU.add)
                dve.tensor_tensor(blocks(qw[s][:]), nMp, mpb[:, h, :].unsqueeze(2).to_broadcast([P, 8, P]), ALU.add)
                dve.tensor_tensor(samples(qw[s][:]), nMs, msb[:, h, :].unsqueeze(2).to_broadcast([P, 8, T]), ALU.add)
                dve.tensor_tensor(ecol[:, s, 0, :], mpb[:, h, :], nMp[:, :, P - 1], ALU.add)
                dve.tensor_tensor(ecol[:, s, 1, :], msb[:, h, :], nMs[:, :, T - 1], ALU.add)
                dve.tensor_tensor(ecol[:, s, 2, :], gcol[:, 0:8, h], nMp[:, :, P - 1], ALU.add)
                link(dve.tensor_tensor(own[:, s, :], nMs[0:SAMP, :, T - 1], msk[0:SAMP, M_BLOCK:M_BLOCK + NB], ALU.mult))
                link(dve.tensor_reduce(wsc[:, s, 0:1], own[:, s, :], AX.X, ALU.add))
                dve.tensor_tensor(wsc[:, s, 1:2], wsc[:, s, 0:1], gcol[0:SAMP, 8, h:h + 1], ALU.add).then_inc(arg_ready, 1)

            def queries(h):
                s = h % 2
                dve.wait_ge(exp_ready, h + 1)
                dve.tensor_tensor(qw[s][:], qT[s][:], qw[s][:], ALU.mult).then_inc(qw_ready, 1)

            def sample_parts(h):
                s = h % 2
                dve.wait_ge(qw_ready, h + 1)
                dve.wait_ge(late_in[s], LATE_IN * (h // 2 + 1))
                dve.tensor_tensor(qn[:].rearrange("p (b t) -> p b t", t=T),
                                  qw[s][:, SEQ:TOK].rearrange("p (b t) -> p b t", t=T),
                                  Cs[s][:, :, DK:DK + 1].to_broadcast([P, NB, T]), ALU.mult)
                link(dve.tensor_scalar(own[:, s, :], msk[0:SAMP, M_BLOCK:M_BLOCK + NB], wsc[:, s, 1:2], None, ALU.mult))
                for b in range(NB):
                    ins = dve.tensor_scalar(vex[:, b, :], v1[s][0:SAMP, 8, :], own[:, s, b:b + 1], None, ALU.mult)
                ins.then_inc(samp_ready, 1)

            def weights(w):
                h, c = divmod(w, 9)
                n = P if c < 8 else SAMP
                dve.wait_ge(ts_full, w + 1)
                if c == 0:
                    dve.wait_ge(wd_ready, h + 1)
                if w >= 2:
                    dve.wait_ge(nd_full, w - 1)
                dve.tensor_tensor(Pm[0:n, w % 2, 0:n], ps[0:n, 1, 0:n], Wd[h % 2][0:n, c * P:c * P + n],
                                  ALU.mult).then_inc(pm_ready, 1)

            def new_state(w):
                h, c = divmod(w, 9)
                n = 8 * h + c
                dve.wait_ge(cu_full, n + 1)
                if w > 0:
                    dve.wait_ge(nd_full, w)
                if n > 0:
                    dve.wait_ge(cp_ready, n)
                if c == 1 and h > 0:
                    dve.wait_ge(cp_stored, 16 * h)
                dst = Cp[:, (c + 1) % 2]
                if c == 0:
                    dve.tensor_copy(dst, ps[:, 3, 0:DK + 1]).then_inc(cp_ready, 1)
                else:
                    dve.scalar_tensor_tensor(dst, Cp[:, c % 2], ecol[:, h % 2, 0, c:c + 1], ps[:, 3, 0:DK + 1],
                                             ALU.mult, ALU.add).then_inc(cp_ready, 1)

            def sample_states(h):
                for b in range(NB):
                    n = 8 * h + b
                    dve.wait_ge(su_full, n + 1)
                    dve.scalar_tensor_tensor(Cs[h % 2][:, b], Cs[h % 2][:, b], ecol[:, h % 2, 1, b:b + 1],
                                             ps[:, 3 - b % 2, 0:DK + 1], ALU.mult, ALU.add).then_inc(cs_ready, 1)

            def hidden(w):
                h, c = divmod(w, 9)
                n = P if c < 8 else SAMP
                b = 2
                tok = slice(c * P, c * P + n)
                dve.wait_ge(nd_full, w + 1)
                if w > 0:
                    dve.wait_ge(hn_ready, w)
                link(dve.scalar_tensor_tensor(den[:, 0:n], ps[:, b, P:P + n], -1.0, nm[h % 2][:, tok], ALU.mult, ALU.max))
                link(dve.tensor_tensor(den[:, 0:n], ps[:, b, P:P + n], den[:, 0:n], ALU.max))
                link(dve.reciprocal(den[:, 0:n], den[:, 0:n]))
                dve.tensor_tensor(hn[h % 2][:, tok], ps[:, b, 0:n], den[:, 0:n], ALU.mult).then_inc(hn_ready, 1)

            def finish(h):
                dve.wait_ge(rs_ready, h + 1)
                link(dve.scalar_tensor_tensor(ss[:], hn[h % 2][:], con[:, C_GM + h:C_GM + h + 1], ss[:], ALU.mult, ALU.mult))
                dve.tensor_tensor(ss[:], ss[:], oT[h % 2][:], ALU.mult).then_inc(head_done, 1)

            def att_max(u):
                nh = UNITS[u][3]
                dve.wait_ge(as_full, u + 1)
                if u >= 4:
                    dve.wait_ge(o_ready, u - 3)
                dve.tensor_reduce(amx[:, u % 4, 0:nh], ps[:, 4 + u % 2, :].rearrange("p (h k) -> p h k", h=nh), AX.X, ALU.max,
                                  negate=True).then_inc(mx_full, 1)

            def att_out(u):
                nh = UNITS[u][3]
                dve.wait_ge(ov_full, u + 1)
                if u >= 2:
                    dve.wait_ge(o_stored[u % 2], 16 * (u // 2))
                dve.tensor_copy(ao[:, u % 2, 0:nh, 0:HD + 1], ps[:, 7, 0:nh * (HD + 1)].rearrange("p (h e) -> p h e", h=nh))
                dve.tensor_copy(ao[:, u % 2, 0:nh, HD + 1], amx[:, u % 4, 0:nh]).then_inc(o_ready, 1)

            def sample_queries():
                dve.wait_ge(s_const, S_CONST)
                dve.tensor_copy(smb[:], smk[:])
                link(dve.memset(sqb[:], 0.0))
                for r in range(2):
                    for p in range(2):
                        h, rw = 2 * p + r, slice(64 * r, 64 * r + 64)
                        ins = dve.tensor_copy(sqb[rw, :, p, :, T * h:T * h + T],
                                              sqs[rw, :, p, :].rearrange("d g (b t) -> d g b t", t=T))
                ins.then_inc(sqb_ready, 1)

            dve.wait_ge(gt_full, 1)
            dve.tensor_copy(gcol[:, 0:8, :].rearrange("p c h -> p h c"),
                            ps[:, 4, 0:32].rearrange("p (h c) -> p h c", h=H)).then_inc(gcol_ready, 1)
            dve.wait_ge(gcol_ready, 1)
            dve.wait_ge(att_const, 16)
            dve.wait_ge(idb_ready, 1)
            dve.tensor_copy(amb[:], amf[:]).then_inc(amb_ready, 1)
            att_max(0)
            att_max(1)
            dve.wait_ge(mix_const, 16 * 4)
            args(0)
            for u in range(LEAD):
                att_out(u)
                if u + 2 <= LEAD:
                    att_max(u + 2)
            weights(0)
            queries(0)
            for w in range(9 * H):
                h, c = divmod(w, 9)
                if w + 1 < 9 * H:
                    weights(w + 1)
                u = w + LEAD
                if u + 1 < NU:
                    att_max(u + 1)
                if c < 8:
                    new_state(w)
                hidden(w)
                if c == 7:
                    sample_parts(h)
                if c == 8:
                    sample_states(h)
                    if h + 1 < H:
                        queries(h + 1)
                if u < NU:
                    att_out(u)
                if c == 4 and h > 0:
                    finish(h - 1)
                if c == 5 and h + 1 < H:
                    args(h + 1)
                if w == 9 * H - 2:
                    sample_queries()
            finish(H - 1)

            def s_max(b):
                s = b % 2
                dve.wait_ge(sample_scored, b + 1)
                for i, wd in enumerate(SC_WIDTH):
                    last = dve.tensor_reduce(smx[:, s, i:i + 1], ps[0:SROW, i, 0:wd], AX.X, ALU.max)
                link(last)
                dve.tensor_reduce(smx[:, s, 3:4], smx[:, s, 0:3], AX.X, ALU.max, negate=True).then_inc(smx_ready, 1)

            def s_turned(b):
                dve.wait_ge(st_full, b + 1)
                if b > 0:
                    dve.wait_ge(sv_full, b)
                dve.tensor_copy(spt[:, 0:9, :], ps[:, 3, 0:9 * SROW].rearrange("p (i t) -> p i t", t=SROW))
                dve.tensor_copy(spt[0:G * T, 9, :], ps[0:G * T, 3, 9 * SROW:10 * SROW]).then_inc(spt_ready, 1)

            def s_outputs(b):
                dve.wait_ge(sv_full, b + 1)
                link(dve.reciprocal(smx[:, b % 2, 0:1], ps[0:SROW, 4, HD:HD + 1]))
                dve.tensor_scalar(so[:, b % 2], ps[0:SROW, 4, 0:H * (HD + 1)].rearrange("p (h e) -> p h e", h=H)[:, :, 0:HD],
                                  smx[:, b % 2, 0:1], None, ALU.mult).then_inc(so_ready, 1)

            def s_out(b):
                dve.wait_ge(sot_full, b + 1)
                dve.tensor_copy(soT[:, :, b, :], ps[0:HD, 5, 0:SROW].rearrange("p (h t) -> p h t", h=H)).then_inc(soT_ready, 1)

            def group_weights(n):
                s = n % 2
                dve.wait_ge(c_in[s], 16 * (n // 2 + 1))
                if n >= 2:
                    dve.wait_ge(ya_ready, n - 1)
                nmax = oc[:, s, :, :, HD + 1]
                link(dve.tensor_tensor(ocm[:, s], nmax[:, 0], nmax[:, 1], ALU.min))
                link(dve.tensor_tensor(ocm[:, s], ocm[:, s], nmax[:, 2], ALU.min))
                dve.tensor_tensor(ocw[:, s], ocm[:, s].unsqueeze(1).to_broadcast([P, G, H]), nmax,
                                  ALU.subtract).then_inc(ocw_ready, 1)

            def combine(n):
                s = n % 2
                dve.wait_ge(oce_ready, n + 1)
                for g in range(G):
                    last = dve.tensor_tensor(oc[:, s, g, :, 0:HD + 1], oc[:, s, g, :, 0:HD + 1],
                                             ocw[:, s, g, :].unsqueeze(2).to_broadcast([P, H, HD + 1]), ALU.mult)
                link(last)
                link(dve.tensor_tensor(oacc[:, s], oc[:, s, 0, :, 0:HD + 1], oc[:, s, 1, :, 0:HD + 1], ALU.add))
                dve.tensor_tensor(oacc[:, s], oacc[:, s], oc[:, s, 2, :, 0:HD + 1], ALU.add).then_inc(oc_read, 1)
                dve.wait_ge(oc_read, n + 1)
                link(dve.reciprocal(ocm[:, s], oacc[:, s, :, HD]))
                if n >= 2:
                    dve.wait_ge(yt_full, n - 1)
                dve.tensor_tensor(yat[:, s].rearrange("p (h e) -> p h e", h=H), oacc[:, s, :, 0:HD],
                                  ocm[:, s].unsqueeze(2).to_broadcast([P, H, HD]), ALU.mult).then_inc(ya_ready, 1)

            def c_out(n):
                s = n % 2
                dve.wait_ge(yt_full, n + 1)
                if n >= 2:
                    dve.wait_ge(mix_stored[s], 16 * (n // 2))
                dve.tensor_copy(yT[:, s].rearrange("p j t -> p (j t)"), ps[:, 6 + s, 0:256]).then_inc(yT_ready, 1)

            s_max(0)
            group_weights(0)
            for b in range(NB):
                if b > 0:
                    s_outputs(b - 1)
                s_turned(b)
                combine(b)
                if b + 1 < NB:
                    group_weights(b + 1)
                    s_max(b + 1)
                if b > 0:
                    s_out(b - 1)
                c_out(b)
            s_outputs(NB - 1)

            def branch_low(c, k):
                n = 6 * c + k
                w = CHUNKS[c][1]
                dve.wait_ge(mx_hid, n + 1)
                dve.tensor_tensor(mx_lo[c % 2][:, k, 0:w], mxin[:, n % 4, 0:w], mx_hi[c % 2][:, k, 0:w].bitcast(F32),
                                  ALU.subtract).then_inc(mx_ready, 1)

            for k in range(6):
                branch_low(0, k)
            s_out(NB - 1)
            for c, (a, w) in enumerate(CHUNKS):
                for d in range(KT):
                    n = KT * c + d
                    A, B = bank(2 * (d % 2), w), bank(2 * (d % 2) + 1, w)
                    dve.wait_ge(sg_in[n % 2], 16 * (n // 2 + 1))
                    dve.wait_ge(gate_full, PU_UP + n + 1)
                    if n > 0:
                        dve.wait_ge(mg_ready, n)
                    dve.tensor_tensor(mgt[:, 0:w], A, sgate[:, n % 2, 0, 0:w], ALU.mult)
                    dve.wait_ge(up_full, PU_UP + n + 1)
                    dve.tensor_tensor(B, B, sgate[:, n % 2, 1, 0:w], ALU.mult).then_inc(sg_read, 1)
                    dve.wait_ge(sg_read, n + 1)
                    dve.tensor_tensor(B, B, mgt[:, 0:w], ALU.add).then_inc(mg_ready, 1)
                    dve.wait_ge(mg_hid, n + 1)
                    dve.tensor_tensor(h_lo[:, d, a:a + w], B, h_hi[:, d, a:a + w].bitcast(F32),
                                      ALU.subtract).then_inc(pair_free, 1)
                    if c + 1 < NC and d >= 2:
                        branch_low(c + 1, d - 2)
            for s in range(4):
                dve.wait_ge(x_rest_back if s else x_back, 16)
                for c, (a, w) in enumerate(CHUNKS):
                    for dd in range(2):
                        v = AU_OUT + 6 * s + 2 * c + dd
                        d = 2 * s + dd
                        dve.wait_ge(acc_full, v + 1)
                        dve.tensor_tensor(x[:, d, a:a + w], bank(4 + v % 4, w), x[:, d, a:a + w], ALU.add).then_inc(acc_free, 1)

            step = norm(2, lambda c: dve.wait_ge(acc_free, 4 + AU_OUT + 18 + 2 * (c + 1)))
            for m in range(24):
                step(m)
            ffn(1, norm(3, lambda c: dve.wait_ge(acc_free, 4 + AU_END - 16 + 8 * c)))


def constants():
    ident = np.eye(P, dtype=np.float32)
    t = np.arange(P)
    masks = np.zeros((P, M_N), np.float32)
    masks[:, M_CAUSAL:M_CAUSAL + P] = np.where(t[:, None] <= t[None, :], 0.0, NEG)
    a = np.arange(SAMP)
    same = a[:, None] // T == a[None, :] // T
    masks[0:SAMP, M_SAMPLE:M_SAMPLE + SAMP] = np.where(same & (a[:, None] <= a[None, :]), 0.0, NEG)
    masks[0:SAMP, M_BLOCK:M_BLOCK + NB] = a[:, None] // T == np.arange(NB)[None, :]
    am = np.zeros((P, A_N), np.float32)
    k = np.arange(2 * P)
    dist = t[:, None] + P - k[None, :]
    am[:, A_BAND:A_BAND + 2 * P] = np.where((dist >= 0) & (dist <= 128), 0.0, NEG)
    am[:, A_PAIR:A_PAIR + P] = np.where((t[:, None] % 2 == t[None, :] % 2) & (t[None, :] <= t[:, None]), 0.0, NEG)
    q = (t % T)[:, None]
    new = np.arange(T)[None, :]
    g2 = np.arange(512)[None, :]
    ok = np.concatenate([t[None, :] >= q,
                         new <= q, (new <= q) & ((q - new) % 4 == 0), new == q,
                         (g2 >= q) & ((g2 - q) % 4 == 0),
                         g2 % 8 == q], 1)
    am[:, A_SAMP:A_N] = np.where(ok, 0.0, NEG)
    half = HD // 2
    inv = np.float32(10000.0) ** (np.float32(-2.0) * np.arange(half, dtype=np.float32) / np.float32(HD))
    pos = np.concatenate([np.arange(SEQ), np.tile(SEQ + np.arange(T), NB)]).astype(np.float32)
    ang = np.tile((inv[:, None] * pos[None, :]).astype(np.float32), (4, 1)).astype(np.float64)
    return ident, masks, am, np.cos(ang).astype(np.float32), np.sin(ang).astype(np.float32)


def kernel(x_prompt, x_sample, state_mlstm_C, state_mlstm_n, state_mlstm_m,
           cache_win128_kv, cache_win512_kv, cache_win2048_kv,
           g_ffn1, w1_gate, w1_up, w1_down, g_mix, w_in, b_igate, b_fgate, g_mhead,
           w_up_m, w_up_a, w_out, g_ffn2, w2_gate, w2_up, w2_down, g_final):
    import concourse.bacc as bacc
    from concourse.bass_utils import run_bass_kernel_spmd

    A = np.asarray
    f32 = np.float32
    ident, masks, am, cos_t, sin_t = constants()
    feat = lambda a, n: A(a).reshape(n, P).T
    x = np.concatenate([A(x_prompt).reshape(SEQ, D), A(x_sample).reshape(SAMP, D)], 0)
    xT = np.ascontiguousarray(x.T.reshape(KT, P, TOK).transpose(1, 0, 2))

    stream = np.zeros((SLABS, P, SLAB), f32)
    tiles = lambda w: A(w).reshape(w.shape[0] // P, P, w.shape[1])

    def ffn(s0, wg, wu, wd):
        both = np.stack([tiles(wg[0]), tiles(wu[0])], 0).reshape(2, KT, P, FFN_ITERS, 2, P)
        v = stream[s0:s0 + 3 * FFN_ITERS].reshape(FFN_ITERS, 3, P, SLAB)
        v[:, 0:2] = both.transpose(3, 4, 2, 0, 1, 5).reshape(FFN_ITERS, 2, P, SLAB)
        v[:, 2] = tiles(wd[0]).reshape(FFN_ITERS, 2, P, D).transpose(0, 2, 1, 3).reshape(FFN_ITERS, P, SLAB)

    ffn(0, A(w1_gate), A(w1_up), A(w1_down))
    ffn(S_FFN2, A(w2_gate), A(w2_up), A(w2_down))
    w = A(w_in)[0]
    o = np.cumsum([0, 512, 512, 512, 4, 4, 512, 768, 768, 768, D, D])
    qm, km, vm_, ig, fg, og, qa, ka, va, gm, ga = (w[:, o[i]:o[i + 1]] for i in range(11))
    wide = lambda m: tiles(m).transpose(1, 0, 2)
    stream[S_IF].reshape(P, KT, 256)[:, :, 0:8] = wide(np.concatenate([ig, fg], 1))
    vs = np.concatenate([vm_, va], 1)
    for i in range(5):
        stream[S_V + i] = wide(vs[:, 256 * i:256 * i + 256]).reshape(P, SLAB)
    pairs = []
    for i in range(2):
        pairs += [m[:, 256 * i:256 * i + 256] for m in (qm, km, og)]
    for m in (qa, ka):
        m = m.reshape(D, G, H, 2, 32).transpose(0, 1, 3, 2, 4)
        pairs += [m[:, g].reshape(D, 256) for g in range(G)]
    for m in (gm, ga):
        pairs += [m[:, 256 * i:256 * i + 256] for i in range(4)]
    for i, m in enumerate(pairs):
        stream[S_F + i] = tiles(m).reshape(KT, P, 2, P).transpose(1, 2, 0, 3).reshape(P, SLAB)
    up = np.concatenate([tiles(A(w_up_m)[0]), tiles(A(w_up_a)[0])], 0)
    for i in range(3):
        stream[S_UP + i] = up[2 * i:2 * i + 2].transpose(1, 0, 2).reshape(P, SLAB)
    for i in range(4):
        stream[S_OUT + i] = wide(A(w_out)[0][:, 256 * i:256 * i + 256]).reshape(P, SLAB)

    cols = np.zeros((P, C_N), f32)
    cols[:, C_ONES:C_ONES + P] = 1.0
    cols[:, C_ID:C_ID + P] = ident
    for i, g in enumerate((g_ffn1, g_mix, g_ffn2, g_final)):
        cols[:, C_G + 8 * i:C_G + 8 * i + 8] = feat(g, KT)
    cols[:, C_GM:C_GM + 4] = feat(g_mhead, H)
    cols[:, C_EPS], cols[:, C_ONE] = EPS, 1.0
    cols[0:32, C_BI] = np.repeat(A(b_igate)[0], 8)
    cols[0:32, C_BF] = np.repeat(A(b_fgate)[0], 8)
    m_in = np.ascontiguousarray(A(state_mlstm_m)[0].T)
    cols[0:32, C_MS] = m_in.reshape(32)
    state_in = np.concatenate([A(state_mlstm_C)[0].transpose(1, 3, 0, 2),
                               A(state_mlstm_n)[0].transpose(1, 2, 0)[..., None]], 3)
    caches = [A(c)[0] for c in (cache_win128_kv, cache_win512_kv, cache_win2048_kv)]
    caches[2] = caches[2].reshape(NB, 64, 16, 2, H, HD)[:, :, 0:8].reshape(NB, 512, 2, H, HD)
    kv = np.concatenate(caches, 1)
    kc_in = kv[:, :, 0].reshape(NB, 1152, 2, 2, HD).transpose(0, 3, 4, 2, 1).reshape(NB, P, 2, 1152)
    vc_in = np.concatenate([kv[:, :, 1], np.ones((NB, 1152, H, 1), f32)], 3)
    vc_in = vc_in.reshape(NB, 9, P, H * (HD + 1)).transpose(0, 2, 1, 3)

    ins = dict(stream=stream, xT=xT, cols=cols, masks=masks, amasks=am, cos_t=cos_t, sin_t=sin_t,
               state_in=state_in, m_in=m_in, kc_in=kc_in, vc_in=vc_in)
    outs = dict(y_out=(P, KT, TOK), c_out=(H, P, DK + 1), m_out=(H, NBLK + 1), cs_out=(H, P, NB, DK + 1),
                ms_out=(32, 1), kr_out=(G, 2, P, TOK), va_out=(TOK, G, H * (HD + 1)))
    nc = bacc.Bacc("TRN2", target_bir_lowering=False, num_devices=1)
    ins = {k: np.ascontiguousarray(v) for k, v in ins.items()}
    args = [nc.dram_tensor(k, v.shape, F32, kind="ExternalInput").ap() for k, v in ins.items()]
    args += [nc.dram_tensor(k, s, F32, kind="ExternalOutput").ap() for k, s in outs.items()]
    program(nc, *args)
    r = run_bass_kernel_spmd(nc, [ins], core_ids=[0]).results[0]

    y = A(r["y_out"]).transpose(2, 1, 0).reshape(TOK, D)
    C = A(r["c_out"]).transpose(0, 2, 1)
    Cs = A(r["cs_out"]).transpose(2, 0, 3, 1)
    k = A(r["kr_out"]).reshape(G, 2, H, 32, TOK).transpose(4, 0, 2, 1, 3).reshape(TOK, G, H, HD)
    v = A(r["va_out"]).reshape(TOK, G, H, HD + 1)[..., 0:HD]
    kvs = np.stack([k, v], 2)
    wins = (128, 512, SEQ)
    prompt = tuple(kvs[SEQ - n:SEQ, g][None, None] for g, n in enumerate(wins))
    sample = tuple(kvs[SEQ:, g].reshape(1, NB, T, 2, H, HD) for g in range(G))
    return (y[0:SEQ].reshape(1, SEQ, D), y[SEQ:].reshape(NB, T, D),
            C[None, None, :, 0:DK], C[None, None, :, DK], A(r["m_out"])[None, None, :, NBLK], *prompt,
            Cs[None, :, :, 0:DK], Cs[None, :, :, DK], A(r["ms_out"]).reshape(H, NB).T[None], *sample)
```
